# Optimizing a Trainium2 kernel written in Bass

```python
import math
import jax, jax.numpy as jnp
from jax import lax
import numpy as np

D_MODEL = 2048
BATCH = 1
SEQ = 256
DEPTH = 1

D_MIX = D_MODEL
SB_HEAD_DIM = 64
SB_WIDTH = D_MIX // 4
SB_HEADS = SB_WIDTH // SB_HEAD_DIM
SSM_WIDTH = D_MIX // 4
SSM_GROUP_CH = 16
SSM_GROUPS = SSM_WIDTH // SSM_GROUP_CH
SSM_STATE = 64
DIFF_WIDTH = D_MIX - SB_WIDTH - SSM_WIDTH
DIFF_HEAD_DIM = 64
DIFF_V_DIM = 2 * DIFF_HEAD_DIM
DIFF_HEADS = DIFF_WIDTH // DIFF_V_DIM
IN_COLS = 3 * SB_WIDTH + SSM_WIDTH + 3 * DIFF_WIDTH
N_GROUPS = 4
EXPERTS_PER_GROUP = 8
N_EXPERTS = N_GROUPS * EXPERTS_PER_GROUP
TOP_K_IN_GROUP = 2
D_EXPERT = D_MODEL // 4
Q_BLOCK = 128
EPS = 1e-6

kernel_name = 'hybrid_sb_s5_diffattn_hmoe'

def rmsnorm(x, g):
    xf = x.astype(jnp.float32)
    y = xf * lax.rsqrt(jnp.mean(xf * xf, axis=-1, keepdims=True) + EPS)
    return (y * g.astype(jnp.float32)).astype(x.dtype)

def stick_breaking_attention(q, k, v):
    seq = q.shape[1]
    scale = q.shape[-1] ** -0.5
    outs = []
    for t0 in range(0, seq, Q_BLOCK):
        t1 = t0 + Q_BLOCK
        z = jnp.einsum('bqhd,bkhd->bhqk', q[:, t0:t1], k[:, :t1]).astype(jnp.float32) * scale
        strict = jnp.arange(t1)[None, :] < (t0 + jnp.arange(Q_BLOCK))[:, None]
        log_fail = jnp.where(strict, jax.nn.log_sigmoid(-z), 0.0)
        log_after = lax.cumsum(log_fail, axis=3, reverse=True) - log_fail
        w = jnp.where(strict, jnp.exp(jax.nn.log_sigmoid(z) + log_after), 0.0)
        outs.append(jnp.einsum('bhqk,bkhd->bqhd', w.astype(v.dtype), v[:, :t1]))
    return jnp.concatenate(outs, axis=1)

def differential_attention(q, k, v, lam):
    seq = q.shape[1]
    scale = q.shape[-1] ** -0.5
    outs = []
    for t0 in range(0, seq, Q_BLOCK):
        t1 = t0 + Q_BLOCK
        s = jnp.einsum('bqhrd,bkhrd->bhrqk', q[:, t0:t1], k[:, :t1]).astype(jnp.float32) * scale
        causal = jnp.arange(t1)[None, :] <= (t0 + jnp.arange(Q_BLOCK))[:, None]
        p = jax.nn.softmax(jnp.where(causal, s, -jnp.inf), axis=-1)
        a = p[:, :, 0] - lam * p[:, :, 1]
        outs.append(jnp.einsum('bhqk,bkhd->bqhd', a.astype(v.dtype), v[:, :t1]))
    return jnp.concatenate(outs, axis=1)

def _diag_combine(e1, e2):
    a1, b1 = e1
    a2, b2 = e2
    return (a1 * a2, a2 * b1 + b2)

def s5_mixer(u, lam_re, lam_im, b_re, b_im, c_re, c_im, d_skip, log_dt, w_glu, b_glu):
    bsz, seq, _ = u.shape
    f32 = jnp.float32
    uf = u.astype(f32).reshape(bsz, seq, SSM_GROUPS, SSM_GROUP_CH)
    lam = lax.complex(lam_re.astype(f32), lam_im.astype(f32))
    dt = jnp.exp(log_dt.astype(f32))[:, None]
    lam_bar = jnp.exp(lam * dt)
    b = lax.complex(b_re.astype(f32), b_im.astype(f32))
    b_bar = ((lam_bar - 1.0) / lam)[:, :, None] * b
    bu = jnp.einsum('blgc,gnc->blgn', uf.astype(jnp.complex64), b_bar)
    a = jnp.broadcast_to(lam_bar, bu.shape)
    _, state = lax.associative_scan(_diag_combine, (a, bu), axis=1)
    c = lax.complex(c_re.astype(f32), c_im.astype(f32))
    y = jnp.einsum('blgn,gcn->blgc', state, c).real + d_skip.astype(f32) * uf
    y = jax.nn.gelu(y.reshape(bsz, seq, SSM_WIDTH))
    y = y * jax.nn.sigmoid(y @ w_glu.astype(f32) + b_glu.astype(f32))
    return y.astype(u.dtype)

def hybrid_mixer(xn, w_in, sb_norm_g, lam_re, lam_im, b_re, b_im, c_re, c_im, d_skip, log_dt,
                 w_glu, b_glu, ssm_norm_g, lq1, lk1, lq2, lk2, diff_subln_g, w_out, lam_init):
    bsz, seq, _ = xn.shape
    f32 = jnp.float32
    proj = xn @ w_in
    cuts = np.cumsum([SB_WIDTH] * 3 + [SSM_WIDTH] + [DIFF_WIDTH] * 2).tolist()
    sb_q, sb_k, sb_v, ssm_u, df_q, df_k, df_v = jnp.split(proj, cuts, axis=-1)
    sb_shape = (bsz, seq, SB_HEADS, SB_HEAD_DIM)
    y_sb = stick_breaking_attention(sb_q.reshape(sb_shape), sb_k.reshape(sb_shape), sb_v.reshape(sb_shape))
    y_sb = rmsnorm(y_sb.reshape(bsz, seq, SB_WIDTH), sb_norm_g)
    y_ssm = rmsnorm(s5_mixer(ssm_u, lam_re, lam_im, b_re, b_im, c_re, c_im, d_skip, log_dt, w_glu, b_glu),
                    ssm_norm_g)
    lam = (jnp.exp(jnp.sum(lq1.astype(f32) * lk1.astype(f32)))
           - jnp.exp(jnp.sum(lq2.astype(f32) * lk2.astype(f32))) + lam_init)
    qk_shape = (bsz, seq, DIFF_HEADS, 2, DIFF_HEAD_DIM)
    y_df = differential_attention(df_q.reshape(qk_shape), df_k.reshape(qk_shape),
                                  df_v.reshape(bsz, seq, DIFF_HEADS, DIFF_V_DIM), lam)
    y_df = (rmsnorm(y_df, diff_subln_g) * (1.0 - lam_init)).reshape(bsz, seq, DIFF_WIDTH)
    y = jnp.concatenate([y_sb, y_ssm, y_df], axis=-1)
    return y @ w_out

def hierarchical_moe(xn, rg_w, rg_b, re_w, re_b, w1, w3, w2):
    bsz, seq, d = xn.shape
    f32 = jnp.float32
    t = xn.reshape(bsz * seq, d)
    g_prob = jax.nn.softmax((t @ rg_w + rg_b).astype(f32), axis=-1)
    g_top, g_idx = lax.top_k(g_prob, 1)
    e_logits_all = (jnp.einsum('td,gde->tge', t, re_w) + re_b).astype(f32)
    e_logits = jnp.take_along_axis(e_logits_all, g_idx[:, :, None], axis=1)[:, 0]
    e_top, e_idx = lax.top_k(jax.nn.softmax(e_logits, axis=-1), TOP_K_IN_GROUP)
    e_w = e_top / jnp.sum(e_top, axis=-1, keepdims=True) * g_top
    expert_id = g_idx * EXPERTS_PER_GROUP + e_idx
    gate = jnp.sum(jax.nn.one_hot(expert_id, N_EXPERTS, dtype=f32) * e_w[..., None], axis=1)
    h = jax.nn.silu(jnp.einsum('td,edf->tef', t, w1)) * jnp.einsum('td,edf->tef', t, w3)
    h = h * gate[:, :, None].astype(h.dtype)
    y = jnp.einsum('tef,efd->td', h, w2)
    return y.reshape(bsz, seq, d)

def setup_inputs(seed: int = 0) -> dict:
    key = jax.random.key(seed)
    ks = jax.random.split(key, 26)
    f32 = jnp.float32

    def nrm(k, shape, scale):
        return jax.random.normal(k, shape, f32) * scale

    L = DEPTH
    G, N, C = SSM_GROUPS, SSM_STATE, SSM_GROUP_CH
    lam_im = jnp.broadcast_to(math.pi * jnp.arange(N, dtype=f32), (L, G, N))
    return {
        'x': nrm(ks[0], (BATCH, SEQ, D_MODEL), 1.0),
        'norm_mix_g': 1.0 + nrm(ks[1], (L, D_MODEL), 0.02),
        'w_in': nrm(ks[2], (L, D_MODEL, IN_COLS), D_MODEL ** -0.5),
        'sb_norm_g': 1.0 + nrm(ks[3], (L, SB_WIDTH), 0.02),
        'ssm_lam_re': -0.5 * jnp.exp(nrm(ks[4], (L, G, N), 0.02)),
        'ssm_lam_im': lam_im,
        'ssm_b_re': nrm(ks[5], (L, G, N, C), (2 * C) ** -0.5),
        'ssm_b_im': nrm(ks[6], (L, G, N, C), (2 * C) ** -0.5),
        'ssm_c_re': nrm(ks[7], (L, G, C, N), N ** -0.5),
        'ssm_c_im': nrm(ks[8], (L, G, C, N), N ** -0.5),
        'ssm_d': nrm(ks[9], (L, G, C), 1.0),
        'ssm_log_dt': jax.random.uniform(ks[10], (L, G), f32, math.log(1e-3), math.log(1e-1)),
        'ssm_w_glu': nrm(ks[11], (L, SSM_WIDTH, SSM_WIDTH), SSM_WIDTH ** -0.5),
        'ssm_b_glu': nrm(ks[12], (L, SSM_WIDTH), 0.01),
        'ssm_norm_g': 1.0 + nrm(ks[13], (L, SSM_WIDTH), 0.02),
        'diff_lq1': nrm(ks[14], (L, DIFF_HEAD_DIM), 0.1),
        'diff_lk1': nrm(ks[15], (L, DIFF_HEAD_DIM), 0.1),
        'diff_lq2': nrm(ks[16], (L, DIFF_HEAD_DIM), 0.1),
        'diff_lk2': nrm(ks[17], (L, DIFF_HEAD_DIM), 0.1),
        'diff_subln_g': 1.0 + nrm(ks[18], (L, DIFF_V_DIM), 0.02),
        'w_out': nrm(ks[19], (L, D_MIX, D_MODEL), D_MIX ** -0.5),
        'norm_ffn_g': 1.0 + nrm(ks[20], (L, D_MODEL), 0.02),
        'router_group_w': nrm(ks[21], (L, D_MODEL, N_GROUPS), D_MODEL ** -0.5),
        'router_group_b': nrm(ks[22], (L, N_GROUPS), 0.01),
        'router_expert_w': nrm(ks[23], (L, N_GROUPS, D_MODEL, EXPERTS_PER_GROUP), D_MODEL ** -0.5),
        'router_expert_b': nrm(ks[24], (L, N_GROUPS, EXPERTS_PER_GROUP), 0.01),
        'expert_w1': nrm(jax.random.fold_in(ks[25], 1), (L, N_EXPERTS, D_MODEL, D_EXPERT), D_MODEL ** -0.5),
        'expert_w3': nrm(jax.random.fold_in(ks[25], 2), (L, N_EXPERTS, D_MODEL, D_EXPERT), D_MODEL ** -0.5),
        'expert_w2': nrm(jax.random.fold_in(ks[25], 3), (L, N_EXPERTS, D_EXPERT, D_MODEL), D_EXPERT ** -0.5),
        'final_norm_g': 1.0 + nrm(jax.random.fold_in(ks[25], 4), (D_MODEL,), 0.02),
    }

def reference(x, norm_mix_g, w_in, sb_norm_g, ssm_lam_re, ssm_lam_im, ssm_b_re, ssm_b_im,
              ssm_c_re, ssm_c_im, ssm_d, ssm_log_dt, ssm_w_glu, ssm_b_glu, ssm_norm_g,
              diff_lq1, diff_lk1, diff_lq2, diff_lk2, diff_subln_g, w_out, norm_ffn_g,
              router_group_w, router_group_b, router_expert_w, router_expert_b,
              expert_w1, expert_w3, expert_w2, final_norm_g):
    for l in range(DEPTH):
        lam_init = 0.8 - 0.6 * math.exp(-0.3 * l)
        h = x + hybrid_mixer(rmsnorm(x, norm_mix_g[l]), w_in[l], sb_norm_g[l],
                             ssm_lam_re[l], ssm_lam_im[l], ssm_b_re[l], ssm_b_im[l],
                             ssm_c_re[l], ssm_c_im[l], ssm_d[l], ssm_log_dt[l],
                             ssm_w_glu[l], ssm_b_glu[l], ssm_norm_g[l],
                             diff_lq1[l], diff_lk1[l], diff_lq2[l], diff_lk2[l],
                             diff_subln_g[l], w_out[l], lam_init)
        x = h + hierarchical_moe(rmsnorm(h, norm_ffn_g[l]), router_group_w[l], router_group_b[l],
                                 router_expert_w[l], router_expert_b[l],
                                 expert_w1[l], expert_w3[l], expert_w2[l])
    return rmsnorm(x, final_norm_g)


_drawn_inputs = setup_inputs


def setup_inputs(seed=0):
    import zlib

    import numpy as np

    out = dict(_drawn_inputs(seed))
    spreads = {}
    factors = {'sb_norm_g': 4.019,
     'ssm_lam_re': 8.0,
     'ssm_b_glu': 6.8,
     'ssm_norm_g': 3.792,
     'diff_lq1': 5.666,
     'diff_subln_g': 3.807,
     'norm_ffn_g': 2.937,
     'router_group_b': 4.58,
     'router_expert_b': 8.0,
     'final_norm_g': 2.818}
    for name, (base, spread) in spreads.items():
        noise = np.random.default_rng([zlib.crc32(name.encode()), seed]).standard_normal(out[name].shape)
        drawn = base * np.exp(spread * noise) if base else spread * noise
        out[name] = __import__('jax').numpy.asarray(drawn.astype(out[name].dtype))
    for name, factor in factors.items():
        out[name] = (out[name] * factor).astype(out[name].dtype)
    return out
```

```python
import concourse.bass as bass
from concourse import mybir
from contextlib import ExitStack
import math

D = 2048
T = 256
P = 128
TB = T // P
DC = D // P
SBW = D // 4
SBH = SBW // 64
SSW = D // 4
SG, SN, SC = SSW // 16, 64, 16
ST = SG * SN // P
DFH = (D - SBW - SSW) // 128
IN_COLS = 3 * SBW + SSW + 3 * (D - SBW - SSW)
NG, EPG = 4, 8
NE = NG * EPG
DE = D // 4
EC = DE // P
EPS = 1e-6
LAM_INIT = 0.8 - 0.6 * math.exp(-0.3 * 0)
QSCALE = 64 ** -0.5
NEG = -1e30

UW = 4096
SLOTS_A = 4
SLOTS_B = 6
SLOT = 64
QE = P // SLOT
ITERS = NE // QE
PASSES = T // SLOT
EXTRA = 8

BLOCKS = ([("u", 0, 3 * SBW)] + [("sbq", 0, 0), ("sbk", 0, SBW), ("sbv", 0, 2 * SBW)]
          + [(k, i, 3 * SBW + SSW + o * (D - SBW - SSW) + 512 * i)
             for i in range(2) for o, k in enumerate(("dfq", "dfk", "dfv"))])
NB = len(BLOCKS)
OUT_UNITS = [(0, 0), (1, 0), (0, 1), (1, 1), (2, 0), (2, 1), (3, 0), (3, 1)]
UNITS_A = 2 * NB + len(OUT_UNITS)


def build(nc, x, norm_mix_g, w_in, sb_norm_g, lam_re, lam_im, b_re, b_im, c_re, c_im, ssm_d, log_dt,
          w_glu, b_glu, ssm_norm_g, lq1, lk1, lq2, lk2, subln_g, w_out, norm_ffn_g,
          rg_w, rg_b, re_w, re_b, e_w1, e_w3, e_w2, final_g, out):
    F = mybir.dt.float32
    BF = mybir.dt.bfloat16
    I32 = mybir.dt.int32
    ALU = mybir.AluOpType
    ACT = mybir.ActivationFunctionType
    AX = mybir.AxisListType.X
    ds = bass.ds

    ctx = ExitStack()
    with ctx:
        def sb(name, shape, dt=F):
            return ctx.enter_context(nc.sbuf_tensor(name, shape, dt))

        def sem(name):
            return ctx.enter_context(nc.semaphore(name))

        ring4 = sb("ring4", [P, SLOTS_A * UW])
        reg_e = sb("reg_e", [P, 2 * UW])
        reg_x = sb("reg_x", [P, TB * D])
        reg_t = sb("reg_t", [P, DC * T])
        reg_y = sb("reg_y", [P, DC * T])
        reg_s = sb("reg_s", [P, 4096])
        reg_d = sb("reg_d", [P, 8192])

        def slot(s):
            return ring4[:, s * UW:(s + 1) * UW] if s < SLOTS_A else reg_e[:, (s - SLOTS_A) * UW:(s - SLOTS_A + 1) * UW]

        def slot_of(j):
            return (j + SLOTS_A) % SLOTS_B

        def used(n_, k):
            return n_ * 6 + SLOTS_B + k

        def unit(s):
            return slot(s).rearrange("p (c n) -> p c n", n=512)

        def unit2(s):
            return slot(s).rearrange("p (c n) -> p c n", n=D)

        def v3(ap, b):
            return ap.rearrange("p (a b) -> p a b", b=b)

        xt = v3(reg_x[:, :], D)
        xnT = v3(reg_t[:, :], T)
        yT = v3(reg_y[:, :], T)
        xn = v3(reg_y[:, :], D)
        uT = yT[:, 4:8, :]
        ph = reg_e[:, :].rearrange("p (k j t) -> p k j t", k=2, t=T)
        bpad = reg_x[:, :].rearrange("p (k j n) -> p k j n", k=2, n=P)
        s_ab = [reg_d[:, i * 1024:(i + 1) * 1024].rearrange("p (k r t) -> p k r t", k=2, t=T) for i in range(2)]
        s_v = [v3(reg_d[:, 2048 + i * 512:2560 + i * 512], T) for i in range(2)]
        s_w = v3(reg_d[:, 3072:3584], T)
        s_df = [reg_d[:, 3584 + i * 1024:4608 + i * 1024].rearrange("p (k r t) -> p k r t", k=2, t=T) for i in range(2)]
        s_s = [v3(reg_d[:, 5632 + i * 512:6144 + i * 512], T) for i in range(2)]
        bnat = reg_d[:, 6656:7680].rearrange("p (k j c) -> p k j c", k=2, c=32)
        cnat = reg_d[:, 7680:8192].rearrange("p (q d n) -> p q d n", q=4, d=2)
        cnat2 = reg_s[:, 0:512].rearrange("p (q d n) -> p q d n", q=4, d=2)
        sq = v3(reg_s[:, 0:1024], T)
        sk = v3(reg_s[:, 1024:3072], T)
        sv = v3(reg_s[:, 3072:4096], 512)
        dq = v3(reg_d[:, 0:2048], T)
        dk = reg_d[:, 2048:6144].rearrange("p (h r t) -> p h r t", h=DFH, r=2)
        dv = v3(reg_d[:, 6144:8192], 1024)
        glu_w = v3(reg_e[:, 0:2048], 512)
        glu_s = v3(reg_e[:, 2048:3072], T)
        nrm_sq = v3(reg_e[:, 3072:4096], T)
        sp_a = v3(reg_e[:, 4096:4864], 384)
        sp_e = v3(reg_e[:, 4864:5632], 384)
        sp_t = v3(reg_e[:, 5632:6400], 384)
        sb_w = v3(reg_e[:, 6400:7168], 384)
        df_p0 = reg_e[:, 0:256]
        df_p1 = reg_e[:, 256:768]
        df_t = reg_e[:, 768:1152]
        df_a = reg_e[:, 1152:1536]
        df_aT = reg_e[:, 1536:1920]
        df_sq = reg_e[:, 7168:7168 + 512]
        rstd_t = reg_e[:, 7680:7936]

        ident = sb("ident", [P, P])
        ones = sb("ones", [P, P])
        tri_neg = sb("tri_neg", [P, P])
        ones_neg = sb("ones_neg", [P, P])
        ident_b = sb("ident_b", [P, P], BF)
        ones_b = sb("ones_b", [P, P], BF)
        before_b = sb("before_b", [P, P], BF)
        mask_b = sb("mask_b", [P, 2, P], BF)
        smask_b = sb("smask_b", [P, P], BF)
        stack2 = sb("stack2", [P, SLOT])
        rowm = sb("rowm", [P, 4])
        cmask = sb("cmask", [P, 2])
        sel_w = reg_d[:, 6144:6144 + TB * P]
        iota_i = sb("iota_i", [P, SLOT], I32)
        iota_s = sb("iota_s", [P, SLOT])
        prow = sb("prow", [DC, 4, P])
        pcol = sb("pcol", [P, 64])
        g_mix, g_ffn = pcol[:, 0:16], pcol[:, 16:32]
        g_sb, g_ssm, b_gl, d_sk = (pcol[:, 32 + 4 * i:36 + 4 * i] for i in range(4))
        g_df = pcol[:, 48:49]
        spar = reg_s[0:ST, 1024:4096].rearrange("p (k n) -> p k n", n=P)
        scol = sb("scol", [P, 5, ST])
        pw = sb("pw", [P, 4, ST])
        dt2 = sb("dt2", [ST, 16, 2])
        ki = sb("ki", [ST, P], I32)
        crT = sb("crT", [P, 2, ST, 32])
        lamv = sb("lamv", [P, 4, 64])
        lam_s = sb("lam_s", [P, 8])
        rmsc = sb("rmsc", [P, 16])
        dfc = sb("dfc", [P, 2, 16])
        rw = sb("rw", [P, DC, 4 + NE])
        rbias = sb("rbias", [P, 4 + NE])

        psb = [ctx.enter_context(nc.psum_tensor(f"ps{i}", [P, 512], F)) for i in range(8)]
        pj, at = psb[0:4], psb[4:8]

        ring_in = [sem(f"ring_in{i}") for i in range(SLOTS_B)]
        unit_used = sem("unit_used")
        slot_free = sem("slot_free")
        x_in = [sem(f"x_in{i}") for i in range(2)]
        par_in = sem("par_in")
        b_in = sem("b_in")
        glu_in = sem("glu_in")
        rw_in = sem("rw_in")
        x2_in = sem("x2_in")
        fg_in = sem("fg_in")
        cst = sem("cst")
        cst_z = sem("cst_z")
        b_zero = sem("b_zero")
        gchain = sem("gchain")
        vchain = sem("vchain")
        achain = sem("achain")
        xsum = sem("xsum")
        xnorm = sem("xnorm")
        rstd_s = sem("rstd_s")
        tr_done = sem("tr_done")
        tr_evac = sem("tr_evac")
        pT_done = sem("pT_done")
        pT_evac = sem("pT_evac")
        sp_done = sem("sp_done")
        sT_done = sem("sT_done")
        sT_evac = sem("sT_evac")
        bT_done = sem("bT_done")
        bT_evac = sem("bT_evac")
        cT_done = sem("cT_done")
        c_ready = sem("c_ready")
        ph_ready = sem("ph_ready")
        pj_evac = sem("pj_evac")
        bu_done = sem("bu_done")
        s_prod = sem("s_prod")
        s_rot = sem("s_rot")
        s_scan = sem("s_scan")
        s_out = sem("s_out")
        s_state = sem("s_state")
        sy_used = sem("sy_used")
        sy_evac = sem("sy_evac")
        gelu_s = sem("gelu_s")
        glu_done = sem("glu_done")
        glu_sig = sem("glu_sig")
        glu_y = sem("glu_y")
        nsq = sem("nsq")
        nsum = sem("nsum")
        nrt = sem("nrt")
        ny = sem("ny")
        k_zero = sem("k_zero")
        dk_zero = sem("dk_zero")
        z_done = sem("z_done")
        z_abs = sem("z_abs")
        z_sp = sem("z_sp")
        z_cum = sem("z_cum")
        z_w = sem("z_w")
        sbo_done = sem("sbo_done")
        sbo_evac = sem("sbo_evac")
        d_sc = sem("d_sc")
        d_max = sem("d_max")
        d_exp = sem("d_exp")
        d_a = sem("d_a")
        d_tr = sem("d_tr")
        d_aT = sem("d_aT")
        d_pv = sem("d_pv")
        d_y = sem("d_y")
        lam_sum = sem("lam_sum")
        lam_exp = sem("lam_exp")
        h_add = sem("h_add")
        h_sq = sem("h_sq")
        h_rs = sem("h_rs")
        hn_s = sem("hn_s")
        h_hi = sem("h_hi")
        h_r1 = sem("h_r1")
        h_mid = sem("h_mid")
        h_lo = sem("h_lo")
        rt_done = sem("rt_done")
        rt_sel = sem("rt_sel")
        rt_m = sem("rt_m")
        rt_e = sem("rt_e")
        rk_done = sem("rk_done")
        rk_ready = sem("rk_ready")
        e_sel = sem("e_sel")
        e_selw = sem("e_selw")
        e_gath = sem("e_gath")
        e_gev = sem("e_gev")
        e_gt = sem("e_gt")
        e_gtev = sem("e_gtev")
        e_a1 = sem("e_a1")
        e_a3 = sem("e_a3")
        e_hT = sem("e_hT")
        e_silu = sem("e_silu")
        e_h = sem("e_h")
        e_yev = sem("e_yev")
        e_comb = sem("e_comb")
        e_acc = sem("e_acc")
        f_sq = sem("f_sq")
        f_rs = sem("f_rs")
        f_out = sem("f_out")
        f_st = sem("f_st")

        block = ctx.enter_context(nc.Block())

        hi = reg_y[:, 0:2048].bitcast(BF).rearrange("p (b d) -> p b d", d=D)
        mid = reg_y[:, 2048:4096].bitcast(BF).rearrange("p (b d) -> p b d", d=D)
        lo = reg_s[:, 0:2048].bitcast(BF).rearrange("p (b d) -> p b d", d=D)
        lg = v3(reg_s[:, 2048:2048 + 2 * 36], 36)
        sel = v3(reg_s[:, 2128:2128 + 2 * NE], NE)
        gat = v3(reg_s[:, 2192:2192 + 2 * NE], NE)
        selb = reg_s[:, 2256:2256 + NE].bitcast(BF).rearrange("p (b e) -> p b e", e=NE)
        pos = v3(reg_s[:, 2288:2288 + 2 * NE], NE)
        rtmp = reg_s[:, 2352:2352 + 256]
        posx = v3(reg_s[:, 2608:2608 + 2 * (NE + EXTRA)], NE + EXTRA)
        gatx = v3(reg_s[:, 2688:2688 + 2 * (NE + EXTRA)], NE + EXTRA)
        x_n = reg_s[:, 2768:2768 + NE]
        x_c = reg_s[:, 2800:2800 + NE]
        x_e = reg_s[:, 2832:2832 + NE]
        x_id = reg_s[:, 2864:2864 + EXTRA]
        n_extra = reg_s[:, 2872:2873].bitcast(I32)
        ids = reg_s[:, 2880:2880 + EXTRA].bitcast(I32)
        x_t = reg_s[:, 2900:2900 + 3 * EXTRA * NE].rearrange("p (k x e) -> p k x e", k=3, e=NE)
        xeT = v3(reg_t[:, 0:2048], P)
        a1 = reg_t[:, 2048:2560]
        a3 = reg_t[:, 2560:3072]
        hs = reg_t[:, 3072:3328]
        hT = v3(reg_t[:, 3328:3584], SLOT)
        gT = reg_t[:, 3584:3840]
        selS = reg_t[:, 3840:3968].bitcast(BF).rearrange("p (b q s) -> p b q s", b=2, q=QE)
        selW = sel_w.rearrange("p (b q s) -> p b q s", b=2, q=QE)
        hn = v3(reg_d[:, 0:4096], D)
        hr1 = v3(reg_d[:, 4096:8192], D)
        ye = reg_d[:, 4096:6144]
        fg = reg_d[:, 0:2048]
        junk = reg_d[:, 2048:4096]
        ob = v3(reg_d[:, 2048:6144], D)

        w_in_u = w_in.rearrange("l (c p) n -> p (l c) n", p=P)
        w_out_u = w_out.rearrange("l (c p) n -> p (l c) n", p=P)
        x_v = x.rearrange("o (b p) d -> p (o b) d", p=P)
        out_v = out.rearrange("o (b p) d -> p (o b) d", p=P)
        w1_v = e_w1.rearrange("l e (h c p) n -> p (l e) h c n", h=2, p=P)
        w3_v = e_w3.rearrange("l e (h c p) n -> p (l e) h c n", h=2, p=P)
        w2_v = e_w2.rearrange("l e (h c p) n -> p (l e) h c n", h=2, p=P)

        @block.sync
        def _(sp):
            for b in range(TB):
                sp.dma_start(xt[:, b, :], x_v[:, b, :]).then_inc(x_in[b], 16)
            for n in range(UNITS_A):
                s = n % SLOTS_A
                if n < 2 * NB:
                    c0 = BLOCKS[n // 2][2]
                    src = w_in_u[:, 8 * (n % 2):8 * (n % 2) + 8, c0:c0 + 512]
                else:
                    ob_, half = OUT_UNITS[n - 2 * NB]
                    src = w_out_u[:, 8 * half:8 * half + 8, 512 * ob_:512 * ob_ + 512]
                if n >= SLOTS_A:
                    sp.wait_ge(unit_used, n - SLOTS_A + 1)
                sp.dma_start(unit(s), src).then_inc(ring_in[s], 16)
                if n == 12:
                    sp.wait_ge(bu_done, ST)
                    for b in range(TB):
                        sp.dma_start(xt[:, b, :], x_v[:, b, :]).then_inc(x2_in, 16)

            def item(n_, e):
                for k in range(6):
                    s = slot_of(k)
                    sp.wait_ge(slot_free, n_ * 6 + k + 1)
                    w = (w1_v, w3_v, w2_v)[k // 2]
                    src = w[:, ds(e, 1), k % 2, :, :]
                    sp.dma_start(unit(s) if k < 4 else unit2(s), src.rearrange("p e c n -> p (e c) n")).then_inc(ring_in[s], 16)

            with sp.Fori(0, NE) as e:
                item(e, e)
            sp.wait_ge(rk_ready, 2)
            extra = sp.value_load(n_extra[0:1, 0:1], min_val=0, max_val=EXTRA - 1)
            with sp.If(extra > 0):
                with sp.Fori(0, extra) as x_:
                    item(x_ + NE, sp.value_load(ids[0:1, ds(x_, 1)], min_val=0, max_val=NE - 1))
            for b in range(TB):
                sp.wait_ge(f_out, b + 1)
                sp.dma_start(out_v[:, b, :], ob[:, b, :]).then_inc(f_st, 16)
            sp.wait_ge(f_st, 16 * TB)

        @block.gpsimd
        def _(g):
            n = [0]

            def link(ins):
                n[0] += 1
                ins.then_inc(gchain, 1)
                g.wait_ge(gchain, n[0])

            G = nc.gpsimd
            for t, val in ((ident, 0.0), (ones, 1.0), (tri_neg, -1.0), (ones_neg, -1.0), (ident_b, 0.0), (ones_b, 1.0),
                           (before_b, 1.0), (mask_b, 0.0), (smask_b, 0.0), (stack2, 0.0), (rowm, 1.0), (cmask, 1.0)):
                last = G.memset(t[:], val)
            link(last)

            def pick(t, pattern, base, cm, op, fill):
                return G.affine_select(out=t, in_=t, compare_op=op, fill=fill, base=base, pattern=pattern,
                                       channel_multiplier=cm)

            pick(ident[:, :], [[-1, P]], 0, 1, ALU.not_equal, 1.0)
            pick(ident_b[:, :], [[-1, P]], 0, 1, ALU.not_equal, 1.0)
            pick(tri_neg[:, :], [[-1, P]], 0, 1, ALU.is_ge, 0.0)
            pick(before_b[:, :], [[1, P]], 0, -1, ALU.is_gt, 0.0)
            pick(mask_b[:, :, :], [[0, 2], [-1, P]], 0, 1, ALU.is_ge, NEG)
            pick(smask_b[:, :], [[1, P]], 0, -1, ALU.is_gt, NEG)
            for k in range(QE):
                link(pick(stack2[:, :], [[-1, SLOT]], -SLOT * k, 1, ALU.not_equal, 1.0))
            pick(rowm[:, :], [[-32, 4]], 0, 1, ALU.is_ge, 0.0)
            link(pick(cmask[:, :], [[-64, 2]], 0, 1, ALU.is_ge, 0.0))
            pick(rowm[:, :], [[32, 4]], 31, -1, ALU.is_ge, 0.0)
            pick(cmask[:, :], [[64, 2]], 63, -1, ALU.is_ge, 0.0)
            link(G.iota(iota_i[:, :], [[1, SLOT]], base=0, channel_multiplier=0))
            G.tensor_copy(iota_s[:, :], iota_i[:, :]).then_inc(cst, 1)
            G.memset(bnat[:, :, :, :], 0.0).then_inc(b_zero, 1)
            g.wait_ge(b_zero, 1)
            for k, b in enumerate((b_re, b_im)):
                bv = b.rearrange("l (j h) n c -> (l h) n j c", h=2)
                for h in range(2):
                    g.dma_start(bnat[64 * h:64 * h + 64, k, :, 16 * h:16 * h + 16], bv[h]).then_inc(b_in, 16)
            G.memset(ph[:, 0, :, 0:1], 1.0)
            G.memset(ph[:, 1, :, 0:1], 0.0).then_inc(k_zero, 1)

            def rot_in(j):
                g.wait_ge(s_prod, j + 1)
                if j >= 2:
                    g.wait_ge(s_scan, j - 1)
                ab, v = s_ab[j % 2], s_v[j % 2]
                G.tensor_tensor(v[:, 0, :], ab[:, 0, 0, :], ab[:, 1, 1, :], ALU.subtract)
                G.tensor_tensor(v[:, 1, :], ab[:, 0, 1, :], ab[:, 1, 0, :], ALU.add).then_inc(s_rot, 1)

            def rot_out(j):
                g.wait_ge(s_out, j + 1)
                if j >= 2:
                    g.wait_ge(sy_used, j - 1)
                df, s = s_df[j % 2], s_s[j % 2]
                G.tensor_tensor(s[:, 0, :], df[:, 0, 0, :], df[:, 1, 1, :], ALU.add)
                G.tensor_tensor(s[:, 1, :], df[:, 0, 1, :], df[:, 1, 0, :], ALU.subtract).then_inc(s_state, 1)

            g.wait_ge(k_zero, 1)
            g.wait_ge(cT_done, 2)
            link(G.memset(sk[64:128, 0:8:2, :], 0.0))
            G.memset(sk[0:64, 1:8:2, :], 0.0).then_inc(dk_zero, 1)
            g.wait_ge(dk_zero, 1)
            for j in range(ST + 1):
                if j < ST:
                    rot_in(j)
                if j >= 1:
                    rot_out(j - 1)
            g.wait_ge(sy_used, ST)
            g.wait_ge(s_state, ST)
            link(G.memset(dk[64:128, :, 0, :], 0.0))
            G.memset(dk[0:64, :, 1, :], 0.0).then_inc(dk_zero, 1)

        @block.scalar
        def _(a):
            A = nc.scalar
            cp = ACT.Copy
            a.dma_start(spar[:, 0, :], lam_re.rearrange("l (j h) n -> (l j) (h n)", h=2)).then_inc(par_in, 16)
            a.dma_start(spar[:, 1, :], lam_im.rearrange("l (j h) n -> (l j) (h n)", h=2)).then_inc(par_in, 16)
            a.dma_start(dt2[:, 0, :], log_dt.rearrange("l (j h) -> (l j) h", h=2)).then_inc(par_in, 16)
            a.dma_start(prow[:, 0, :], norm_mix_g.rearrange("l (c p) -> (l c) p", p=P)).then_inc(par_in, 16)
            a.dma_start(prow[:, 1, :], norm_ffn_g.rearrange("l (c p) -> (l c) p", p=P)).then_inc(par_in, 16)
            for i, r in enumerate((sb_norm_g, ssm_norm_g, b_glu)):
                a.dma_start(prow[4 * i:4 * i + 4, 2, :], r.rearrange("l (c p) -> (l c) p", p=P)).then_inc(par_in, 16)
            a.dma_start(prow[12:16, 2, :], ssm_d.rearrange("l (q g) c -> (l q) (g c)", q=4)).then_inc(par_in, 16)
            a.dma_start(prow[0:1, 3, :], subln_g).then_inc(par_in, 16)
            for i, r in enumerate((lq1, lk1, lq2, lk2)):
                a.dma_start(lamv[:, i, :], r.broadcast_to([P, 64])).then_inc(par_in, 16)
            for k, (cn, c) in enumerate(((cnat, c_re), (cnat2, c_im))):
                cv = c.rearrange("l (q g) c n -> (l g c) q n", q=4)
                for d in range(2):
                    a.dma_start(cn[:, :, d, :], cv).then_inc(par_in, 16)
            for k in range(NG):
                a.dma_start(rw[:, :, NG + EPG * k:NG + EPG * (k + 1)],
                            re_w[:, k].rearrange("l (c p) e -> p (l c) e", p=P)).then_inc(rw_in, 16)
            a.dma_start(rw[:, :, 0:NG], rg_w.rearrange("l (c p) e -> p (l c) e", p=P)).then_inc(rw_in, 16)
            a.dma_start(rbias[:, 0:NG], rg_b.broadcast_to([P, NG])).then_inc(rw_in, 16)
            a.dma_start(rbias[:, NG:], re_b.rearrange("l g e -> l (g e)").broadcast_to([P, NE])).then_inc(rw_in, 16)
            for b in range(TB):
                a.wait_ge(x_in[b], 16)
                A.activation(xn[:, b, :], xt[:, b, :], ACT.Square, accum_out=rmsc[:, b:b + 1]).then_inc(xsum, 1)
            a.wait_ge(rstd_s, 1)
            A.activation(rmsc[:, 4:6], rmsc[:, 2:4], ACT.Sqrt).then_inc(achain, 1)
            a.wait_ge(rstd_s, 2)
            for b in range(TB):
                A.activation(xn[:, b, :], xt[:, b, :], cp, scale=rmsc[:, 6 + b:7 + b]).then_inc(xnorm, 1)
            a.wait_ge(par_in, 16 * 18)
            a.wait_ge(pT_evac, 1)
            for n_ in range(DC // 2):
                a.wait_ge(tr_done, n_ + 1)
                for k in range(2):
                    c = 2 * n_ + k
                    last = A.activation(xnT[:, c, :], pj[n_ % 4][:, k * T:(k + 1) * T], cp, scale=g_mix[:, c:c + 1])
                last.then_inc(tr_evac, 1)

            def evac(n_):
                kind, i, _c = BLOCKS[n_]
                a.wait_ge(unit_used, 2 * n_ + 2)
                for k in range(2):
                    src = pj[2 * (n_ % 2) + k]
                    if kind == "u":
                        last = A.activation(uT[:, 2 * k:2 * k + 2, :], v3(src[:, :], T), cp)
                    elif kind in ("sbq", "dfq"):
                        q = sq if kind == "sbq" else dq
                        last = A.activation(q[:, 4 * i + 2 * k:4 * i + 2 * k + 2, :], v3(src[:, :], T), cp, scale=QSCALE)
                    elif kind == "sbk":
                        for h in range(2):
                            rows = slice(64 * h, 64 * h + 64)
                            last = A.activation(sk[rows, 4 * k + h:4 * k + h + 3:2, :], v3(src[rows, :], T), cp)
                    elif kind == "dfk":
                        for h in range(2):
                            rows = slice(64 * h, 64 * h + 64)
                            last = A.activation(dk[rows, 4 * i + 2 * k:4 * i + 2 * k + 2, h, :], v3(src[rows, :], T), cp)
                    elif kind == "sbv":
                        last = A.activation(sv[:, k, :], src[:, :], cp)
                    else:
                        last = A.activation(dv[:, k, 512 * i:512 * i + 512], src[:, :], cp)
                last.then_inc(pj_evac, 1)

            evac(0)
            a.wait_ge(dk_zero, 1)
            for n_ in (1, 2, 3):
                evac(n_)
            a.wait_ge(s_state, ST)
            a.dma_start(glu_w[:, :, :], w_glu.rearrange("l (c p) n -> p (l c) n", p=P)).then_inc(glu_in, 16)
            for q in range(4):
                a.wait_ge(sy_evac, q + 1)
                A.activation(uT[:, q, :], uT[:, q, :], ACT.Gelu_apprx_tanh).then_inc(gelu_s, 1)
            for q in range(4):
                a.wait_ge(glu_done, 2 * (q // 2) + 2)
                A.activation(glu_s[:, q, :], at[q // 2][:, (q % 2) * T:(q % 2) * T + T], ACT.Sigmoid,
                             bias=b_gl[:, q:q + 1]).then_inc(glu_sig, 1)

            a.wait_ge(glu_y, 1)
            A.activation(nrm_sq[:, :, :], yT[:, 4:8, :], ACT.Square).then_inc(nsq, 1)
            a.wait_ge(nsum, 1)
            A.activation(rstd_t, at[2][:, 0:T], ACT.Sqrt, scale=1.0 / SSW, bias=lam_s[:, 6:7]).then_inc(nrt, 1)
            for hp in range(SBH // 2):
                a.wait_ge(z_done, hp + 1)
                for k in range(2):
                    A.activation(sp_a[:, k, :], at[k][:, 0:384], ACT.Abs).then_inc(z_abs, 1)
                a.wait_ge(z_abs, 6 * hp + 2)
                if hp == 0:
                    a.wait_ge(nrt, 1)
                A.activation(sp_e[:, :, :], sp_a[:, :, :], ACT.Exp, scale=-1.0).then_inc(z_abs, 2)
                a.wait_ge(z_abs, 6 * hp + 4)
                A.activation(sp_a[:, :, :], sp_e[:, :, :], ACT.Ln, bias=1.0).then_inc(z_abs, 2)
                a.wait_ge(z_cum, hp + 1)
                if hp:
                    a.wait_ge(sbo_done, hp)
                for k in range(2):
                    last = A.activation(sb_w[:, k, :], at[k][:, 0:384], ACT.Exp)
                last.then_inc(z_w, 1)
                a.wait_ge(sbo_done, hp + 1)
                A.activation(yT[:, hp, :], at[2][:, 0:T], cp).then_inc(sbo_evac, 1)
            a.wait_ge(ny, 1)
            a.wait_ge(sbo_evac, SBH // 2)
            A.activation(nrm_sq[:, :, :], yT[:, 0:4, :], ACT.Square).then_inc(nsq, 1)
            a.wait_ge(nsum, 2)
            A.activation(rstd_t, at[3][:, 0:T], ACT.Sqrt, scale=1.0 / SBW, bias=lam_s[:, 6:7]).then_inc(nrt, 1)
            a.wait_ge(lam_sum, 1)
            A.activation(lam_s[:, 2:4], lam_s[:, 0:2], ACT.Exp).then_inc(lam_exp, 1)
            a.wait_ge(dk_zero, 2)
            a.wait_ge(glu_y, 1)
            for n_ in (4, 5, 6):
                evac(n_)

            def df_exp(h):
                a.wait_ge(d_max, h + 1)
                nm, su = dfc[:, h % 2, 0:4], dfc[:, h % 2, 4:8]
                if h:
                    a.wait_ge(d_a, h)
                for r in range(2):
                    A.activation(df_p0[:, r * P:(r + 1) * P], at[0][:, r * P:(r + 1) * P], ACT.Exp,
                                 bias=nm[:, r:r + 1], accum_out=su[:, r:r + 1])
                for r in range(2):
                    last = A.activation(df_p1[:, r * T:(r + 1) * T], at[1][:, r * T:(r + 1) * T], ACT.Exp,
                                        bias=nm[:, 2 + r:3 + r], accum_out=su[:, 2 + r:3 + r])
                last.then_inc(d_exp, 1)

            def df_copy(h):
                a.wait_ge(d_pv, h + 1)
                A.activation(yT[:, 8 + h, :], at[3][:, (h % 2) * T:(h % 2) * T + T], cp).then_inc(d_y, 1)

            for h in range(DFH):
                df_exp(h)
                df_copy(h)
                if h == 1:
                    evac(7)
                if h == 3:
                    evac(8)
                    evac(9)
            for h in range(DFH):
                if h >= 2:
                    a.wait_ge(nsum, 2 + h - 1)
                a.wait_ge(d_y, h + 1)
                A.activation(df_sq[:, (h % 2) * T:(h % 2) * T + T], yT[:, 8 + h, :], ACT.Square).then_inc(nsq, 1)
                a.wait_ge(nsum, 3 + h)
                a.wait_ge(ny, 2 + h)
                A.activation(rstd_t, at[h % 2][:, 0:T], ACT.Sqrt, scale=1.0 / P, bias=lam_s[:, 6:7]).then_inc(nrt, 1)
            for b in range(TB):
                a.wait_ge(h_add, 4 * TB)
                if b == 0:
                    a.wait_ge(d_pv, DFH)
                A.activation(hr1[:, b, :], xt[:, b, :], ACT.Square, accum_out=rmsc[:, 8 + b:9 + b]).then_inc(h_sq, 1)
            a.wait_ge(h_rs, 1)
            A.activation(rmsc[:, 4:6], rmsc[:, 2:4], ACT.Sqrt).then_inc(achain, 1)
            a.wait_ge(h_rs, 2)
            for b in range(TB):
                A.activation(hn[:, b, :], xt[:, b, :], cp, scale=rmsc[:, 10 + b:11 + b]).then_inc(hn_s, 1)
            for n_ in range(DC // 2):
                a.wait_ge(tr_done, DC // 2 + n_ + 1)
                for k in range(2):
                    c = 2 * n_ + k
                    last = A.activation(xnT[:, c, :], pj[n_ % 4][:, k * T:(k + 1) * T], cp, scale=g_ffn[:, c:c + 1])
                last.then_inc(tr_evac, 1)
            for b in range(TB):
                A.activation(hi[:, b, :], hn[:, b, :], cp).then_inc(h_hi, 1)
                a.wait_ge(h_r1, b + 1)
                A.activation(mid[:, b, :], hr1[:, b, :], cp).then_inc(h_mid, 1)
            a.wait_ge(h_r1, TB)
            a.dma_start(fg, final_g.unsqueeze(0).broadcast_to([P, D])).then_inc(fg_in, 16)
            a.wait_ge(rt_m, TB)
            A.activation(rtmp[:, 128:138], rtmp[:, 96:106], ACT.Exp).then_inc(rt_e, 1)

            def a_items(i_, n0, nq):
                for q in range(nq):
                    n_ = n0 + q
                    a.wait_ge(slot_free, used(n_, 2))
                    a.wait_ge(e_hT, n_ + 1)
                    A.activation(a1, psb[0][:, :], cp).then_inc(e_a1, 1)
                    a.wait_ge(e_hT, n_ + 2)
                    a.wait_ge(e_h, n_ + 1)
                    A.activation(hs, psb[2][:, 0:256], ACT.Silu).then_inc(e_silu, 1)
                    a.wait_ge(slot_free, used(n_, 6))
                    a.wait_ge(e_comb, i_ * 8 + 1)
                    for b in range(2):
                        last = A.activation(ye[64 * q:64 * q + 64, 512 * b:512 * b + 512], psb[3][64 * b:64 * b + 64, :], cp)
                    last.then_inc(e_yev, 1)

            with a.Fori(0, ITERS) as it:
                a_items(it, it * QE, QE)
            a.wait_ge(rk_ready, 2)
            extra = a.value_load(n_extra[0:1, 0:1], min_val=0, max_val=EXTRA - 1)
            with a.If(extra > 0):
                with a.Fori(0, extra) as x_:
                    a_items(x_ + ITERS, x_ + NE, 1)
            a.wait_ge(e_comb, (extra + ITERS) * 8 + 1)
            a.wait_ge(e_acc, (extra + ITERS) * 8)
            for b in range(TB):
                A.activation(junk if b == 0 else hr1[:, 0, :], xt[:, b, :], ACT.Square,
                             accum_out=rmsc[:, 12 + b:13 + b]).then_inc(f_sq, 1)
            a.wait_ge(f_rs, 1)
            A.activation(rmsc[:, 4:6], rmsc[:, 2:4], ACT.Sqrt).then_inc(f_sq, 1)

        @block.vector
        def _(v):
            V = nc.vector
            n = [0]

            def link(ins):
                n[0] += 1
                ins.then_inc(vchain, 1)
                v.wait_ge(vchain, n[0])

            MAGIC = 1.5 * 2.0 ** 23

            def exp_rows(dst, src, k, f, t, kint):
                link(V.tensor_scalar(dst, src, -87.0, 88.0, ALU.max, ALU.min))
                src = dst
                link(V.tensor_scalar(t, src, 1.0 / math.log(2.0), MAGIC, ALU.mult, ALU.add))
                link(V.tensor_scalar(k, t, MAGIC, -126.0, ALU.subtract, ALU.max))
                link(V.tensor_scalar(k, k, 127.0, None, ALU.min))
                link(V.scalar_tensor_tensor(f, k, -0.693359375, src, ALU.mult, ALU.add))
                link(V.scalar_tensor_tensor(f, k, 2.12194440054690583e-4, f, ALU.mult, ALU.add))
                link(V.tensor_scalar(t, f, 1.0 / 5040, None, ALU.mult))
                for c in (1.0 / 720, 1.0 / 120, 1.0 / 24, 1.0 / 6, 0.5, 1.0):
                    link(V.scalar_tensor_tensor(t, t, c, f, ALU.add, ALU.mult))
                link(V.tensor_scalar(kint, k, 127.0, 2.0 ** 23, ALU.add, ALU.mult))
                link(V.scalar_tensor_tensor(dst, t, 1.0, kint.bitcast(F), ALU.add, ALU.mult))

            V.memset(lam_s[:, 6:7], EPS)
            v.wait_ge(xsum, TB)
            V.tensor_scalar(rmsc[:, 2:4], rmsc[:, 0:2], 1.0 / D, EPS, ALU.mult, ALU.add).then_inc(rstd_s, 1)
            v.wait_ge(achain, 1)
            V.reciprocal(rmsc[:, 6:8], rmsc[:, 4:6]).then_inc(rstd_s, 1)
            v.wait_ge(pT_done, 1)
            V.tensor_copy(pcol[:, 0:49], at[0][:, 0:49]).then_inc(pT_evac, 1)
            v.wait_ge(par_in, 16 * 18)
            R = lambda i: spar[:, i, :]
            DT = lambda i: dt2[:, i, :]
            exp_rows(DT(1), DT(0), DT(2), DT(3), DT(4), ki[:, 0:2])
            dtb = dt2[:, 1, :].unsqueeze(2).broadcast_to([ST, 2, 64])
            r3 = lambda i: spar[:, i, :].rearrange("p (h n) -> p h n", h=2)
            link(V.tensor_tensor(r3(2), r3(0), dtb, ALU.mult))
            link(V.tensor_tensor(r3(3), r3(1), dtb, ALU.mult))
            exp_rows(R(4), R(2), R(5), R(6), R(7), ki[:, :])
            link(V.tensor_scalar(R(5), R(3), 1.0 / (2 * math.pi), MAGIC, ALU.mult, ALU.add))
            link(V.tensor_scalar(R(5), R(5), MAGIC, None, ALU.subtract))
            c1 = 6.28125
            c2 = 1.935307179586e-3 - (1.935307179586e-3 % 2.0 ** -20)
            c3 = 2 * math.pi - c1 - c2
            link(V.scalar_tensor_tensor(R(6), R(5), -c1, R(3), ALU.mult, ALU.add))
            link(V.scalar_tensor_tensor(R(6), R(5), -c2, R(6), ALU.mult, ALU.add))
            link(V.scalar_tensor_tensor(R(6), R(5), -c3, R(6), ALU.mult, ALU.add))
            link(V.tensor_scalar(R(6), R(6), 0.5, None, ALU.mult))
            link(V.tensor_tensor(R(7), R(6), R(6), ALU.mult))
            link(V.tensor_scalar(R(8), R(7), 1.0 / math.factorial(13), None, ALU.mult))
            for k in (11, 9, 7, 5, 3):
                link(V.scalar_tensor_tensor(R(8), R(8), (-1) ** ((k - 1) // 2) / math.factorial(k), R(7), ALU.add, ALU.mult))
            link(V.scalar_tensor_tensor(R(8), R(8), 1.0, R(6), ALU.add, ALU.mult))
            link(V.tensor_scalar(R(9), R(7), -1.0 / math.factorial(14), None, ALU.mult))
            for k in (12, 10, 8, 6, 4, 2):
                link(V.scalar_tensor_tensor(R(9), R(9), (-1) ** (k // 2) / math.factorial(k), R(7), ALU.add, ALU.mult))
            link(V.tensor_scalar(R(9), R(9), 1.0, None, ALU.add))
            link(V.tensor_tensor(R(10), R(8), R(8), ALU.mult))
            link(V.tensor_scalar(R(20), R(10), -2.0, 1.0, ALU.mult, ALU.add))
            link(V.scalar_tensor_tensor(R(21), R(8), -2.0, R(9), ALU.mult, ALU.mult))
            link(V.tensor_tensor(R(10), R(4), R(20), ALU.mult))
            link(V.tensor_scalar(R(10), R(10), 1.0, None, ALU.subtract))
            link(V.scalar_tensor_tensor(R(11), R(4), -1.0, R(21), ALU.mult, ALU.mult))
            link(V.tensor_tensor(R(12), R(0), R(0), ALU.mult))
            link(V.tensor_tensor(R(13), R(1), R(1), ALU.mult))
            link(V.tensor_tensor(R(12), R(12), R(13), ALU.add))
            link(V.reciprocal(R(13), R(12)))
            link(V.tensor_tensor(R(14), R(10), R(0), ALU.mult))
            link(V.tensor_tensor(R(15), R(11), R(1), ALU.mult))
            link(V.tensor_tensor(R(14), R(14), R(15), ALU.add))
            link(V.tensor_tensor(R(22), R(14), R(13), ALU.mult))
            link(V.tensor_tensor(R(14), R(11), R(0), ALU.mult))
            link(V.tensor_tensor(R(15), R(10), R(1), ALU.mult))
            link(V.tensor_tensor(R(14), R(14), R(15), ALU.subtract))
            link(V.tensor_tensor(R(23), R(14), R(13), ALU.mult))
            V.tensor_copy(R(19), R(4)).then_inc(sp_done, 1)
            v.wait_ge(sT_done, 1)
            link(V.tensor_copy(scol[:, :, :], at[1][:, 0:5 * ST].rearrange("p (k j) -> p k j", j=ST)))
            m4 = rowm[:, :].unsqueeze(2).broadcast_to([P, 4, P])
            v.wait_ge(xnorm, TB)
            for n_ in range(8):
                k, q = n_ // 4, n_ % 4
                v.wait_ge(bT_done, n_ + 1)
                V.tensor_tensor(bpad[:, k, 4 * q:4 * q + 4, :], at[2 + n_ % 2][:, 0:P].unsqueeze(1).broadcast_to([P, 4, P]),
                                m4, ALU.mult).then_inc(bT_evac, 1)
            v.wait_ge(cT_done, 2)
            fre = scol[:, 3, :].unsqueeze(2).broadcast_to([P, ST, 32])
            fim = scol[:, 4, :].unsqueeze(2).broadcast_to([P, ST, 32])
            cr = at[0][:, :].rearrange("p (j c) -> p j c", c=32)
            ci = at[1][:, :].rearrange("p (j c) -> p j c", c=32)
            tc1 = reg_d[:, 0:512].rearrange("p (j c) -> p j c", c=32)
            tc2 = reg_d[:, 512:1024].rearrange("p (j c) -> p j c", c=32)
            for o, (f0, f1, op, sg) in enumerate(((fre, fim, ALU.subtract, 1.0), (fim, fre, ALU.add, -1.0))):
                link(V.tensor_tensor(tc1, cr, f0, ALU.mult))
                link(V.tensor_tensor(tc2, ci, f1, ALU.mult))
                link(V.tensor_tensor(tc1, tc1, tc2, op))
                for h in range(2):
                    last = V.tensor_scalar(crT[:, o, :, 16 * h:16 * h + 16], tc1[:, :, 16 * h:16 * h + 16],
                                           cmask[:, h:h + 1], sg, ALU.mult, ALU.mult)
                last.then_inc(c_ready, 1)
                v.wait_ge(c_ready, o + 1)
            v.wait_ge(k_zero, 1)
            link(V.tensor_copy(pw[:, 0:2, :], scol[:, 1:3, :]))
            w_ = 1
            while w_ < T:
                pr = pw[:, 0, :].unsqueeze(2).broadcast_to([P, ST, w_])
                pi = pw[:, 1, :].unsqueeze(2).broadcast_to([P, ST, w_])
                er, ei = ph[:, 0, :, 0:w_], ph[:, 1, :, 0:w_]
                t1 = reg_d[:, 0:2048].rearrange("p (j t) -> p j t", j=ST)[:, :, 0:w_]
                t2 = reg_d[:, 2048:4096].rearrange("p (j t) -> p j t", j=ST)[:, :, 0:w_]
                V.tensor_tensor(t1, er, pr, ALU.mult)
                link(V.tensor_tensor(t2, ei, pi, ALU.mult))
                link(V.tensor_tensor(ph[:, 0, :, w_:2 * w_], t1, t2, ALU.subtract))
                V.tensor_tensor(t1, er, pi, ALU.mult)
                link(V.tensor_tensor(t2, ei, pr, ALU.mult))
                link(V.tensor_tensor(ph[:, 1, :, w_:2 * w_], t1, t2, ALU.add))
                w_ *= 2
                if w_ < T:
                    V.tensor_tensor(pw[:, 2, :], pw[:, 0, :], pw[:, 0, :], ALU.mult)
                    link(V.tensor_tensor(pw[:, 3, :], pw[:, 1, :], pw[:, 1, :], ALU.mult))
                    link(V.scalar_tensor_tensor(pw[:, 1, :], pw[:, 0, :], 2.0, pw[:, 1, :], ALU.mult, ALU.mult))
                    link(V.tensor_tensor(pw[:, 0, :], pw[:, 2, :], pw[:, 3, :], ALU.subtract))

            def ph_b(k, j):
                return ph[:, k, j, :].unsqueeze(1).broadcast_to([P, 2, T])

            def s_products(j):
                v.wait_ge(bu_done, j + 1)
                if j >= 2:
                    v.wait_ge(s_rot, j - 1)
                bu = v3(at[j % 2][:, :], T)
                V.tensor_tensor(s_ab[j % 2][:, 0, :, :], bu, ph_b(0, j), ALU.mult)
                V.tensor_tensor(s_ab[j % 2][:, 1, :, :], bu, ph_b(1, j), ALU.mult).then_inc(s_prod, 1)

            def s_scans(j):
                v.wait_ge(s_rot, j + 1)
                rr = scol[:, 0, j:j + 1].broadcast_to([P, T])
                if j:
                    v.wait_ge(s_out, j)
                for k in range(2):
                    last = V.tensor_tensor_scan(s_w[:, k, :], rr, s_v[j % 2][:, k, :], 0.0, ALU.mult, ALU.add)
                last.then_inc(s_scan, 1)
                v.wait_ge(s_scan, j + 1)
                if j >= 2:
                    v.wait_ge(s_state, j - 1)
                V.tensor_tensor(s_df[j % 2][:, 0, :, :], s_w[:, :, :], ph_b(0, j), ALU.mult)
                V.tensor_tensor(s_df[j % 2][:, 1, :, :], s_w[:, :, :], ph_b(1, j), ALU.mult).then_inc(s_out, 1)

            def s_skip(q):
                v.wait_ge(sy_used, 4 * q + 4)
                V.scalar_tensor_tensor(uT[:, q, :], uT[:, q, :], d_sk[:, q:q + 1], at[2 + q % 2][:, 0:T],
                                       ALU.mult, ALU.add).then_inc(sy_evac, 1)

            for j in range(ST + 1):
                if j < ST:
                    s_products(j)
                if j >= 1:
                    s_scans(j - 1)
                if j >= 8 and j % 4 == 0:
                    s_skip(j // 4 - 2)
            s_skip(3)
            for q in range(4):
                v.wait_ge(glu_sig, q + 1)
            last = V.tensor_tensor(uT[:, :, :], uT[:, :, :], glu_s[:, :, :], ALU.mult)
            last.then_inc(glu_y, 1)

            def norm_four(n_, first, gain):
                v.wait_ge(nrt, n_)
                link(V.reciprocal(rstd_t, rstd_t))
                for q in range(4):
                    last = V.scalar_tensor_tensor(yT[:, first + q, :], yT[:, first + q, :], gain[:, q:q + 1], rstd_t,
                                                  ALU.mult, ALU.mult)
                last.then_inc(ny, 1)
            norm_four(1, 4, g_ssm)
            for i in range(2):
                link(V.tensor_tensor(lamv[:, 2 * i, :], lamv[:, 2 * i, :], lamv[:, 2 * i + 1, :], ALU.mult))
                last = V.reduce_sum(lam_s[:, i:i + 1], lamv[:, 2 * i, :], axis=AX)
            last.then_inc(lam_sum, 1)
            for hp in range(SBH // 2):
                v.wait_ge(z_abs, 6 * hp + 6)
                if hp:
                    v.wait_ge(z_cum, hp)
                for k in range(2):
                    last = V.scalar_tensor_tensor(sp_t[:, k, :], at[k][:, 0:384], 0.0, sp_a[:, k, :], ALU.max, ALU.add)
                last.then_inc(z_sp, 1)
            norm_four(2, 0, g_sb)
            v.wait_ge(lam_exp, 1)
            link(V.tensor_tensor(lam_s[:, 4:5], lam_s[:, 2:3], lam_s[:, 3:4], ALU.subtract))
            link(V.tensor_scalar(lam_s[:, 5:6], lam_s[:, 4:5], LAM_INIT, None, ALU.add))
            link(V.tensor_scalar(g_df, g_df, 1.0 - LAM_INIT, None, ALU.mult))

            def df_max(h):
                v.wait_ge(d_sc, h + 1)
                if h >= 2:
                    v.wait_ge(d_a, h - 1)
                mx = dfc[:, h % 2, 8:12]
                V.reduce_max(mx[:, 0:2], at[0][:, 0:2 * P].rearrange("p (r k) -> p r k", r=2), axis=AX)
                link(V.reduce_max(mx[:, 2:4], at[1][:, :].rearrange("p (r k) -> p r k", r=2), axis=AX))
                V.tensor_scalar(dfc[:, h % 2, 0:4], mx, -1.0, None, ALU.mult).then_inc(d_max, 1)

            def df_diff(h):
                v.wait_ge(d_exp, h + 1)
                ri = dfc[:, h % 2, 12:16]
                link(V.reciprocal(ri, dfc[:, h % 2, 4:8]))
                link(V.tensor_scalar(ri[:, 1:4:2], ri[:, 1:4:2], lam_s[:, 5:6], None, ALU.mult))
                V.tensor_scalar(df_t[:, 0:P], df_p0[:, P:2 * P], ri[:, 1:2], None, ALU.mult)
                link(V.tensor_scalar(df_t[:, P:3 * P], df_p1[:, T:2 * T], ri[:, 3:4], None, ALU.mult))
                if h:
                    v.wait_ge(d_tr, h)
                V.scalar_tensor_tensor(df_a[:, 0:P], df_p0[:, 0:P], ri[:, 0:1], df_t[:, 0:P], ALU.mult, ALU.subtract)
                V.scalar_tensor_tensor(df_a[:, P:3 * P], df_p1[:, 0:T], ri[:, 2:3], df_t[:, P:3 * P],
                                       ALU.mult, ALU.subtract).then_inc(d_a, 1)
                v.wait_ge(d_tr, h + 1)
                if h:
                    v.wait_ge(d_pv, h)
                V.tensor_copy(df_aT, at[2][:, 0:384]).then_inc(d_aT, 1)

            for h in range(DFH):
                df_max(h)
                df_diff(h)
            for h in range(DFH):
                v.wait_ge(nrt, 3 + h)
                link(V.reciprocal(df_t[:, 0:T], rstd_t))
                V.scalar_tensor_tensor(yT[:, 8 + h, :], yT[:, 8 + h, :], g_df, df_t[:, 0:T], ALU.mult, ALU.mult).then_inc(ny, 1)
            v.wait_ge(x2_in, 16 * TB)
            for k in range(4):
                v.wait_ge(*((unit_used, 2 * NB + 3), (unit_used, 2 * NB + 4), (slot_free, 4), (slot_free, 6))[k])
                for b in range(TB):
                    w = slice(512 * k, 512 * k + 512)
                    V.tensor_tensor(xt[:, b, w], pj[2 * (k % 2) + b][:, :], xt[:, b, w], ALU.add).then_inc(h_add, 1)
            v.wait_ge(h_sq, TB)
            V.tensor_scalar(rmsc[:, 2:4], rmsc[:, 8:10], 1.0 / D, EPS, ALU.mult, ALU.add).then_inc(h_rs, 1)
            v.wait_ge(achain, 2)
            V.reciprocal(rmsc[:, 10:12], rmsc[:, 4:6]).then_inc(h_rs, 1)
            for b in range(TB):
                v.wait_ge(h_hi, b + 1)
                V.tensor_tensor(hr1[:, b, :], hn[:, b, :], hi[:, b, :], ALU.subtract).then_inc(h_r1, 1)
                v.wait_ge(h_mid, b + 1)
                V.tensor_tensor(lo[:, b, :], hr1[:, b, :], mid[:, b, :], ALU.subtract).then_inc(h_lo, 1)
            v.wait_ge(rt_done, 1)
            v.wait_ge(rw_in, 16 * 7)
            for b in range(TB):
                link(V.tensor_tensor(lg[:, b, :], at[0][:, 36 * b:36 * b + 36], rbias[:, :], ALU.add))

            def first_hit(dst, src, mx, tmp, w):
                link(V.tensor_scalar(tmp, src, mx, None, ALU.is_ge))
                link(V.tensor_tensor_scan(dst, ones[:, 0:w], tmp, 0.0, ALU.mult, ALU.add))
                link(V.scalar_tensor_tensor(dst, dst, 1.0, tmp, ALU.is_equal, ALU.mult))

            def tmp_(b, i, w):
                o = 48 * b + i
                return rtmp[:, o:o + w]
            for b in range(TB):
                gm, goh, tp, el, e1, m1, m2, e2 = (tmp_(b, 0, 1), tmp_(b, 1, 4), tmp_(b, 5, 8), tmp_(b, 13, 8), tmp_(b, 21, 8),
                                                  tmp_(b, 29, 1), tmp_(b, 30, 1), tmp_(b, 31, 8))
                link(V.reduce_max(gm, lg[:, b, 0:4], axis=AX))
                first_hit(goh, lg[:, b, 0:4], gm, tp[:, 0:4], 4)
                link(V.tensor_scalar(rtmp[:, 96 + 5 * b:100 + 5 * b], lg[:, b, 0:4], gm, None, ALU.subtract))
                link(V.tensor_scalar(el, lg[:, b, 4:12], goh[:, 0:1], None, ALU.mult))
                for k in range(1, NG):
                    link(V.scalar_tensor_tensor(el, lg[:, b, 4 + 8 * k:12 + 8 * k], goh[:, k:k + 1], el, ALU.mult, ALU.add))
                link(V.reduce_max(m1, el, axis=AX))
                first_hit(e1, el, m1, tp, 8)
                link(V.scalar_tensor_tensor(el, e1, NEG, el, ALU.mult, ALU.add))
                link(V.reduce_max(m2, el, axis=AX))
                first_hit(e2, el, m2, tp, 8)
                V.tensor_tensor(rtmp[:, 100 + 5 * b:101 + 5 * b], m2, m1, ALU.subtract).then_inc(rt_m, 1)
            v.wait_ge(rt_e, 1)
            for b in range(TB):
                goh, e1, e2 = tmp_(b, 1, 4), tmp_(b, 21, 8), tmp_(b, 31, 8)
                ex = rtmp[:, 128 + 5 * b:133 + 5 * b]
                gs, dn, w1_, w2_ = (rtmp[:, 140 + 8 * b + i:141 + 8 * b + i] for i in range(4))
                link(V.reduce_sum(gs, ex[:, 0:4], axis=AX))
                link(V.tensor_scalar(dn, ex[:, 4:5], 1.0, gs, ALU.add, ALU.mult))
                link(V.reciprocal(w1_, dn))
                link(V.tensor_tensor(w2_, w1_, ex[:, 4:5], ALU.mult))
                g8, s8 = rtmp[:, 160 + 16 * b:168 + 16 * b], rtmp[:, 168 + 16 * b:176 + 16 * b]
                link(V.tensor_scalar(g8, e1, w1_, None, ALU.mult))
                link(V.scalar_tensor_tensor(g8, e2, w2_, g8, ALU.mult, ALU.add))
                link(V.tensor_tensor(s8, e1, e2, ALU.add))
                for k in range(NG):
                    V.tensor_scalar(gat[:, b, 8 * k:8 * k + 8], g8, goh[:, k:k + 1], None, ALU.mult)
                    last = V.tensor_scalar(sel[:, b, 8 * k:8 * k + 8], s8, goh[:, k:k + 1], None, ALU.mult)
                link(last)
                V.tensor_copy(selb[:, b, :], sel[:, b, :]).then_inc(rt_sel, 1)
            v.wait_ge(rk_done, 1)
            rk = at[1][:, 0:2 * NE].rearrange("p (b e) -> p b e", e=NE)
            link(V.tensor_tensor(pos[:, :, :], rk, sel[:, :, :], ALU.mult))
            link(V.tensor_tensor(pos[:, :, :], pos[:, :, :], sel[:, :, :], ALU.add))
            V.tensor_scalar(posx[:, :, 0:NE], pos[:, :, :], 1.0, None, ALU.subtract)
            V.tensor_copy(gatx[:, :, 0:NE], gat[:, :, :]).then_inc(rk_ready, 1)
            cnt = at[2][:, 0:NE]
            link(V.tensor_scalar(x_n, cnt, float(SLOT), None, ALU.is_gt))
            for k in range(2, PASSES):
                link(V.tensor_scalar(x_c, cnt, float(SLOT * k), None, ALU.is_gt))
                link(V.tensor_tensor(x_n, x_n, x_c, ALU.add))
            link(V.tensor_tensor_scan(x_e, ones[:, 0:NE], x_n, 0.0, ALU.mult, ALU.add))
            link(V.tensor_tensor(x_c, x_e, x_n, ALU.subtract))
            V.tensor_copy(n_extra, x_e[:, NE - 1:NE])
            o8 = [P, EXTRA, NE]
            c8, e8 = x_c.unsqueeze(1).broadcast_to(o8), x_e.unsqueeze(1).broadcast_to(o8)
            i8 = iota_s[:, 0:EXTRA].unsqueeze(2).broadcast_to(o8)
            link(V.tensor_tensor(x_t[:, 0], i8, c8, ALU.is_ge))
            link(V.tensor_tensor(x_t[:, 1], i8, e8, ALU.is_lt))
            link(V.tensor_tensor(x_t[:, 0], x_t[:, 0], x_t[:, 1], ALU.mult))
            link(V.tensor_tensor(x_t[:, 1], x_t[:, 0], iota_s[:, 0:NE].unsqueeze(1).broadcast_to(o8), ALU.mult))
            link(V.reduce_sum(x_id, x_t[:, 1], axis=AX))
            V.tensor_copy(ids, x_id)
            for b in range(TB):
                link(V.tensor_tensor(x_t[:, 1], c8, i8, ALU.subtract))
                link(V.tensor_scalar(x_t[:, 1], x_t[:, 1], 1.0, float(SLOT), ALU.subtract, ALU.mult))
                link(V.tensor_tensor(x_t[:, 1], x_t[:, 1], posx[:, b, 0:NE].unsqueeze(1).broadcast_to(o8), ALU.add))
                link(V.tensor_tensor(x_t[:, 1], x_t[:, 1], x_t[:, 0], ALU.mult))
                link(V.tensor_tensor(x_t[:, 2], x_t[:, 0], gat[:, b, :].unsqueeze(1).broadcast_to(o8), ALU.mult))
                link(V.reduce_sum(posx[:, b, NE:], x_t[:, 1], axis=AX))
                last = V.reduce_sum(gatx[:, b, NE:], x_t[:, 2], axis=AX)
            last.then_inc(rk_ready, 1)
            v.wait_ge(rk_ready, 2)
            v.sem_inc(e_h, 1)
            gfb = g_ffn.unsqueeze(2).broadcast_to([P, DC, P])

            def v_items(i_, n0, nq):
                v.wait_ge(e_gt, i_ + 1)
                ob3 = [P, nq, SLOT]
                for b in range(TB):
                    at_s = posx[:, b, ds(n0, nq)].unsqueeze(2).broadcast_to(ob3)
                    last = V.tensor_tensor(selS[:, b, 0:nq, :], at_s, iota_s[:, :].unsqueeze(1).broadcast_to(ob3), ALU.is_equal)
                last.then_inc(e_sel, 1)
                v.wait_ge(e_sel, i_ + 1)
                for b in range(TB):
                    w = gatx[:, b, ds(n0, nq)].unsqueeze(2).broadcast_to(ob3)
                    last = V.tensor_tensor(selW[:, b, 0:nq, :], selS[:, b, 0:nq, :], w, ALU.mult)
                last.then_inc(e_selw, 1)
                ns = nq * SLOT
                for k in range(4):
                    v.wait_ge(e_gath, i_ * 4 + k + 1)
                    V.tensor_tensor(xeT[:, 4 * k:4 * k + 4, 0:ns], v3(psb[4 + k % 2][:, :], P)[:, :, 0:ns],
                                    gfb[:, 4 * k:4 * k + 4, 0:ns], ALU.mult).then_inc(e_gev, 1)
                v.wait_ge(e_gt, i_ + 2)
                V.tensor_copy(gT[0:ns, :], psb[6][0:ns, 0:256]).then_inc(e_gtev, 1)
                for q in range(nq):
                    n_ = n0 + q
                    v.wait_ge(slot_free, used(n_, 4))
                    v.wait_ge(e_hT, n_ + 1)
                    V.tensor_copy(a3, psb[1][:, :]).then_inc(e_a3, 1)
                    v.wait_ge(e_silu, n_ + 1)
                    V.tensor_tensor(hT[:, :, :], v3(psb[2][:, 256:512], SLOT), v3(hs, SLOT), ALU.mult).then_inc(e_h, 1)
                    v.wait_ge(slot_free, used(n_, 6))
                    v.wait_ge(e_comb, i_ * 8 + 1)
                    for b in range(2):
                        last = V.tensor_copy(ye[64 * q:64 * q + 64, 1024 + 512 * b:1536 + 512 * b],
                                             psb[4][64 * b:64 * b + 64, :])
                    last.then_inc(e_yev, 1)
                for k in range(8):
                    c, b = k // 2, k % 2
                    v.wait_ge(e_comb, i_ * 8 + k + 2)
                    w = slice(512 * c, 512 * c + 512)
                    V.tensor_tensor(xt[:, b, w], psb[6 + k % 2][:, :], xt[:, b, w], ALU.add).then_inc(e_acc, 1)

            with v.Fori(0, ITERS) as it:
                v_items(it, it * QE, QE)
            extra = v.value_load(n_extra[0:1, 0:1], min_val=0, max_val=EXTRA - 1)
            with v.If(extra > 0):
                with v.Fori(0, extra) as x_:
                    v_items(x_ + ITERS, x_ + NE, 1)
            v.wait_ge(f_sq, TB)
            V.tensor_scalar(rmsc[:, 2:4], rmsc[:, 12:14], 1.0 / D, EPS, ALU.mult, ALU.add).then_inc(f_rs, 1)
            v.wait_ge(f_sq, TB + 1)
            V.reciprocal(rmsc[:, 6:8], rmsc[:, 4:6]).then_inc(f_rs, 1)
            v.wait_ge(f_rs, 2)
            v.wait_ge(fg_in, 16)
            for b in range(TB):
                V.scalar_tensor_tensor(ob[:, b, :], xt[:, b, :], rmsc[:, 6 + b:7 + b], fg, ALU.mult, ALU.mult).then_inc(f_out, 1)

        @block.tensor
        def _(pe):
            M = nc.tensor.matmul
            TR = nc.tensor.transpose
            pe.wait_ge(cst, 1)
            pe.wait_ge(par_in, 16 * 18)
            for i in range(3):
                TR(at[0][:, 16 * i:16 * i + 16], prow[:, i, :], ident[0:16, 0:16])
            last = TR(at[0][:, 48:49], prow[0:1, 3, :], ident[0:1, 0:1])
            last.then_inc(pT_done, 1)
            pe.wait_ge(b_in, 16 * 4)
            for n_ in range(8):
                k, q = n_ // 4, n_ % 4
                if n_ >= 2:
                    pe.wait_ge(bT_evac, n_ - 1)
                TR(at[2 + n_ % 2][:, 0:P], bnat[:, k, 4 * q:4 * q + 4, :].rearrange("p a c -> p (a c)"), ident[:, :]).then_inc(bT_done, 1)
                if n_ == 1:
                    for m in range(DC // 2):
                        pe.wait_ge(xnorm, TB)
                        if m >= 4:
                            pe.wait_ge(tr_evac, m - 3)
                        for k2 in range(2):
                            for b in range(TB):
                                c = 2 * m + k2
                                last = TR(pj[m % 4][:, k2 * T + b * P:k2 * T + b * P + P], xn[:, b, c * P:(c + 1) * P], ident[:, :])
                        last.then_inc(tr_done, 1)
                    pe.wait_ge(sp_done, 1)
                    for i in range(5):
                        last = TR(at[1][:, 16 * i:16 * i + 16], spar[:, 19 + i, :], ident[0:16, 0:16])
                    last.then_inc(sT_done, 1)
            pe.wait_ge(pT_evac, 1)
            for k, cn in enumerate((cnat, cnat2)):
                if k == 1:
                    pe.wait_ge(bT_evac, 1)
                for q in range(4):
                    last = TR(at[k][:, P * q:P * q + P], cn[:, q, :, :].rearrange("p d n -> p (d n)"), ident[:, :])
                last.then_inc(cT_done, 1)

            def wait_unit(n_):
                pe.wait_ge(ring_in[n_ % SLOTS_A], 16 * (n_ // SLOTS_A + 1))

            def project(n_, half, ct):
                kind = BLOCKS[n_][0]
                u = 2 * n_ + half
                w = unit(u % SLOTS_A)
                if ct == 0:
                    wait_unit(u)
                    if half == 0 and n_ >= 2:
                        pe.wait_ge(pj_evac, n_ - 1)
                    if half == 0 and n_ < 2:
                        pe.wait_ge(tr_evac, DC // 2)
                bank = pj[2 * (n_ % 2) + (ct if kind in ("sbv", "dfv") else ct // 2)]
                for c in range(8):
                    cc = 8 * half + c
                    if kind in ("sbv", "dfv"):
                        last = M(bank[:, :], xnT[:, cc, ct * P:(ct + 1) * P], w[:, c, :], start=cc == 0, stop=cc == DC - 1)
                    else:
                        last = M(bank[:, (ct % 2) * T:(ct % 2) * T + T], w[:, c, ct * P:(ct + 1) * P], xnT[:, cc, :],
                                 start=cc == 0 and ct % 2 == 0, stop=cc == DC - 1, skip_group_check=True)
                if ct == (1 if kind in ("sbv", "dfv") else 3):
                    last.then_inc(unit_used, 1)

            def s_in(j):
                if j == 0:
                    pe.wait_ge(bT_evac, 8)
                    pe.wait_ge(pj_evac, 1)
                    pe.wait_ge(c_ready, 2)
                if j >= 2:
                    pe.wait_ge(s_prod, j - 1)
                for k in range(2):
                    last = M(at[j % 2][:, k * T:(k + 1) * T], bpad[:, k, j, :], uT[:, j // 4, :], start=True, stop=True)
                last.then_inc(bu_done, 1)

            def s_y(j):
                pe.wait_ge(s_state, j + 1)
                q, i = j // 4, j % 4
                if q >= 2 and i == 0:
                    pe.wait_ge(sy_evac, q - 1)
                o = at[2 + q % 2][32 * i:32 * i + 32, 0:T]
                M(o, crT[:, 0, j, :], s_s[j % 2][:, 0, :], start=True, stop=False)
                last = M(o, crT[:, 1, j, :], s_s[j % 2][:, 1, :], start=False, stop=True)
                last.then_inc(sy_used, 1)

            for half in range(2):
                for ct in range(4):
                    project(0, half, ct)
            step = 0
            for n_ in (1, 2, 3):
                for half in range(2):
                    for ct in range(2 if n_ == 3 else 4):
                        project(n_, half, ct)
                        if 1 <= step < ST + 1:
                            s_in(step - 1)
                        if 3 <= step < ST + 3:
                            s_y(step - 3)
                        step += 1
            def glu():
                pe.wait_ge(glu_in, 16)
                pe.wait_ge(gelu_s, 4)
                for co in range(4):
                    for c in range(4):
                        last = M(at[co // 2][:, (co % 2) * T:(co % 2) * T + T], glu_w[:, c, co * P:(co + 1) * P], uT[:, c, :],
                                 start=c == 0, stop=c == 3)
                    last.then_inc(glu_done, 1)

            def sums4(n_, bank):
                pe.wait_ge(nsq, n_)
                for q in range(4):
                    last = M(bank[:, 0:T], ones[:, :], nrm_sq[:, q, :], start=q == 0, stop=q == 3)
                last.then_inc(nsum, 1)

            def sb_scores(hp):
                if hp == 0:
                    pe.wait_ge(pj_evac, 4)
                    pe.wait_ge(glu_sig, 4)
                else:
                    pe.wait_ge(z_w, hp)
                for k in range(2):
                    h = 2 * hp + k
                    z = at[k]
                    M(z[:, 0:T], sk[:, h, 0:P], sq[:, hp, :], start=True, stop=True, skip_group_check=True)
                    M(z[:, T:T + P], sk[:, h, P:T], sq[:, hp, P:T], start=False, stop=True, skip_group_check=True)
                    M(z[:, 0:P], ident_b[:, :], smask_b[:, :], start=False, stop=True, skip_group_check=True)
                    last = M(z[:, T:T + P], ident_b[:, :], smask_b[:, :], start=False, stop=True, skip_group_check=True)
                last.then_inc(z_done, 1)

            def sb_cum(hp):
                pe.wait_ge(z_sp, hp + 1)
                for k in range(2):
                    z = at[k]
                    M(z[:, 0:T], tri_neg[:, :], sp_t[:, k, 0:T], start=False, stop=True, skip_group_check=True)
                    M(z[:, P:T], ones_neg[:, :], sp_t[:, k, T:T + P], start=False, stop=True, skip_group_check=True)
                    last = M(z[:, T:T + P], tri_neg[:, :], sp_t[:, k, T:T + P], start=False, stop=True, skip_group_check=True)
                last.then_inc(z_cum, 1)

            def sb_out(hp):
                pe.wait_ge(z_w, hp + 1)
                if hp:
                    pe.wait_ge(sbo_evac, hp)
                else:
                    pe.wait_ge(nrt, 1)
                for k in range(2):
                    h = 2 * hp + k
                    o = at[2][64 * k:64 * k + 64, :]
                    M(o[:, 0:T], sv[:, 0, 64 * h:64 * h + 64], sb_w[:, k, 0:T], start=True, stop=True)
                    last = M(o[:, P:T], sv[:, 1, 64 * h:64 * h + 64], sb_w[:, k, T:T + P], start=False, stop=True, skip_group_check=True)
                last.then_inc(sbo_done, 1)

            for n_ in (4, 5, 6):
                for half in range(2):
                    for ct in range(2 if n_ == 6 else 4):
                        project(n_, half, ct)
                        at_ = (n_, half, ct)
                        if at_ == (4, 0, 1):
                            glu()
                        if at_ == (4, 0, 2):
                            sums4(1, at[2])
                            sb_scores(0)
                        if at_ == (4, 0, 3):
                            sb_cum(0)
                        if at_ == (4, 1, 0):
                            sb_out(0)
                            sb_scores(1)
                        if at_ == (4, 1, 1):
                            sb_cum(1)
                        if at_ == (4, 1, 2):
                            sb_out(1)
                            sb_scores(2)
                        if at_ == (4, 1, 3):
                            sb_cum(2)
                        if at_ == (5, 0, 0):
                            sb_out(2)
                            sb_scores(3)
                        if at_ == (5, 0, 1):
                            sb_cum(3)
                        if at_ == (5, 0, 2):
                            sb_out(3)
                        if at_ == (5, 1, 0):
                            sums4(2, at[3])

            def df_scores(h):
                if h == 0:
                    pe.wait_ge(pj_evac, 7)
                    pe.wait_ge(nrt, 2)
                if h == 4:
                    pe.wait_ge(pj_evac, NB)
                if h:
                    pe.wait_ge(d_exp, h)
                M(at[0][:, 0:2 * P], dq[:, h, 0:P], dk[:, h, :, 0:P], start=True, stop=False)
                M(at[0][:, 0:2 * P], ident_b[:, :], mask_b[:, :, :], start=False, stop=True)
                M(at[1][:, :], dq[:, h, P:T], dk[:, h, :, :], start=True, stop=True)
                M(at[1][:, :].rearrange("p (r k) -> p r k", r=2)[:, :, P:T], ident_b[:, :], mask_b[:, :, :],
                  start=False, stop=True, skip_group_check=True).then_inc(d_sc, 1)

            def df_tr(h):
                pe.wait_ge(d_a, h + 1)
                if h:
                    pe.wait_ge(d_aT, h)
                for k in range(3):
                    last = TR(at[2][:, k * P:(k + 1) * P], df_a[:, k * P:(k + 1) * P], ident[:, :])
                last.then_inc(d_tr, 1)

            def df_out(h):
                pe.wait_ge(d_aT, h + 1)
                if h:
                    pe.wait_ge(d_y, h)
                o = at[3][:, (h % 2) * T:(h % 2) * T + T]
                M(o, dv[:, 0, h * P:(h + 1) * P], df_aT[:, 0:T], start=True, stop=True)
                M(o[:, P:T], dv[:, 1, h * P:(h + 1) * P], df_aT[:, T:T + P], start=False, stop=True,
                  skip_group_check=True).then_inc(d_pv, 1)

            k_ = 0
            for n_ in (7, 8, 9):
                for half in range(2):
                    for ct in range(2 if n_ == 9 else 4):
                        project(n_, half, ct)
                        h, what = k_ // 4, k_ % 4
                        if h < 4:
                            (df_scores if what == 0 else df_tr if what == 2 else df_out if what == 3 else (lambda h: None))(h)
                        k_ += 1

            def out_unit(n_, parts=(0, 1)):
                o_, half = OUT_UNITS[n_]
                u = 2 * NB + n_
                w = unit(u % SLOTS_A)
                for b in parts:
                    if b == 0:
                        wait_unit(u)
                        if half == 0 and o_ < 2:
                            pe.wait_ge(pj_evac, NB)
                        if half == 0 and o_ >= 2:
                            pe.wait_ge(h_add, 2 * (o_ - 1))
                        if n_ == 0:
                            pe.wait_ge(ny, 2)
                        if n_ == 2:
                            pe.wait_ge(ny, 2 + DFH)
                            pe.sem_inc(slot_free, SLOTS_B - SLOTS_A)
                    for c in range(8):
                        cc = 8 * half + c
                        last = M(pj[2 * (o_ % 2) + b][:, :], yT[:, cc, b * P:(b + 1) * P], w[:, c, :], start=cc == 0, stop=cc == DC - 1)
                    if b == 1:
                        last.then_inc(slot_free if n_ >= len(OUT_UNITS) - SLOTS_A else unit_used, 1)

            def df_sums(h):
                pe.wait_ge(nsq, 3 + h)
                if h == 0:
                    pe.wait_ge(d_exp, DFH)
                if h >= 2:
                    pe.wait_ge(nrt, 2 + h - 1)
                M(at[h % 2][:, 0:T], ones[:, :], df_sq[:, (h % 2) * T:(h % 2) * T + T], start=True, stop=True).then_inc(nsum, 1)

            df_scores(4)
            for h in range(4, DFH):
                if h % 2 == 0:
                    out_unit((h - 4) // 2, (0,))
                else:
                    out_unit((h - 5) // 2, (1,))
                df_tr(h)
                if h + 1 < DFH:
                    df_scores(h + 1)
                df_out(h)
            for h in range(DFH):
                df_sums(h)
            for n_ in range(2, 8):
                out_unit(n_)
            pe.wait_ge(hn_s, TB)
            for m in range(DC // 2):
                if m < 4:
                    pe.wait_ge(h_add, 4 * TB)
                else:
                    pe.wait_ge(tr_evac, DC // 2 + m - 3)
                for k2 in range(2):
                    for b in range(TB):
                        c = 2 * m + k2
                        last = TR(pj[m % 4][:, k2 * T + b * P:k2 * T + b * P + P], hn[:, b, c * P:(c + 1) * P], ident[:, :])
                last.then_inc(tr_done, 1)
            pe.wait_ge(tr_evac, DC)
            pe.wait_ge(rw_in, 16 * 7)
            for b in range(TB):
                for c in range(DC):
                    last = M(at[0][:, 36 * b:36 * b + 36], xnT[:, c, b * P:(b + 1) * P], rw[:, c, :], start=c == 0, stop=c == DC - 1)
            last.then_inc(rt_done, 1)
            pe.wait_ge(rt_sel, TB)
            M(at[1][:, 0:NE], before_b[:, :], selb[:, 0, :], start=True, stop=True)
            M(at[1][:, NE:2 * NE], before_b[:, :], selb[:, 1, :], start=True, stop=False)
            M(at[1][:, NE:2 * NE], ones_b[:, :], selb[:, 0, :], start=False, stop=True)
            M(at[2][:, 0:NE], ones_b[:, :], selb[:, 0, :], start=True, stop=False)
            M(at[2][:, 0:NE], ones_b[:, :], selb[:, 1, :], start=False, stop=True).then_inc(rk_done, 1)
            pe.wait_ge(h_lo, TB)
            pe.sem_inc(e_gt, 1)
            pe.sem_inc(e_hT, 1)
            pe.sem_inc(e_comb, 1)
            pe.sem_inc(e_yev, 1)

            def landed(n_, k):
                s = slot_of(k)
                base = 16 * (UNITS_A // SLOTS_A) if s < SLOTS_A else 0
                pe.wait_ge(ring_in[s], n_ * 16 + base + 16)
                return s

            def pe_items(i_, n0, nq):
                ns = nq * SLOT
                pe.wait_ge(e_sel, i_ + 1)
                for c in range(DC):
                    if c % 4 == 0 and c >= 8:
                        pe.wait_ge(e_gev, i_ * 4 + c // 4 - 1)
                    k = 0
                    for part in (hi, mid, lo):
                        for b in range(TB):
                            last = M(psb[4 + (c // 4) % 2][:, (c % 4) * P:(c % 4) * P + ns], part[:, b, c * P:(c + 1) * P],
                                     selS[:, b, 0:nq, :].rearrange("p q s -> p (q s)"), start=k == 0, stop=k == 5)
                            k += 1
                    if c % 4 == 3:
                        last.then_inc(e_gath, 1)
                pe.wait_ge(e_selw, i_ + 1)
                for b in range(TB):
                    last = TR(psb[6][:, b * P:b * P + P], selW[:, b, :, :].rearrange("p q s -> p (q s)"), ident[:, :])
                last.then_inc(e_gt, 1)
                pe.wait_ge(e_gev, i_ * 4 + 4)
                pe.wait_ge(e_gtev, i_ + 1)
                for q in range(nq):
                    n_ = n0 + q
                    for m in range(2):
                        for half in range(2):
                            s = landed(n_, 2 * m + half)
                            for c in range(8):
                                cc = 8 * half + c
                                i = c % 2
                                last = M(psb[m][64 * i:64 * i + 64, :], xeT[:, cc, 64 * q:64 * q + 64], unit(s)[:, c, :],
                                         start=cc < 2, stop=cc >= DC - 2)
                            last.then_inc(slot_free, 1)
                    for m, (ready, src) in enumerate(((e_a1, a1), (e_a3, a3))):
                        pe.wait_ge(ready, n_ + 1)
                        for f in range(EC):
                            last = M(psb[2][:, 256 * m + 64 * f:256 * m + 64 * f + 64], src[:, f * P:(f + 1) * P], stack2[:, :],
                                     start=True, stop=True)
                    last.then_inc(e_hT, 1)
                    pe.wait_ge(e_h, n_ + 2)
                    pe.wait_ge(e_yev, n_ * 2 + 1)
                    for half in range(2):
                        s = landed(n_, 4 + half)
                        for f in range(2):
                            for i in range(4):
                                last = M(psb[3 + i // 2][64 * (i % 2):64 * (i % 2) + 64, :], hT[:, 2 * half + f, :],
                                         unit2(s)[:, f, 512 * i:512 * i + 512],
                                         start=half == 0 and f == 0, stop=half == 1 and f == 1)
                        last.then_inc(slot_free, 1)
                pe.wait_ge(e_yev, n0 * 2 + 2 * nq + 1)
                for k in range(8):
                    c, b = k // 2, k % 2
                    if k >= 2:
                        pe.wait_ge(e_acc, i_ * 8 + k - 1)
                    M(psb[6 + k % 2][:, :], gT[0:ns, b * P:b * P + P], ye[0:ns, 512 * c:512 * c + 512],
                      start=True, stop=True).then_inc(e_comb, 1)

            with pe.Fori(0, ITERS) as it:
                pe_items(it, it * QE, QE)
            pe.wait_ge(rk_ready, 2)
            extra = pe.value_load(n_extra[0:1, 0:1], min_val=0, max_val=EXTRA - 1)
            with pe.If(extra > 0):
                with pe.Fori(0, extra) as x_:
                    pe_items(x_ + ITERS, x_ + NE, 1)


_INS = ['x', 'norm_mix_g', 'w_in', 'sb_norm_g', 'ssm_lam_re', 'ssm_lam_im', 'ssm_b_re', 'ssm_b_im', 'ssm_c_re',
        'ssm_c_im', 'ssm_d', 'ssm_log_dt', 'ssm_w_glu', 'ssm_b_glu', 'ssm_norm_g', 'diff_lq1', 'diff_lk1',
        'diff_lq2', 'diff_lk2', 'diff_subln_g', 'w_out', 'norm_ffn_g', 'router_group_w', 'router_group_b',
        'router_expert_w', 'router_expert_b', 'expert_w1', 'expert_w3', 'expert_w2', 'final_norm_g']
_OUTS = [((1, T, D), 'float32')]


def kernel(**inputs):
    import numpy as _np
    import concourse.bacc as _bacc
    from concourse import mybir as _mybir
    from concourse.bass_utils import run_bass_kernel_spmd as _run

    nc = _bacc.Bacc("TRN2", target_bir_lowering=False, num_devices=1)
    arrays, args = {}, []
    for name in _INS:
        a = _np.ascontiguousarray(inputs[name])
        arrays[f"in_{name}_dram"] = a
        args.append(nc.dram_tensor(f"in_{name}_dram", a.shape, _mybir.dt.from_np(a.dtype), kind="ExternalInput").ap())
    for i, (shape, dtype) in enumerate(_OUTS):
        dt = _mybir.dt.from_np(_np.dtype(dtype))
        args.append(nc.dram_tensor(f"out_{i}_dram", shape, dt, kind="ExternalOutput").ap())
    build(nc, *args)
    r = _run(nc, [arrays], core_ids=[0])
    got = tuple(r.results[0][f"out_{i}_dram"] for i in range(len(_OUTS)))
    return got[0]
```

```python
import concourse.bass as bass
from concourse import mybir
from contextlib import ExitStack
import math

D = 2048
T = 256
P = 128
TB = T // P
DC = D // P
SBW = D // 4
SBH = SBW // 64
SSW = D // 4
SG, SN, SC = SSW // 16, 64, 16
ST = SG * SN // P
DFH = (D - SBW - SSW) // 128
IN_COLS = 3 * SBW + SSW + 3 * (D - SBW - SSW)
NG, EPG = 4, 8
NE = NG * EPG
DE = D // 4
EC = DE // P
EPS = 1e-6
LAM_INIT = 0.8 - 0.6 * math.exp(-0.3 * 0)
QSCALE = 64 ** -0.5
NEG = -1e30

UW = 4096
SLOTS_A = 4
SLOTS_B = 6
SLOT = 64
QE = P // SLOT
ITERS = NE // QE
PASSES = T // SLOT
EXTRA = 8

BLOCKS = ([("u", 0, 3 * SBW)] + [("sbq", 0, 0), ("sbk", 0, SBW), ("sbv", 0, 2 * SBW)]
          + [(k, i, 3 * SBW + SSW + o * (D - SBW - SSW) + 512 * i)
             for i in range(2) for o, k in enumerate(("dfq", "dfk", "dfv"))])
NB = len(BLOCKS)
OUT_UNITS = [(0, 0), (1, 0), (0, 1), (1, 1), (2, 0), (2, 1), (3, 0), (3, 1)]
UNITS_A = 2 * NB + len(OUT_UNITS)


def build(nc, x, norm_mix_g, w_in, sb_norm_g, lam_re, lam_im, b_re, b_im, c_re, c_im, ssm_d, log_dt,
          w_glu, b_glu, ssm_norm_g, lq1, lk1, lq2, lk2, subln_g, w_out, norm_ffn_g,
          rg_w, rg_b, re_w, re_b, e_w1, e_w3, e_w2, final_g, out):
    F = mybir.dt.float32
    BF = mybir.dt.bfloat16
    I32 = mybir.dt.int32
    ALU = mybir.AluOpType
    ACT = mybir.ActivationFunctionType
    AX = mybir.AxisListType.X
    ds = bass.ds

    ctx = ExitStack()
    with ctx:
        def sb(name, shape, dt=F):
            return ctx.enter_context(nc.sbuf_tensor(name, shape, dt))

        def sem(name):
            return ctx.enter_context(nc.semaphore(name))

        ring4 = sb("ring4", [P, SLOTS_A * UW])
        reg_e = sb("reg_e", [P, 2 * UW])
        reg_x = sb("reg_x", [P, TB * D])
        reg_t = sb("reg_t", [P, DC * T])
        reg_y = sb("reg_y", [P, DC * T])
        reg_s = sb("reg_s", [P, 4096])
        reg_d = sb("reg_d", [P, 8192])

        def slot(s):
            return ring4[:, s * UW:(s + 1) * UW] if s < SLOTS_A else reg_e[:, (s - SLOTS_A) * UW:(s - SLOTS_A + 1) * UW]

        def slot_of(j):
            return (j + SLOTS_A) % SLOTS_B

        def used(n_, k):
            return n_ * 6 + SLOTS_B + k

        def unit(s):
            return slot(s).rearrange("p (c n) -> p c n", n=512)

        def unit2(s):
            return slot(s).rearrange("p (c n) -> p c n", n=D)

        def v3(ap, b):
            return ap.rearrange("p (a b) -> p a b", b=b)

        xt = v3(reg_x[:, :], D)
        xnT = v3(reg_t[:, :], T)
        yT = v3(reg_y[:, :], T)
        xn = v3(reg_y[:, :], D)
        uT = yT[:, 4:8, :]
        ph = reg_e[:, :].rearrange("p (k j t) -> p k j t", k=2, t=T)
        bpad = reg_x[:, :].rearrange("p (k j n) -> p k j n", k=2, n=P)
        s_ab = [reg_d[:, i * 1024:(i + 1) * 1024].rearrange("p (k r t) -> p k r t", k=2, t=T) for i in range(2)]
        s_v = [v3(reg_d[:, 2048 + i * 512:2560 + i * 512], T) for i in range(2)]
        s_w = v3(reg_d[:, 3072:3584], T)
        s_df = [reg_d[:, 3584 + i * 1024:4608 + i * 1024].rearrange("p (k r t) -> p k r t", k=2, t=T) for i in range(2)]
        s_s = [v3(reg_d[:, 5632 + i * 512:6144 + i * 512], T) for i in range(2)]
        bnat = reg_d[:, 6656:7680].rearrange("p (k j c) -> p k j c", k=2, c=32)
        cnat = reg_d[:, 7680:8192].rearrange("p (q d n) -> p q d n", q=4, d=2)
        cnat2 = reg_s[:, 0:512].rearrange("p (q d n) -> p q d n", q=4, d=2)
        sq = v3(reg_s[:, 0:1024], T)
        sk = v3(reg_s[:, 1024:3072], T)
        sv = v3(reg_s[:, 3072:4096], 512)
        dq = v3(reg_d[:, 0:2048], T)
        dk = reg_d[:, 2048:6144].rearrange("p (h r t) -> p h r t", h=DFH, r=2)
        dv = v3(reg_d[:, 6144:8192], 1024)
        glu_w = v3(reg_e[:, 0:2048], 512)
        glu_s = v3(reg_e[:, 2048:3072], T)
        nrm_sq = v3(reg_e[:, 3072:4096], T)
        sp_a = v3(reg_e[:, 4096:4864], 384)
        sp_e = v3(reg_e[:, 4864:5632], 384)
        sp_t = v3(reg_e[:, 5632:6400], 384)
        sb_w = v3(reg_e[:, 6400:7168], 384)
        df_p0 = reg_e[:, 0:256]
        df_p1 = reg_e[:, 256:768]
        df_t = reg_e[:, 768:1152]
        df_a = reg_e[:, 1152:1536]
        df_aT = reg_e[:, 1536:1920]
        df_sq = reg_e[:, 2048:3072]
        df_rt = reg_e[:, 3072:4096]
        rstd_t = reg_e[:, 7680:7936]

        ident = sb("ident", [P, P])
        ones = sb("ones", [P, P])
        tri_neg = sb("tri_neg", [P, P])
        ones_neg = sb("ones_neg", [P, P])
        ident_b = sb("ident_b", [P, P], BF)
        ones_b = sb("ones_b", [P, P], BF)
        before_b = sb("before_b", [P, P], BF)
        mask_b = sb("mask_b", [P, 2, P], BF)
        smask_b = sb("smask_b", [P, P], BF)
        stack2 = sb("stack2", [P, SLOT])
        rowm = sb("rowm", [P, 4])
        cmask = sb("cmask", [P, 2])
        iota_i = reg_s[:, 3072:3072 + SLOT].bitcast(I32)
        iota_s = sb("iota_s", [P, SLOT])
        prow = sb("prow", [DC, 4, P])
        pcol = sb("pcol", [P, 64])
        g_mix, g_ffn = pcol[:, 0:16], pcol[:, 16:32]
        g_sb, g_ssm, b_gl, d_sk = (pcol[:, 32 + 4 * i:36 + 4 * i] for i in range(4))
        g_df = pcol[:, 48:49]
        spar = reg_s[0:ST, 1024:1024 + 3 * P].rearrange("p (k n) -> p k n", n=P)
        sw = sb("sw", [P, 24, ST])
        scol = sw[:, 19:24, :]
        pw = sb("pw", [P, 4, ST])
        dt2 = sb("dt2", [ST, 2])
        ki = sb("ki", [P, ST], I32)
        crT = sb("crT", [P, 2, ST, 32])
        lamv = sb("lamv", [P, 4, 64])
        lam_s = sb("lam_s", [P, 8])
        rmsc = sb("rmsc", [P, 16])
        dfc = sb("dfc", [P, 2, 16])
        rw = sb("rw", [P, DC, 4 + NE])
        rbias = sb("rbias", [P, 4 + NE])

        psb = [ctx.enter_context(nc.psum_tensor(f"ps{i}", [P, 512], F)) for i in range(8)]
        pj, at = psb[0:4], psb[4:8]

        ring_in = [sem(f"ring_in{i}") for i in range(SLOTS_B)]
        unit_used = sem("unit_used")
        slot_free = sem("slot_free")
        x_in = [sem(f"x_in{i}") for i in range(2)]
        lam_in = sem("lam_in")
        par_in = sem("par_in")
        c_in = sem("c_in")
        lq_in = sem("lq_in")
        b_in = sem("b_in")
        glu_in = sem("glu_in")
        rw_in = sem("rw_in")
        x2_in = sem("x2_in")
        fg_in = sem("fg_in")
        cst = sem("cst")
        cst_z = sem("cst_z")
        b_zero = sem("b_zero")
        gchain = sem("gchain")
        vchain = sem("vchain")
        achain = sem("achain")
        xsum = sem("xsum")
        xnorm_v = sem("xnorm_v")
        tr_evac_v = sem("tr_evac_v")
        xnorm = sem("xnorm")
        rstd_s = sem("rstd_s")
        tr_done = sem("tr_done")
        tr_evac = sem("tr_evac")
        pT_done = sem("pT_done")
        pT_evac = sem("pT_evac")
        sp_done = sem("sp_done")
        sp_read = sem("sp_read")
        sT_done = sem("sT_done")
        sT_evac = sem("sT_evac")
        bT_done = sem("bT_done")
        bT_evac = sem("bT_evac")
        cT_done = sem("cT_done")
        c_ready = sem("c_ready")
        ph_ready = sem("ph_ready")
        pj_evac = sem("pj_evac")
        bu_done = sem("bu_done")
        s_prod = sem("s_prod")
        s_rot = sem("s_rot")
        s_scan = sem("s_scan")
        s_out = sem("s_out")
        s_state = sem("s_state")
        s_im = sem("s_im")
        sy_used = sem("sy_used")
        sy_evac = sem("sy_evac")
        gelu_s = sem("gelu_s")
        glu_done = sem("glu_done")
        glu_sig = sem("glu_sig")
        glu_y = sem("glu_y")
        nsq = sem("nsq")
        nsum = sem("nsum")
        nrt = sem("nrt")
        ny = sem("ny")
        k_zero = sem("k_zero")
        dk_zero = sem("dk_zero")
        z_done = sem("z_done")
        z_abs = sem("z_abs")
        z_sp = sem("z_sp")
        z_cum = sem("z_cum")
        z_w = sem("z_w")
        sbo_done = sem("sbo_done")
        sbo_evac = sem("sbo_evac")
        d_sc = sem("d_sc")
        d_max = sem("d_max")
        d_exp = sem("d_exp")
        d_a = sem("d_a")
        d_tr = sem("d_tr")
        d_aT = sem("d_aT")
        d_pv = sem("d_pv")
        d_y = sem("d_y")
        lam_sum = sem("lam_sum")
        lam_exp = sem("lam_exp")
        h_add = sem("h_add")
        h_sq = sem("h_sq")
        h_rs = sem("h_rs")
        hn_s = sem("hn_s")
        h_hi = sem("h_hi")
        h_r1 = sem("h_r1")
        h_r1_v = sem("h_r1_v")
        h_mid = sem("h_mid")
        h_lo = sem("h_lo")
        h_lo_v = sem("h_lo_v")
        rt_done = sem("rt_done")
        rt_sel = sem("rt_sel")
        rt_m = sem("rt_m")
        rt_e = sem("rt_e")
        rk_done = sem("rk_done")
        rk_ready = sem("rk_ready")
        e_sel = sem("e_sel")
        e_selw = sem("e_selw")
        e_gath = sem("e_gath")
        e_gev = sem("e_gev")
        e_gt = sem("e_gt")
        e_gtev = sem("e_gtev")
        e_a1 = sem("e_a1")
        e_a3 = sem("e_a3")
        e_hT = sem("e_hT")
        e_silu = sem("e_silu")
        e_h = sem("e_h")
        e_yev = sem("e_yev")
        e_comb = sem("e_comb")
        e_acc = sem("e_acc")
        f_sq = sem("f_sq")
        f_rs = sem("f_rs")
        f_out = sem("f_out")
        f_st = sem("f_st")

        block = ctx.enter_context(nc.Block())

        hi = reg_y[:, 0:2048].bitcast(BF).rearrange("p (b d) -> p b d", d=D)
        mid = reg_y[:, 2048:4096].bitcast(BF).rearrange("p (b d) -> p b d", d=D)
        lo = reg_s[:, 0:2048].bitcast(BF).rearrange("p (b d) -> p b d", d=D)
        lg = v3(reg_s[:, 2048:2048 + 2 * 36], 36)
        sel = v3(reg_s[:, 2128:2128 + 2 * NE], NE)
        selb = reg_s[:, 2256:2256 + NE].bitcast(BF).rearrange("p (b e) -> p b e", e=NE)
        x_cnt = reg_s[:, 2192:2192 + NE]
        x_q = v3(reg_s[:, 2288:2288 + 2 * NE], NE)
        rtmp = reg_s[:, 2352:2352 + 256]
        posx = v3(reg_s[:, 2608:2608 + 2 * (NE + EXTRA)], NE + EXTRA)
        gatx = v3(reg_s[:, 2688:2688 + 2 * (NE + EXTRA)], NE + EXTRA)
        pos, gat = posx[:, :, 0:NE], gatx[:, :, 0:NE]
        x_n = reg_s[:, 2768:2768 + NE]
        x_c = reg_s[:, 2800:2800 + NE]
        x_e = reg_s[:, 2832:2832 + NE]
        x_id = reg_s[:, 2864:2864 + EXTRA]
        n_extra = reg_s[:, 2872:2873].bitcast(I32)
        ids = reg_s[:, 2880:2880 + EXTRA].bitcast(I32)
        x_in_e = v3(reg_s[:, 2900:2900 + EXTRA * NE], NE)
        x_t = reg_s[:, 3156:3156 + 2 * EXTRA * NE].rearrange("p (b x e) -> p b x e", b=2, e=NE)
        r_ = lambda o, w: v3(rtmp[:, o:o + 2 * w], w)
        r_gm, r_m1, r_m2, r_mx, r_gs, r_dn, r_w1, r_w2 = (r_(2 * i, 1) for i in range(8))
        r_tp, r_el, r_e1, r_e2, r_s8, r_g8, r_t8 = (r_(16 + 16 * i, EPG) for i in range(7))
        r_goh, r_xg, r_ex, r_desc = r_(128, NG), r_(136, 5), r_(146, 5), rtmp[:, 156:164]
        r_big = rtmp[:, 164:228].rearrange("p (b k e) -> p b k e", b=2, e=EPG)
        xeT = v3(reg_t[:, 0:2048], P)
        a1 = reg_t[:, 2048:2560]
        a3 = reg_t[:, 2560:3072]
        hs = reg_t[:, 3072:3328]
        hT = v3(reg_t[:, 3328:3584], SLOT)
        gT = reg_t[:, 3584:3840]
        selS = reg_t[:, 3840:3968].bitcast(BF).rearrange("p (b q s) -> p b q s", b=2, q=QE)
        selW = reg_s[:, 3840:4096].rearrange("p (b q s) -> p b q s", b=2, q=QE)
        hn = v3(reg_d[:, 0:4096], D)
        hr1 = v3(reg_d[:, 4096:8192], D)

        def piece(t, u):
            return t[:, u % 2, D // 2 * (u // 2):D // 2 * (u // 2) + D // 2]

        ye = reg_d[:, 4096:6144]
        fg = reg_d[:, 0:2048]
        junk = (reg_d[:, 2048:4096], reg_d[:, 6144:8192])
        fin = dfc[:, 0, 0:8]

        w_in_u = w_in.rearrange("l (c p) n -> p (l c) n", p=P)
        w_out_u = w_out.rearrange("l (c p) n -> p (l c) n", p=P)
        x_v = x.rearrange("o (b p) d -> p (o b) d", p=P)
        out_v = out.rearrange("o (b p) d -> p (o b) d", p=P)
        w1_v = e_w1.rearrange("l e (h c p) n -> p (l e) h c n", h=2, p=P)
        w3_v = e_w3.rearrange("l e (h c p) n -> p (l e) h c n", h=2, p=P)
        w2_v = e_w2.rearrange("l e (h c p) n -> p (l e) h c n", h=2, p=P)

        @block.sync
        def _(sp):
            for b in range(TB):
                sp.dma_start(xt[:, b, :], x_v[:, b, :]).then_inc(x_in[b], 16)
            sp.dma_start(spar[:, 0, :], lam_re.rearrange("l (j h) n -> (l j) (h n)", h=2)).then_inc(lam_in, 16)
            sp.dma_start(spar[:, 1, :], lam_im.rearrange("l (j h) n -> (l j) (h n)", h=2)).then_inc(lam_in, 16)
            sp.dma_start(dt2[:, :], log_dt.rearrange("l (j h) -> (l j) h", h=2)).then_inc(lam_in, 16)
            sp.dma_start(prow[:, 0, :], norm_mix_g.rearrange("l (c p) -> (l c) p", p=P)).then_inc(par_in, 16)
            sp.dma_start(prow[:, 1, :], norm_ffn_g.rearrange("l (c p) -> (l c) p", p=P)).then_inc(par_in, 16)
            for i, r in enumerate((sb_norm_g, ssm_norm_g, b_glu)):
                sp.dma_start(prow[4 * i:4 * i + 4, 2, :], r.rearrange("l (c p) -> (l c) p", p=P)).then_inc(par_in, 16)
            sp.dma_start(prow[12:16, 2, :], ssm_d.rearrange("l (q g) c -> (l q) (g c)", q=4)).then_inc(par_in, 16)
            sp.dma_start(prow[0:1, 3, :], subln_g).then_inc(par_in, 16)

            def later_parameters():
                for k, (cn, c) in enumerate(((cnat, c_re), (cnat2, c_im))):
                    cv = c.rearrange("l (q g) c n -> (l g c) q n", q=4)
                    for d in range(2):
                        sp.dma_start(cn[:, :, d, :], cv).then_inc(c_in, 16)
                for i, r in enumerate((lq1, lk1, lq2, lk2)):
                    sp.dma_start(lamv[:, i, :], r.broadcast_to([P, 64])).then_inc(lq_in, 16)
                for k in range(NG):
                    sp.dma_start(rw[:, :, NG + EPG * k:NG + EPG * (k + 1)],
                                 re_w[:, k].rearrange("l (c p) e -> p (l c) e", p=P)).then_inc(rw_in, 16)
                sp.dma_start(rw[:, :, 0:NG], rg_w.rearrange("l (c p) e -> p (l c) e", p=P)).then_inc(rw_in, 16)
                sp.dma_start(rbias[:, 0:NG], rg_b.broadcast_to([P, NG])).then_inc(rw_in, 16)
                sp.dma_start(rbias[:, NG:], re_b.rearrange("l g e -> l (g e)").broadcast_to([P, NE])).then_inc(rw_in, 16)

            for n in range(UNITS_A):
                s = n % SLOTS_A
                if n < 2 * NB:
                    c0 = BLOCKS[n // 2][2]
                    src = w_in_u[:, 8 * (n % 2):8 * (n % 2) + 8, c0:c0 + 512]
                else:
                    ob_, half = OUT_UNITS[n - 2 * NB]
                    src = w_out_u[:, 8 * half:8 * half + 8, 512 * ob_:512 * ob_ + 512]
                if n >= SLOTS_A:
                    sp.wait_ge(unit_used, n - SLOTS_A + 1)
                sp.dma_start(unit(s), src).then_inc(ring_in[s], 16)
                if n == 1:
                    later_parameters()
                if n == 12:
                    sp.wait_ge(bu_done, ST)
                    for b in range(TB):
                        sp.dma_start(xt[:, b, :], x_v[:, b, :]).then_inc(x2_in, 16)

            def item(n_, e):
                for k in range(6):
                    s = slot_of(k)
                    sp.wait_ge(slot_free, n_ * 6 + k + 1)
                    w = (w1_v, w3_v, w2_v)[k // 2]
                    src = w[:, ds(e, 1), k % 2, :, :]
                    sp.dma_start(unit(s) if k < 4 else unit2(s), src.rearrange("p e c n -> p (e c) n")).then_inc(ring_in[s], 16)

            with sp.Fori(0, NE) as e:
                item(e, e)
            sp.wait_ge(rk_ready, 2)
            extra = sp.value_load(n_extra[0:1, 0:1], min_val=0, max_val=EXTRA - 1)
            with sp.If(extra > 0):
                with sp.Fori(0, extra) as x_:
                    item(x_ + NE, sp.value_load(ids[0:1, ds(x_, 1)], min_val=0, max_val=NE - 1))
            for k in range(2 * TB):
                sp.wait_ge(f_out, k + 1)
                w = slice(D // 2 * (k % 2), D // 2 * (k % 2) + D // 2)
                sp.dma_start(out_v[:, k // 2, w], xt[:, k // 2, w]).then_inc(f_st, 16)
            sp.wait_ge(f_st, 16 * 2 * TB)

        @block.gpsimd
        def _(g):
            n = [0]

            def link(ins):
                n[0] += 1
                ins.then_inc(gchain, 1)
                g.wait_ge(gchain, n[0])

            G = nc.gpsimd
            link(G.memset(ident[:], 0.0))
            pick_ident = G.affine_select(out=ident[:, :], in_=ident[:, :], compare_op=ALU.not_equal, fill=1.0, base=0,
                                         pattern=[[-1, P]], channel_multiplier=1)
            pick_ident.then_inc(cst, 1)
            for t, val in ((ones, 1.0), (tri_neg, -1.0), (ones_neg, -1.0), (ident_b, 0.0), (ones_b, 1.0),
                           (before_b, 1.0), (mask_b, 0.0), (smask_b, 0.0), (stack2, 0.0), (rowm, 1.0), (cmask, 1.0)):
                last = G.memset(t[:], val)
            link(last)

            def pick(t, pattern, base, cm, op, fill):
                return G.affine_select(out=t, in_=t, compare_op=op, fill=fill, base=base, pattern=pattern,
                                       channel_multiplier=cm)

            pick(ident_b[:, :], [[-1, P]], 0, 1, ALU.not_equal, 1.0)
            pick(tri_neg[:, :], [[-1, P]], 0, 1, ALU.is_ge, 0.0)
            pick(before_b[:, :], [[1, P]], 0, -1, ALU.is_gt, 0.0)
            pick(mask_b[:, :, :], [[0, 2], [-1, P]], 0, 1, ALU.is_ge, NEG)
            pick(smask_b[:, :], [[1, P]], 0, -1, ALU.is_gt, NEG)
            for k in range(QE):
                link(pick(stack2[:, :], [[-1, SLOT]], -SLOT * k, 1, ALU.not_equal, 1.0))
            pick(rowm[:, :], [[-32, 4]], 0, 1, ALU.is_ge, 0.0)
            link(pick(cmask[:, :], [[-64, 2]], 0, 1, ALU.is_ge, 0.0))
            pick(rowm[:, :], [[32, 4]], 31, -1, ALU.is_ge, 0.0)
            pick(cmask[:, :], [[64, 2]], 63, -1, ALU.is_ge, 0.0)
            link(G.iota(iota_i, [[1, SLOT]], base=0, channel_multiplier=0))
            G.tensor_copy(iota_s[:, :], iota_i).then_inc(cst, 1)
            G.memset(bnat[:, :, :, :], 0.0).then_inc(b_zero, 1)
            g.wait_ge(b_zero, 1)
            for k, b in enumerate((b_re, b_im)):
                bv = b.rearrange("l (j h) n c -> (l h) n j c", h=2)
                for h in range(2):
                    g.dma_start(bnat[64 * h:64 * h + 64, k, :, 16 * h:16 * h + 16], bv[h]).then_inc(b_in, 16)
            G.memset(ph[:, 0, :, 0:1], 1.0)
            G.memset(ph[:, 1, :, 0:1], 0.0).then_inc(k_zero, 1)

            def rot_in(j):
                g.wait_ge(s_prod, j + 1)
                if j >= 2:
                    g.wait_ge(s_scan, j - 1)
                ab, v = s_ab[j % 2], s_v[j % 2]
                G.tensor_tensor(v[:, 0, :], ab[:, 0, 0, :], ab[:, 1, 1, :], ALU.subtract)
                G.tensor_tensor(v[:, 1, :], ab[:, 0, 1, :], ab[:, 1, 0, :], ALU.add).then_inc(s_rot, 1)

            def rot_out(j):
                g.wait_ge(s_out, j + 1)
                if j >= 2:
                    g.wait_ge(sy_used, j - 1)
                df, s = s_df[j % 2], s_s[j % 2]
                G.tensor_tensor(s[:, 0, :], df[:, 0, 0, :], df[:, 1, 1, :], ALU.add).then_inc(s_state, 1)

            g.wait_ge(k_zero, 1)
            g.wait_ge(cT_done, 2)
            link(G.memset(sk[64:128, 0:8:2, :], 0.0))
            G.memset(sk[0:64, 1:8:2, :], 0.0).then_inc(dk_zero, 1)
            g.wait_ge(dk_zero, 1)
            for j in range(ST + 1):
                if j < ST:
                    rot_in(j)
                if j >= 1:
                    rot_out(j - 1)
            g.wait_ge(sy_used, ST)
            g.wait_ge(s_state, ST)
            link(G.memset(dk[64:128, :, 0, :], 0.0))
            G.memset(dk[0:64, :, 1, :], 0.0).then_inc(dk_zero, 1)

            def h_rest(u):
                g.wait_ge(h_hi, u + 1)
                G.tensor_tensor(piece(hr1, u), piece(hn, u), piece(hi, u), ALU.subtract).then_inc(h_r1, 1)

            def h_low(u):
                g.wait_ge(h_mid, u + 1)
                G.tensor_tensor(piece(lo, u), piece(hr1, u), piece(mid, u), ALU.subtract).then_inc(h_lo, 1)

            for u in range(3):
                h_rest(u)
            h_low(1)
            h_low(3)

        @block.scalar
        def _(a):
            A = nc.scalar
            cp = ACT.Copy
            half = D // 2
            a.wait_ge(x_in[0], 16)
            A.activation(xn[:, 0, :], xt[:, 0, :], ACT.Square, accum_out=rmsc[:, 0:1]).then_inc(xsum, 1)
            a.wait_ge(x_in[1], 16)
            A.activation(xn[:, 1, 0:half], xt[:, 1, 0:half], ACT.Square, accum_out=rmsc[:, 14:15]).then_inc(xsum, 1)
            a.wait_ge(rstd_s, 1)
            A.activation(rmsc[:, 4:6], rmsc[:, 2:4], ACT.Sqrt).then_inc(achain, 1)
            a.wait_ge(rstd_s, 2)
            for i in range(2):
                w = slice(half * i, half * i + half)
                A.activation(xn[:, 0, w], xt[:, 0, w], cp, scale=rmsc[:, 6:7]).then_inc(xnorm, 1)
            a.wait_ge(pT_evac, 1)
            for n_ in range(0, DC // 2, 2):
                a.wait_ge(tr_done, n_ + 1)
                for k in range(2):
                    c = 2 * n_ + k
                    last = A.activation(xnT[:, c, :], pj[n_ % 4][:, k * T:(k + 1) * T], cp, scale=g_mix[:, c:c + 1])
                last.then_inc(tr_evac, 1)

            def evac(n_):
                kind, i, _c = BLOCKS[n_]
                a.wait_ge(unit_used, 2 * n_ + 2)
                for k in range(2):
                    src = pj[2 * (n_ % 2) + k]
                    if kind == "u":
                        last = A.activation(uT[:, 2 * k:2 * k + 2, :], v3(src[:, :], T), cp)
                    elif kind in ("sbq", "dfq"):
                        q = sq if kind == "sbq" else dq
                        last = A.activation(q[:, 4 * i + 2 * k:4 * i + 2 * k + 2, :], v3(src[:, :], T), cp, scale=QSCALE)
                    elif kind == "sbk":
                        for h in range(2):
                            rows = slice(64 * h, 64 * h + 64)
                            last = A.activation(sk[rows, 4 * k + h:4 * k + h + 3:2, :], v3(src[rows, :], T), cp)
                    elif kind == "dfk":
                        for h in range(2):
                            rows = slice(64 * h, 64 * h + 64)
                            last = A.activation(dk[rows, 4 * i + 2 * k:4 * i + 2 * k + 2, h, :], v3(src[rows, :], T), cp)
                    elif kind == "sbv":
                        last = A.activation(sv[:, k, :], src[:, :], cp)
                    else:
                        last = A.activation(dv[:, k, 512 * i:512 * i + 512], src[:, :], cp)
                last.then_inc(pj_evac, 1)

            evac(0)
            for n_ in range(8):
                k, q = n_ // 4, n_ % 4
                a.wait_ge(bT_done, n_ + 1)
                a.wait_ge(xnorm, 2)
                a.wait_ge(xnorm_v, 2)
                for i in range(4):
                    last = A.activation(bpad[:, k, 4 * q + i, :], at[2 + n_ % 2][:, 0:P], cp, scale=rowm[:, i:i + 1])
                last.then_inc(bT_evac, 1)
            a.wait_ge(dk_zero, 1)
            for n_ in (1, 2, 3):
                evac(n_)
            a.wait_ge(s_state, ST)
            a.dma_start(glu_w[:, :, :], w_glu.rearrange("l (c p) n -> p (l c) n", p=P)).then_inc(glu_in, 16)
            for q in range(4):
                a.wait_ge(sy_evac, q + 1)
                A.activation(uT[:, q, :], uT[:, q, :], ACT.Gelu_apprx_tanh).then_inc(gelu_s, 1)
            evac(4)
            for q in range(4):
                a.wait_ge(glu_done, 2 * (q // 2) + 2)
                A.activation(glu_s[:, q, :], at[q // 2][:, (q % 2) * T:(q % 2) * T + T], ACT.Sigmoid,
                             bias=b_gl[:, q:q + 1]).then_inc(glu_sig, 1)

            a.wait_ge(glu_y, 1)
            A.activation(nrm_sq[:, :, :], yT[:, 4:8, :], ACT.Square).then_inc(nsq, 1)
            a.wait_ge(nsum, 1)
            A.activation(rstd_t, at[2][:, 0:T], ACT.Sqrt, scale=1.0 / SSW, bias=lam_s[:, 6:7]).then_inc(nrt, 1)
            for hp in range(SBH // 2):
                a.wait_ge(z_done, hp + 1)
                for k in range(2):
                    A.activation(sp_a[:, k, :], at[k][:, 0:384], ACT.Abs).then_inc(z_abs, 1)
                a.wait_ge(z_abs, 6 * hp + 2)
                if hp == 0:
                    a.wait_ge(nrt, 1)
                A.activation(sp_e[:, :, :], sp_a[:, :, :], ACT.Exp, scale=-1.0).then_inc(z_abs, 2)
                a.wait_ge(z_abs, 6 * hp + 4)
                A.activation(sp_a[:, :, :], sp_e[:, :, :], ACT.Ln, bias=1.0).then_inc(z_abs, 2)
                a.wait_ge(z_cum, hp + 1)
                if hp:
                    a.wait_ge(sbo_done, hp)
                for k in range(2):
                    last = A.activation(sb_w[:, k, :], at[k][:, 0:384], ACT.Exp)
                last.then_inc(z_w, 1)
                a.wait_ge(sbo_done, hp + 1)
                A.activation(yT[:, hp, :], at[2][:, 0:T], cp).then_inc(sbo_evac, 1)
                if hp == 1:
                    a.wait_ge(dk_zero, 2)
                    evac(5)
            evac(6)
            a.wait_ge(ny, 1)
            a.wait_ge(sbo_evac, SBH // 2)
            A.activation(nrm_sq[:, :, :], yT[:, 0:4, :], ACT.Square).then_inc(nsq, 1)
            a.wait_ge(nsum, 2)
            A.activation(rstd_t, at[3][:, 0:T], ACT.Sqrt, scale=1.0 / SBW, bias=lam_s[:, 6:7]).then_inc(nrt, 1)
            a.wait_ge(lam_sum, 1)
            A.activation(lam_s[:, 2:4], lam_s[:, 0:2], ACT.Exp).then_inc(lam_exp, 1)

            def df_exp(h):
                a.wait_ge(d_max, h + 1)
                nm, su = dfc[:, h % 2, 0:4], dfc[:, h % 2, 4:8]
                if h:
                    a.wait_ge(d_a, h)
                for r in range(2):
                    A.activation(df_p0[:, r * P:(r + 1) * P], at[0][:, r * P:(r + 1) * P], ACT.Exp,
                                 bias=nm[:, r:r + 1], accum_out=su[:, r:r + 1])
                for r in range(2):
                    last = A.activation(df_p1[:, r * T:(r + 1) * T], at[1][:, r * T:(r + 1) * T], ACT.Exp,
                                        bias=nm[:, 2 + r:3 + r], accum_out=su[:, 2 + r:3 + r])
                last.then_inc(d_exp, 1)

            def df_copy(h):
                a.wait_ge(d_pv, h + 1)
                A.activation(yT[:, 8 + h, :], at[3][:, (h % 2) * T:(h % 2) * T + T], cp).then_inc(d_y, 1)

            def df_squares(k):
                a.wait_ge(d_y, 4 * k + 4)
                A.activation(v3(df_sq, T), yT[:, 8 + 4 * k:12 + 4 * k, :], ACT.Square).then_inc(nsq, 1)

            def df_roots(k):
                a.wait_ge(nsum, 3 + k)
                a.wait_ge(ny, 2 + k)
                for i in range(2):
                    last = A.activation(df_rt[:, 512 * i:512 * i + 512], at[i][:, :], ACT.Sqrt, scale=1.0 / P, bias=lam_s[:, 6:7])
                last.then_inc(nrt, 1)

            for h in range(DFH):
                df_exp(h)
                df_copy(h)
                if h == 1:
                    evac(7)
                if h == 3:
                    df_squares(0)
                    evac(8)
                    df_roots(0)
                    evac(9)
            df_squares(1)
            df_roots(1)
            def h_squares(k):
                a.wait_ge(h_add, TB * (k + 1))
                w = slice(512 * k, 512 * k + 512)
                for b in range(TB):
                    last = A.activation(hr1[:, b, w], xt[:, b, w], ACT.Square, accum_out=fin[:, 4 * b + k:4 * b + k + 1])
                last.then_inc(h_sq, 1)

            def h_evac(n_):
                a.wait_ge(tr_done, DC // 2 + n_ + 1)
                for k in range(2):
                    c = 2 * n_ + k
                    last = A.activation(xnT[:, c, :], at[2 + n_ % 2][:, k * T:(k + 1) * T], cp, scale=g_ffn[:, c:c + 1])
                last.then_inc(tr_evac, 1)

            for k in range(4):
                h_squares(k)
                h_evac(2 * k)
                if k < 3:
                    h_evac(2 * k + 1)
            a.wait_ge(h_rs, 1)
            A.activation(rmsc[:, 4:6], rmsc[:, 2:4], ACT.Sqrt).then_inc(achain, 1)
            a.wait_ge(h_rs, 2)
            def h_high(u):
                A.activation(piece(hn, u), piece(xt, u), cp, scale=rmsc[:, 10 + u % 2:11 + u % 2]).then_inc(hn_s, 1)
                a.wait_ge(hn_s, u + 1)
                A.activation(piece(hi, u), piece(hn, u), cp).then_inc(h_hi, 1)

            def h_middle(u):
                if u < 3:
                    a.wait_ge(h_r1, u + 1)
                else:
                    a.wait_ge(h_r1_v, 1)
                A.activation(piece(mid, u), piece(hr1, u), cp).then_inc(h_mid, 1)

            for u in range(3):
                h_high(u)
            h_middle(0)
            h_high(3)
            for u in range(1, 4):
                h_middle(u)
            a.wait_ge(rt_m, 1)
            A.activation(r_ex, r_xg, ACT.Exp).then_inc(rt_e, 1)
            a.dma_start(fg, final_g.unsqueeze(0).broadcast_to([P, D])).then_inc(fg_in, 16)

            def a_items(i_, n0, nq):
                for q in range(nq):
                    n_ = n0 + q
                    a.wait_ge(slot_free, used(n_, 2))
                    a.wait_ge(e_hT, n_ + 1)
                    A.activation(a1, psb[0][:, :], cp).then_inc(e_a1, 1)
                    a.wait_ge(e_hT, n_ + 2)
                    a.wait_ge(e_h, n_ + 1)
                    A.activation(hs, psb[2][:, 0:256], ACT.Silu).then_inc(e_silu, 1)
                    a.wait_ge(slot_free, used(n_, 6))
                    a.wait_ge(e_comb, i_ * 8 + 1)
                    for b in range(2):
                        last = A.activation(ye[64 * q:64 * q + 64, 512 * b:512 * b + 512], psb[3][64 * b:64 * b + 64, :], cp)
                    last.then_inc(e_yev, 1)

            with a.Fori(0, ITERS) as it:
                a_items(it, it * QE, QE)
            a.wait_ge(rk_ready, 2)
            extra = a.value_load(n_extra[0:1, 0:1], min_val=0, max_val=EXTRA - 1)
            with a.If(extra > 0):
                with a.Fori(0, extra) as x_:
                    a_items(x_ + ITERS, x_ + NE, 1)
            for b in range(TB):
                for c in range(4):
                    a.wait_ge(e_acc, (extra + (ITERS - 1)) * 8 + 4 * b + c + 1)
                    w = slice(512 * c, 512 * c + 512)
                    last = A.activation(junk[b][:, w], xt[:, b, w], ACT.Square, accum_out=fin[:, 4 * b + c:4 * b + c + 1])
                last.then_inc(f_sq, 1)
                a.wait_ge(f_rs, 2 * b + 1)
                A.activation(rmsc[:, 4 + b:5 + b], rmsc[:, 2 + b:3 + b], ACT.Sqrt).then_inc(f_sq, 1)

        @block.vector
        def _(v):
            V = nc.vector
            n = [0]

            def link(ins):
                n[0] += 1
                ins.then_inc(vchain, 1)
                v.wait_ge(vchain, n[0])

            MAGIC = 1.5 * 2.0 ** 23

            def exp_rows(dst, src, k, f, t, kint):
                link(V.tensor_scalar(dst, src, -87.0, 88.0, ALU.max, ALU.min))
                src = dst
                link(V.tensor_scalar(t, src, 1.0 / math.log(2.0), MAGIC, ALU.mult, ALU.add))
                link(V.tensor_scalar(k, t, MAGIC, -126.0, ALU.subtract, ALU.max))
                link(V.tensor_scalar(k, k, 127.0, None, ALU.min))
                link(V.scalar_tensor_tensor(f, k, -0.693359375, src, ALU.mult, ALU.add))
                link(V.scalar_tensor_tensor(f, k, 2.12194440054690583e-4, f, ALU.mult, ALU.add))
                link(V.tensor_scalar(t, f, 1.0 / 5040, None, ALU.mult))
                for c in (1.0 / 720, 1.0 / 120, 1.0 / 24, 1.0 / 6, 0.5, 1.0):
                    link(V.scalar_tensor_tensor(t, t, c, f, ALU.add, ALU.mult))
                link(V.tensor_scalar(kint, k, 127.0, 2.0 ** 23, ALU.add, ALU.mult))
                link(V.scalar_tensor_tensor(dst, t, 1.0, kint.bitcast(F), ALU.add, ALU.mult))

            V.memset(lam_s[:, 6:7], EPS)
            v.wait_ge(x_in[1], 16)
            half = D // 2
            V.scalar_tensor_tensor(xn[:, 1, half:], xt[:, 1, half:], 1.0, xt[:, 1, half:], ALU.mult, ALU.mult,
                                   accum_out=rmsc[:, 15:16]).then_inc(xsum, 1)
            v.wait_ge(xsum, 3)
            link(V.tensor_tensor(rmsc[:, 1:2], rmsc[:, 14:15], rmsc[:, 15:16], ALU.add))
            V.tensor_scalar(rmsc[:, 2:4], rmsc[:, 0:2], 1.0 / D, EPS, ALU.mult, ALU.add).then_inc(rstd_s, 1)
            v.wait_ge(achain, 1)
            V.reciprocal(rmsc[:, 6:8], rmsc[:, 4:6]).then_inc(rstd_s, 1)
            v.wait_ge(rstd_s, 2)
            for i in range(2):
                w = slice(half * i, half * i + half)
                V.tensor_scalar(xn[:, 1, w], xt[:, 1, w], rmsc[:, 7:8], None, ALU.mult).then_inc(xnorm_v, 1)
            v.wait_ge(pT_done, 1)
            V.tensor_copy(pcol[:, 0:49], at[0][:, 0:49]).then_inc(pT_evac, 1)
            v.wait_ge(pT_evac, 1)
            for n_ in range(1, DC // 2, 2):
                v.wait_ge(tr_done, n_ + 1)
                for k in range(2):
                    c = 2 * n_ + k
                    last = V.tensor_scalar(xnT[:, c, :], pj[n_ % 4][:, k * T:(k + 1) * T], g_mix[:, c:c + 1], None, ALU.mult)
                last.then_inc(tr_evac_v, 1)
                if n_ == 1:
                    v.wait_ge(lam_in, 16 * 3)
                    V.tensor_copy(spar[:, 2, :].rearrange("p (h n) -> p h n", h=2),
                                  dt2[:, :].unsqueeze(2).broadcast_to([ST, 2, 64])).then_inc(sp_done, 1)
            v.wait_ge(sT_done, 1)
            V.tensor_copy(sw[:, 0:3, :], at[1][:, 0:3 * ST].rearrange("p (k j) -> p k j", j=ST)).then_inc(sp_read, 1)
            v.wait_ge(sp_read, 1)
            R = lambda i: sw[:, i, :]
            exp_rows(R(16), R(2), R(5), R(6), R(7), ki[:, :])
            link(V.tensor_tensor(R(2), R(0), R(16), ALU.mult))
            link(V.tensor_tensor(R(3), R(1), R(16), ALU.mult))
            exp_rows(R(4), R(2), R(5), R(6), R(7), ki[:, :])
            link(V.tensor_scalar(R(5), R(3), 1.0 / (2 * math.pi), MAGIC, ALU.mult, ALU.add))
            link(V.tensor_scalar(R(5), R(5), MAGIC, None, ALU.subtract))
            c1 = 6.28125
            c2 = 1.935307179586e-3 - (1.935307179586e-3 % 2.0 ** -20)
            c3 = 2 * math.pi - c1 - c2
            link(V.scalar_tensor_tensor(R(6), R(5), -c1, R(3), ALU.mult, ALU.add))
            link(V.scalar_tensor_tensor(R(6), R(5), -c2, R(6), ALU.mult, ALU.add))
            link(V.scalar_tensor_tensor(R(6), R(5), -c3, R(6), ALU.mult, ALU.add))
            link(V.tensor_scalar(R(6), R(6), 0.5, None, ALU.mult))
            link(V.tensor_tensor(R(7), R(6), R(6), ALU.mult))
            V.tensor_scalar(R(8), R(7), 1.0 / math.factorial(13), None, ALU.mult)
            link(V.tensor_scalar(R(9), R(7), -1.0 / math.factorial(14), None, ALU.mult))
            for k in (11, 9, 7, 5, 3):
                V.scalar_tensor_tensor(R(8), R(8), (-1) ** ((k - 1) // 2) / math.factorial(k), R(7), ALU.add, ALU.mult)
                link(V.scalar_tensor_tensor(R(9), R(9), (-1) ** ((k + 1) // 2) / math.factorial(k + 1), R(7), ALU.add, ALU.mult))
            V.scalar_tensor_tensor(R(8), R(8), 1.0, R(6), ALU.add, ALU.mult)
            link(V.scalar_tensor_tensor(R(9), R(9), -0.5, R(7), ALU.add, ALU.mult))
            link(V.tensor_scalar(R(9), R(9), 1.0, None, ALU.add))
            link(V.tensor_tensor(R(10), R(8), R(8), ALU.mult))
            V.tensor_scalar(R(20), R(10), -2.0, 1.0, ALU.mult, ALU.add)
            link(V.scalar_tensor_tensor(R(21), R(8), -2.0, R(9), ALU.mult, ALU.mult))
            V.tensor_tensor(R(12), R(0), R(0), ALU.mult)
            V.tensor_tensor(R(13), R(1), R(1), ALU.mult)
            V.tensor_copy(R(19), R(4))
            V.scalar_tensor_tensor(R(11), R(4), -1.0, R(21), ALU.mult, ALU.mult)
            link(V.tensor_tensor(R(10), R(4), R(20), ALU.mult))
            V.tensor_tensor(R(12), R(12), R(13), ALU.add)
            link(V.tensor_scalar(R(10), R(10), 1.0, None, ALU.subtract))
            V.reciprocal(R(13), R(12))
            V.tensor_tensor(R(14), R(10), R(0), ALU.mult)
            V.tensor_tensor(R(15), R(11), R(1), ALU.mult)
            V.tensor_tensor(R(16), R(11), R(0), ALU.mult)
            link(V.tensor_tensor(R(17), R(10), R(1), ALU.mult))
            V.tensor_tensor(R(14), R(14), R(15), ALU.add)
            link(V.tensor_tensor(R(16), R(16), R(17), ALU.subtract))
            V.tensor_tensor(R(22), R(14), R(13), ALU.mult)
            link(V.tensor_tensor(R(23), R(16), R(13), ALU.mult))
            v.wait_ge(cT_done, 2)
            fre = scol[:, 3, :].unsqueeze(2).broadcast_to([P, ST, 32])
            fim = scol[:, 4, :].unsqueeze(2).broadcast_to([P, ST, 32])
            cr = at[0][:, :].rearrange("p (j c) -> p j c", c=32)
            ci = at[1][:, :].rearrange("p (j c) -> p j c", c=32)
            tc1 = reg_d[:, 0:512].rearrange("p (j c) -> p j c", c=32)
            tc2 = reg_d[:, 512:1024].rearrange("p (j c) -> p j c", c=32)
            for o, (f0, f1, op, sg) in enumerate(((fre, fim, ALU.subtract, 1.0), (fim, fre, ALU.add, -1.0))):
                link(V.tensor_tensor(tc1, cr, f0, ALU.mult))
                link(V.tensor_tensor(tc2, ci, f1, ALU.mult))
                link(V.tensor_tensor(tc1, tc1, tc2, op))
                for h in range(2):
                    last = V.tensor_scalar(crT[:, o, :, 16 * h:16 * h + 16], tc1[:, :, 16 * h:16 * h + 16],
                                           cmask[:, h:h + 1], sg, ALU.mult, ALU.mult)
                last.then_inc(c_ready, 1)
                v.wait_ge(c_ready, o + 1)
            v.wait_ge(k_zero, 1)
            link(V.tensor_copy(pw[:, 0:2, :], scol[:, 1:3, :]))
            w_ = 1
            while w_ < T:
                pr = pw[:, 0, :].unsqueeze(2).broadcast_to([P, ST, w_])
                pi = pw[:, 1, :].unsqueeze(2).broadcast_to([P, ST, w_])
                er, ei = ph[:, 0, :, 0:w_], ph[:, 1, :, 0:w_]
                t1 = reg_d[:, 0:2048].rearrange("p (j t) -> p j t", j=ST)[:, :, 0:w_]
                t2 = reg_d[:, 2048:4096].rearrange("p (j t) -> p j t", j=ST)[:, :, 0:w_]
                V.tensor_tensor(t1, er, pr, ALU.mult)
                link(V.tensor_tensor(t2, ei, pi, ALU.mult))
                link(V.tensor_tensor(ph[:, 0, :, w_:2 * w_], t1, t2, ALU.subtract))
                V.tensor_tensor(t1, er, pi, ALU.mult)
                link(V.tensor_tensor(t2, ei, pr, ALU.mult))
                link(V.tensor_tensor(ph[:, 1, :, w_:2 * w_], t1, t2, ALU.add))
                w_ *= 2
                if w_ < T:
                    V.tensor_tensor(pw[:, 2, :], pw[:, 0, :], pw[:, 0, :], ALU.mult)
                    link(V.tensor_tensor(pw[:, 3, :], pw[:, 1, :], pw[:, 1, :], ALU.mult))
                    link(V.scalar_tensor_tensor(pw[:, 1, :], pw[:, 0, :], 2.0, pw[:, 1, :], ALU.mult, ALU.mult))
                    link(V.tensor_tensor(pw[:, 0, :], pw[:, 2, :], pw[:, 3, :], ALU.subtract))

            def ph_b(k, j):
                return ph[:, k, j, :].unsqueeze(1).broadcast_to([P, 2, T])

            def s_products(j):
                v.wait_ge(bu_done, j + 1)
                if j >= 2:
                    v.wait_ge(s_rot, j - 1)
                bu = v3(at[j % 2][:, :], T)
                V.tensor_tensor(s_ab[j % 2][:, 0, :, :], bu, ph_b(0, j), ALU.mult)
                V.tensor_tensor(s_ab[j % 2][:, 1, :, :], bu, ph_b(1, j), ALU.mult).then_inc(s_prod, 1)

            def s_scans(j):
                v.wait_ge(s_rot, j + 1)
                rr = scol[:, 0, j:j + 1].broadcast_to([P, T])
                if j:
                    v.wait_ge(s_out, j)
                for k in range(2):
                    last = V.tensor_tensor_scan(s_w[:, k, :], rr, s_v[j % 2][:, k, :], 0.0, ALU.mult, ALU.add)
                last.then_inc(s_scan, 1)
                v.wait_ge(s_scan, j + 1)
                if j >= 2:
                    v.wait_ge(s_state, j - 1)
                V.tensor_tensor(s_df[j % 2][:, 0, :, :], s_w[:, :, :], ph_b(0, j), ALU.mult)
                V.tensor_tensor(s_df[j % 2][:, 1, :, :], s_w[:, :, :], ph_b(1, j), ALU.mult).then_inc(s_out, 1)
                v.wait_ge(s_out, j + 1)
                if j >= 2:
                    v.wait_ge(sy_used, j - 1)
                df = s_df[j % 2]
                V.tensor_tensor(s_s[j % 2][:, 1, :], df[:, 0, 1, :], df[:, 1, 0, :], ALU.subtract).then_inc(s_im, 1)

            def s_skip(q):
                v.wait_ge(sy_used, 4 * q + 4)
                V.scalar_tensor_tensor(uT[:, q, :], uT[:, q, :], d_sk[:, q:q + 1], at[2 + q % 2][:, 0:T],
                                       ALU.mult, ALU.add).then_inc(sy_evac, 1)

            for j in range(ST + 1):
                if j < ST:
                    s_products(j)
                if j >= 1:
                    s_scans(j - 1)
                if j >= 8 and j % 4 == 0:
                    s_skip(j // 4 - 2)
            s_skip(3)
            for q in range(4):
                v.wait_ge(glu_sig, q + 1)
            last = V.tensor_tensor(uT[:, :, :], uT[:, :, :], glu_s[:, :, :], ALU.mult)
            last.then_inc(glu_y, 1)

            def norm_four(n_, first, gain):
                v.wait_ge(nrt, n_)
                link(V.reciprocal(rstd_t, rstd_t))
                for q in range(4):
                    last = V.scalar_tensor_tensor(yT[:, first + q, :], yT[:, first + q, :], gain[:, q:q + 1], rstd_t,
                                                  ALU.mult, ALU.mult)
                last.then_inc(ny, 1)
            norm_four(1, 4, g_ssm)
            v.wait_ge(lq_in, 16 * 4)
            for i in range(2):
                link(V.tensor_tensor(lamv[:, 2 * i, :], lamv[:, 2 * i, :], lamv[:, 2 * i + 1, :], ALU.mult))
                last = V.reduce_sum(lam_s[:, i:i + 1], lamv[:, 2 * i, :], axis=AX)
            last.then_inc(lam_sum, 1)
            for hp in range(SBH // 2):
                v.wait_ge(z_abs, 6 * hp + 6)
                if hp:
                    v.wait_ge(z_cum, hp)
                for k in range(2):
                    last = V.scalar_tensor_tensor(sp_t[:, k, :], at[k][:, 0:384], 0.0, sp_a[:, k, :], ALU.max, ALU.add)
                last.then_inc(z_sp, 1)
            norm_four(2, 0, g_sb)
            v.wait_ge(lam_exp, 1)
            link(V.tensor_tensor(lam_s[:, 4:5], lam_s[:, 2:3], lam_s[:, 3:4], ALU.subtract))
            link(V.tensor_scalar(lam_s[:, 5:6], lam_s[:, 4:5], LAM_INIT, None, ALU.add))
            link(V.tensor_scalar(g_df, g_df, 1.0 - LAM_INIT, None, ALU.mult))

            def df_max(h):
                v.wait_ge(d_sc, h + 1)
                if h >= 2:
                    v.wait_ge(d_a, h - 1)
                mx = dfc[:, h % 2, 8:12]
                V.reduce_max(mx[:, 0:2], at[0][:, 0:2 * P].rearrange("p (r k) -> p r k", r=2), axis=AX)
                link(V.reduce_max(mx[:, 2:4], at[1][:, :].rearrange("p (r k) -> p r k", r=2), axis=AX))
                V.tensor_scalar(dfc[:, h % 2, 0:4], mx, -1.0, None, ALU.mult).then_inc(d_max, 1)

            def df_diff(h):
                v.wait_ge(d_exp, h + 1)
                ri = dfc[:, h % 2, 12:16]
                link(V.reciprocal(ri, dfc[:, h % 2, 4:8]))
                link(V.tensor_scalar(ri[:, 1:4:2], ri[:, 1:4:2], lam_s[:, 5:6], None, ALU.mult))
                V.tensor_scalar(df_t[:, 0:P], df_p0[:, P:2 * P], ri[:, 1:2], None, ALU.mult)
                link(V.tensor_scalar(df_t[:, P:3 * P], df_p1[:, T:2 * T], ri[:, 3:4], None, ALU.mult))
                if h:
                    v.wait_ge(d_tr, h)
                V.scalar_tensor_tensor(df_a[:, 0:P], df_p0[:, 0:P], ri[:, 0:1], df_t[:, 0:P], ALU.mult, ALU.subtract)
                V.scalar_tensor_tensor(df_a[:, P:3 * P], df_p1[:, 0:T], ri[:, 2:3], df_t[:, P:3 * P],
                                       ALU.mult, ALU.subtract).then_inc(d_a, 1)
                v.wait_ge(d_tr, h + 1)
                if h:
                    v.wait_ge(d_pv, h)
                V.tensor_copy(df_aT, at[2][:, 0:384]).then_inc(d_aT, 1)

            for h in range(DFH):
                df_max(h)
                df_diff(h)
                if h % 4 == 3:
                    v.wait_ge(nrt, 3 + h // 4)
                    link(V.reciprocal(df_rt, df_rt))
                    y4 = yT[:, 5 + h:9 + h, :]
                    V.scalar_tensor_tensor(y4, y4, g_df, v3(df_rt, T), ALU.mult, ALU.mult).then_inc(ny, 1)
            v.wait_ge(x2_in, 16 * TB)
            for k in range(4):
                v.wait_ge(*((unit_used, 2 * NB + 3), (unit_used, 2 * NB + 4), (slot_free, 4), (slot_free, 6))[k])
                for b in range(TB):
                    w = slice(512 * k, 512 * k + 512)
                    V.tensor_tensor(xt[:, b, w], pj[2 * (k % 2) + b][:, :], xt[:, b, w], ALU.add).then_inc(h_add, 1)
            v.wait_ge(tr_done, DC)
            for k in range(2):
                c = DC - 2 + k
                last = V.tensor_scalar(xnT[:, c, :], at[3][:, k * T:(k + 1) * T], g_ffn[:, c:c + 1], None, ALU.mult)
            last.then_inc(tr_evac, 1)
            v.wait_ge(h_sq, 4)
            link(V.reduce_sum(rmsc[:, 8:10], v3(fin, 4), axis=AX))
            V.tensor_scalar(rmsc[:, 2:4], rmsc[:, 8:10], 1.0 / D, EPS, ALU.mult, ALU.add).then_inc(h_rs, 1)
            link(V.tensor_scalar(r_desc, iota_s[:, 0:EPG], -1.0, float(EPG), ALU.mult, ALU.add))
            v.wait_ge(achain, 2)
            V.reciprocal(rmsc[:, 10:12], rmsc[:, 4:6]).then_inc(h_rs, 1)
            v.wait_ge(h_rs, 2)
            v.wait_ge(rt_done, 1)
            v.wait_ge(rw_in, 16 * 7)
            for b in range(TB):
                last = V.scalar_tensor_tensor(lg[:, b, :], at[0][:, 36 * b:36 * b + 36], rmsc[:, 10 + b:11 + b], rbias[:, :],
                                              ALU.mult, ALU.add)
            link(last)

            def along(ap, w):
                return ap.broadcast_to([P, TB, w])

            def first_hit(dst, src, mx, w):
                link(V.reduce_max(mx, src, axis=AX))
                link(V.tensor_tensor(r_tp[:, :, 0:w], src, along(mx, w), ALU.is_ge))
                link(V.tensor_tensor(r_tp[:, :, 0:w], r_tp[:, :, 0:w], r_desc[:, 0:w].unsqueeze(1).broadcast_to([P, TB, w]), ALU.mult))
                link(V.reduce_max(r_mx, r_tp[:, :, 0:w], axis=AX))
                link(V.tensor_tensor(dst, r_tp[:, :, 0:w], along(r_mx, w), ALU.is_equal))

            o4 = [P, TB, NG, EPG]
            g4 = r_goh.unsqueeze(3).broadcast_to(o4)

            def by_group(ap):
                return ap.unsqueeze(2).broadcast_to(o4)

            first_hit(r_goh, lg[:, :, 0:NG], r_gm, NG)
            V.tensor_tensor(r_xg[:, :, 0:NG], lg[:, :, 0:NG], along(r_gm, NG), ALU.subtract)
            link(V.tensor_tensor(r_big, lg[:, :, NG:].rearrange("p b (k e) -> p b k e", e=EPG), g4, ALU.mult))
            link(V.reduce_sum(r_el, r_big.rearrange("p b k e -> p b e k"), axis=AX))
            first_hit(r_e1, r_el, r_m1, EPG)
            link(V.scalar_tensor_tensor(r_el, r_e1, NEG, r_el, ALU.mult, ALU.add))
            first_hit(r_e2, r_el, r_m2, EPG)
            V.tensor_tensor(r_xg[:, :, NG:NG + 1], r_m2, r_m1, ALU.subtract).then_inc(rt_m, 1)
            link(V.tensor_tensor(r_s8, r_e1, r_e2, ALU.add))
            sel4, gat4, selb4 = (t.rearrange("p b (k e) -> p b k e", e=EPG) for t in (sel, gat, selb))
            V.tensor_tensor(selb4, by_group(r_s8), g4, ALU.mult).then_inc(rt_sel, 1)
            link(V.tensor_tensor(sel4, by_group(r_s8), g4, ALU.mult))
            v.wait_ge(rk_done, 1)
            rk = at[1][:, 0:2 * NE].rearrange("p (b e) -> p b e", e=NE)
            V.tensor_copy(x_cnt, at[2][:, 0:NE])
            link(V.scalar_tensor_tensor(pos, rk, 1.0, sel[:, :, :], ALU.add, ALU.mult))
            V.tensor_scalar(pos, pos, 1.0, None, ALU.subtract).then_inc(rk_ready, 1)
            v.wait_ge(rk_ready, 1)

            def extra_items():
                link(V.tensor_scalar(x_n, x_cnt, float(SLOT), None, ALU.is_gt))
                for k in range(2, PASSES):
                    link(V.scalar_tensor_tensor(x_n, x_cnt, float(SLOT * k), x_n, ALU.is_gt, ALU.add))
                link(V.tensor_tensor_scan(x_e, ones[:, 0:NE], x_n, 0.0, ALU.mult, ALU.add))
                link(V.tensor_tensor(x_c, x_e, x_n, ALU.subtract))
                V.tensor_copy(n_extra, x_e[:, NE - 1:NE])
                o8, o9 = [P, EXTRA, NE], [P, TB, EXTRA, NE]
                c8, e8 = x_c.unsqueeze(1).broadcast_to(o8), x_e.unsqueeze(1).broadcast_to(o8)
                i8 = iota_s[:, 0:EXTRA].unsqueeze(2).broadcast_to(o8)
                V.tensor_tensor(x_in_e, i8, c8, ALU.is_ge)
                link(V.tensor_tensor(x_t[:, 1], i8, e8, ALU.is_lt))
                link(V.tensor_tensor(x_in_e, x_in_e, x_t[:, 1], ALU.mult))
                link(V.tensor_tensor(x_t[:, 0], x_in_e, iota_s[:, 0:NE].unsqueeze(1).broadcast_to(o8), ALU.mult))
                link(V.reduce_sum(x_id, x_t[:, 0], axis=AX))
                V.tensor_copy(ids, x_id)
                link(V.tensor_scalar(x_c, x_c, 1.0, float(SLOT), ALU.subtract, ALU.mult))
                link(V.tensor_tensor(x_q[:, :, :], pos, x_c.unsqueeze(1).broadcast_to([P, TB, NE]), ALU.add))
                x9 = x_in_e.unsqueeze(1).broadcast_to(o9)
                link(V.tensor_tensor(x_t, x9, x_q.unsqueeze(2).broadcast_to(o9), ALU.mult))
                link(V.reduce_sum(posx[:, :, NE:], x_t, axis=AX))
                V.scalar_tensor_tensor(posx[:, :, NE:], iota_s[:, 0:EXTRA].unsqueeze(1).broadcast_to([P, TB, EXTRA]), -float(SLOT),
                                       posx[:, :, NE:], ALU.mult, ALU.add)
                link(V.tensor_tensor(x_t, x9, gat.unsqueeze(2).broadcast_to(o9), ALU.mult))
                V.reduce_sum(gatx[:, :, NE:], x_t, axis=AX).then_inc(rk_ready, 1)
                v.wait_ge(rk_ready, 2)

            v.sem_inc(e_h, 1)
            gfb = g_ffn.unsqueeze(2).broadcast_to([P, DC, P])

            def select_slots(i_, n0, nq):
                ob3 = [P, nq, SLOT]
                for b in range(TB):
                    at_s = posx[:, b, ds(n0, nq)].unsqueeze(2).broadcast_to(ob3)
                    last = V.tensor_tensor(selS[:, b, 0:nq, :], at_s, iota_s[:, :].unsqueeze(1).broadcast_to(ob3), ALU.is_equal)
                last.then_inc(e_sel, 1)

            def select_weights(i_, n0, nq):
                ob3 = [P, nq, SLOT]
                v.wait_ge(e_sel, i_ + 1)
                for b in range(TB):
                    w = gatx[:, b, ds(n0, nq)].unsqueeze(2).broadcast_to(ob3)
                    last = V.tensor_tensor(selW[:, b, 0:nq, :], selS[:, b, 0:nq, :], w, ALU.mult)
                last.then_inc(e_selw, 1)

            select_slots(0, 0, QE)
            def h_low(u):
                v.wait_ge(h_mid, u + 1)
                V.tensor_tensor(piece(lo, u), piece(hr1, u), piece(mid, u), ALU.subtract).then_inc(h_lo_v, 1)

            h_low(0)
            v.wait_ge(h_hi, 4)
            V.tensor_tensor(piece(hr1, 3), piece(hn, 3), piece(hi, 3), ALU.subtract).then_inc(h_r1_v, 1)
            h_low(2)

            def gates():
                v.wait_ge(rt_e, 1)
                ex2 = r_ex[:, :, NG:NG + 1]
                link(V.reduce_sum(r_gs, r_ex[:, :, 0:NG], axis=AX))
                link(V.scalar_tensor_tensor(r_dn, ex2, 1.0, r_gs, ALU.add, ALU.mult))
                link(V.reciprocal(r_w1, r_dn))
                link(V.tensor_tensor(r_w2, r_w1, ex2, ALU.mult))
                V.tensor_tensor(r_g8, r_e1, along(r_w1, EPG), ALU.mult)
                link(V.tensor_tensor(r_t8, r_e2, along(r_w2, EPG), ALU.mult))
                link(V.tensor_tensor(r_g8, r_g8, r_t8, ALU.add))
                link(V.tensor_tensor(gat4, by_group(r_g8), g4, ALU.mult))


            def v_items(i_, n0, nq, first=False):
                ns = nq * SLOT
                for k in range(4):
                    v.wait_ge(e_gath, i_ * 4 + k + 1)
                    V.tensor_tensor(xeT[:, 4 * k:4 * k + 4, 0:ns], v3(psb[4 + k % 2][:, :], P)[:, :, 0:ns],
                                    gfb[:, 4 * k:4 * k + 4, 0:ns], ALU.mult).then_inc(e_gev, 1)
                if first:
                    gates()
                    select_weights(0, 0, QE)
                    extra_items()
                for q in range(nq):
                    n_ = n0 + q
                    v.wait_ge(slot_free, used(n_, 4))
                    v.wait_ge(e_hT, n_ + 1)
                    V.tensor_copy(a3, psb[1][:, :]).then_inc(e_a3, 1)
                    v.wait_ge(e_silu, n_ + 1)
                    V.tensor_tensor(hT[:, :, :], v3(psb[2][:, 256:512], SLOT), v3(hs, SLOT), ALU.mult).then_inc(e_h, 1)
                    if q == 0:
                        v.wait_ge(e_gt, i_ + 1)
                        V.tensor_copy(gT[0:ns, :], psb[6][0:ns, 0:256]).then_inc(e_gtev, 1)
                        select_slots(i_ + 1, n0 + nq, nq)
                        select_weights(i_ + 1, n0 + nq, nq)
                    v.wait_ge(slot_free, used(n_, 6))
                    v.wait_ge(e_comb, i_ * 8 + 1)
                    for b in range(2):
                        last = V.tensor_copy(ye[64 * q:64 * q + 64, 1024 + 512 * b:1536 + 512 * b],
                                             psb[4][64 * b:64 * b + 64, :])
                    last.then_inc(e_yev, 1)
                for k in range(8):
                    b, c = k // 4, k % 4
                    v.wait_ge(e_comb, i_ * 8 + k + 2)
                    w = slice(512 * c, 512 * c + 512)
                    V.tensor_tensor(xt[:, b, w], psb[6 + k % 2][:, :], xt[:, b, w], ALU.add).then_inc(e_acc, 1)

            v_items(0, 0, QE, first=True)
            with v.Fori(1, ITERS) as it:
                v_items(it, it * QE, QE)
            extra = v.value_load(n_extra[0:1, 0:1], min_val=0, max_val=EXTRA - 1)
            v.wait_ge(e_comb, ITERS * 8 + 1)
            V.memset(gT[SLOT:, :], 0.0)
            with v.If(extra > 0):
                with v.Fori(0, extra) as x_:
                    v_items(x_ + ITERS, x_ + NE, 1)
            v.wait_ge(fg_in, 16)
            for b in range(TB):
                v.wait_ge(f_sq, 2 * b + 1)
                link(V.reduce_sum(rmsc[:, 12 + b:13 + b], fin[:, 4 * b:4 * b + 4], axis=AX))
                V.tensor_scalar(rmsc[:, 2 + b:3 + b], rmsc[:, 12 + b:13 + b], 1.0 / D, EPS, ALU.mult, ALU.add).then_inc(f_rs, 1)
                v.wait_ge(f_sq, 2 * b + 2)
                V.reciprocal(rmsc[:, 6 + b:7 + b], rmsc[:, 4 + b:5 + b]).then_inc(f_rs, 1)
                v.wait_ge(f_rs, 2 * b + 2)
                for k in range(2):
                    w = slice(D // 2 * k, D // 2 * k + D // 2)
                    V.scalar_tensor_tensor(xt[:, b, w], xt[:, b, w], rmsc[:, 6 + b:7 + b], fg[:, w], ALU.mult, ALU.mult).then_inc(f_out, 1)

        @block.tensor
        def _(pe):
            M = nc.tensor.matmul
            TR = nc.tensor.transpose
            pe.wait_ge(cst, 1)
            for m in range(DC // 2):
                if m % 4 == 0:
                    pe.wait_ge(xnorm, m // 4 + 1)
                    pe.wait_ge(xnorm_v, m // 4 + 1)
                if m >= 4:
                    pe.wait_ge(tr_evac_v if m % 2 else tr_evac, (m - 4) // 2 + 1)
                for k2 in range(2):
                    for b in range(TB):
                        c = 2 * m + k2
                        last = TR(pj[m % 4][:, k2 * T + b * P:k2 * T + b * P + P], xn[:, b, c * P:(c + 1) * P], ident[:, :])
                last.then_inc(tr_done, 1)
                if m == 1:
                    pe.wait_ge(par_in, 16 * 7)
                    for i in range(3):
                        TR(at[0][:, 16 * i:16 * i + 16], prow[:, i, :], ident[0:16, 0:16])
                    TR(at[0][:, 48:49], prow[0:1, 3, :], ident[0:1, 0:1]).then_inc(pT_done, 1)
                if m == 3:
                    pe.wait_ge(sp_done, 1)
                    for i in range(3):
                        last = TR(at[1][:, 16 * i:16 * i + 16], spar[:, i, :], ident[0:16, 0:16])
                    last.then_inc(sT_done, 1)
            pe.wait_ge(cst, 2)

            def b_transpose(n_):
                if n_ == 0:
                    pe.wait_ge(b_in, 16 * 4)
                if n_ >= 2:
                    pe.wait_ge(bT_evac, n_ - 1)
                k, q = n_ // 4, n_ % 4
                TR(at[2 + n_ % 2][:, 0:P], bnat[:, k, 4 * q:4 * q + 4, :].rearrange("p a c -> p (a c)"), ident[:, :]).then_inc(bT_done, 1)

            def c_transpose(k):
                if k == 0:
                    pe.wait_ge(c_in, 16 * 4)
                    pe.wait_ge(pT_evac, 1)
                    pe.wait_ge(sp_read, 1)
                for q in range(4):
                    last = TR(at[k][:, P * q:P * q + P], (cnat, cnat2)[k][:, q, :, :].rearrange("p d n -> p (d n)"), ident[:, :])
                last.then_inc(cT_done, 1)

            def wait_unit(n_):
                pe.wait_ge(ring_in[n_ % SLOTS_A], 16 * (n_ // SLOTS_A + 1))

            def project(n_, half, part):
                kind = BLOCKS[n_][0]
                u = 2 * n_ + half
                w = unit(u % SLOTS_A)
                if part == 0:
                    wait_unit(u)
                    if half == 0 and n_ >= 2:
                        pe.wait_ge(pj_evac, n_ - 1)
                    if half == 0 and n_ < 2:
                        pe.wait_ge(tr_evac, DC // 4)
                        pe.wait_ge(tr_evac_v, DC // 4)
                banks = pj[2 * (n_ % 2):2 * (n_ % 2) + 2]
                if kind in ("sbv", "dfv"):
                    b = part // 2
                    for c in range(4 * (part % 2), 4 * (part % 2) + 4):
                        cc = 8 * half + c
                        last = M(banks[b][:, :], xnT[:, cc, b * P:(b + 1) * P], w[:, c, :], start=cc == 0, stop=cc == DC - 1)
                else:
                    for c in range(8):
                        cc = 8 * half + c
                        last = M(banks[part // 2][:, (part % 2) * T:(part % 2) * T + T], w[:, c, part * P:(part + 1) * P], xnT[:, cc, :],
                                 start=cc == 0 and part % 2 == 0, stop=cc == DC - 1, skip_group_check=True)
                if part == 3:
                    last.then_inc(unit_used, 1)

            def s_in(j):
                if j == 0:
                    pe.wait_ge(bT_evac, 8)
                    pe.wait_ge(pj_evac, 1)
                    pe.wait_ge(c_ready, 2)
                if j >= 2:
                    pe.wait_ge(s_prod, j - 1)
                for k in range(2):
                    last = M(at[j % 2][:, k * T:(k + 1) * T], bpad[:, k, j, :], uT[:, j // 4, :], start=True, stop=True)
                last.then_inc(bu_done, 1)

            def s_y(j):
                pe.wait_ge(s_state, j + 1)
                pe.wait_ge(s_im, j + 1)
                q, i = j // 4, j % 4
                if q >= 2 and i == 0:
                    pe.wait_ge(sy_evac, q - 1)
                o = at[2 + q % 2][32 * i:32 * i + 32, 0:T]
                M(o, crT[:, 0, j, :], s_s[j % 2][:, 0, :], start=True, stop=False)
                last = M(o, crT[:, 1, j, :], s_s[j % 2][:, 1, :], start=False, stop=True)
                last.then_inc(sy_used, 1)

            step = 0
            for n_ in range(5):
                for half in range(2):
                    for part in range(4):
                        project(n_, half, part)
                        if n_ == 1:
                            b_transpose(4 * half + part)
                        if n_ == 0 and half == 1 and part >= 2:
                            c_transpose(part - 2)
                        if n_ > 2 or (n_ == 2 and half == 1):
                            if step < ST:
                                s_in(step)
                            if 2 <= step < ST + 2:
                                s_y(step - 2)
                            step += 1

            def glu():
                pe.wait_ge(glu_in, 16)
                pe.wait_ge(gelu_s, 4)
                for co in range(4):
                    for c in range(4):
                        last = M(at[co // 2][:, (co % 2) * T:(co % 2) * T + T], glu_w[:, c, co * P:(co + 1) * P], uT[:, c, :],
                                 start=c == 0, stop=c == 3)
                    last.then_inc(glu_done, 1)

            def sums4(n_, bank):
                pe.wait_ge(nsq, n_)
                for q in range(4):
                    last = M(bank[:, 0:T], ones[:, :], nrm_sq[:, q, :], start=q == 0, stop=q == 3)
                last.then_inc(nsum, 1)

            def sb_scores(hp):
                if hp == 0:
                    pe.wait_ge(pj_evac, 4)
                    pe.wait_ge(glu_sig, 4)
                else:
                    pe.wait_ge(z_w, hp)
                for k in range(2):
                    h = 2 * hp + k
                    z = at[k]
                    M(z[:, 0:T], sk[:, h, 0:P], sq[:, hp, :], start=True, stop=True, skip_group_check=True)
                    M(z[:, T:T + P], sk[:, h, P:T], sq[:, hp, P:T], start=False, stop=True, skip_group_check=True)
                    M(z[:, 0:P], ident_b[:, :], smask_b[:, :], start=False, stop=True, skip_group_check=True)
                    last = M(z[:, T:T + P], ident_b[:, :], smask_b[:, :], start=False, stop=True, skip_group_check=True)
                last.then_inc(z_done, 1)

            def sb_cum(hp):
                pe.wait_ge(z_sp, hp + 1)
                for k in range(2):
                    z = at[k]
                    M(z[:, 0:T], tri_neg[:, :], sp_t[:, k, 0:T], start=False, stop=True, skip_group_check=True)
                    M(z[:, P:T], ones_neg[:, :], sp_t[:, k, T:T + P], start=False, stop=True, skip_group_check=True)
                    last = M(z[:, T:T + P], tri_neg[:, :], sp_t[:, k, T:T + P], start=False, stop=True, skip_group_check=True)
                last.then_inc(z_cum, 1)

            def sb_out(hp):
                pe.wait_ge(z_w, hp + 1)
                if hp:
                    pe.wait_ge(sbo_evac, hp)
                else:
                    pe.wait_ge(nrt, 1)
                for k in range(2):
                    h = 2 * hp + k
                    o = at[2][64 * k:64 * k + 64, :]
                    M(o[:, 0:T], sv[:, 0, 64 * h:64 * h + 64], sb_w[:, k, 0:T], start=True, stop=True)
                    last = M(o[:, P:T], sv[:, 1, 64 * h:64 * h + 64], sb_w[:, k, T:T + P], start=False, stop=True, skip_group_check=True)
                last.then_inc(sbo_done, 1)

            steps = {2: (glu,), 3: (lambda: sums4(1, at[2]), lambda: sb_scores(0))}
            for hp in range(SBH // 2):
                steps[5 + 3 * hp] = (lambda hp=hp: sb_cum(hp),)
                steps[6 + 3 * hp] = (lambda hp=hp: sb_out(hp),) + ((lambda hp=hp: sb_scores(hp + 1),) if hp + 1 < SBH // 2 else ())
            for i in range(16):
                project(5 + i // 8, i // 4 % 2, i % 4)
                for step in steps.get(i, ()):
                    step()

            def df_scores(h):
                if h == 0:
                    pe.wait_ge(pj_evac, 7)
                    pe.wait_ge(nrt, 2)
                if h == 4:
                    pe.wait_ge(pj_evac, NB)
                    pe.wait_ge(nrt, 3)
                if h:
                    pe.wait_ge(d_exp, h)
                M(at[0][:, 0:2 * P], dq[:, h, 0:P], dk[:, h, :, 0:P], start=True, stop=False)
                M(at[0][:, 0:2 * P], ident_b[:, :], mask_b[:, :, :], start=False, stop=True)
                M(at[1][:, :], dq[:, h, P:T], dk[:, h, :, :], start=True, stop=True)
                M(at[1][:, :].rearrange("p (r k) -> p r k", r=2)[:, :, P:T], ident_b[:, :], mask_b[:, :, :],
                  start=False, stop=True, skip_group_check=True).then_inc(d_sc, 1)

            def df_tr(h):
                pe.wait_ge(d_a, h + 1)
                if h:
                    pe.wait_ge(d_aT, h)
                for k in range(3):
                    last = TR(at[2][:, k * P:(k + 1) * P], df_a[:, k * P:(k + 1) * P], ident[:, :])
                last.then_inc(d_tr, 1)

            def df_out(h):
                pe.wait_ge(d_aT, h + 1)
                if h:
                    pe.wait_ge(d_y, h)
                o = at[3][:, (h % 2) * T:(h % 2) * T + T]
                M(o, dv[:, 0, h * P:(h + 1) * P], df_aT[:, 0:T], start=True, stop=True)
                M(o[:, P:T], dv[:, 1, h * P:(h + 1) * P], df_aT[:, T:T + P], start=False, stop=True,
                  skip_group_check=True).then_inc(d_pv, 1)

            def df_sums(k):
                pe.wait_ge(nsq, 3 + k)
                pe.wait_ge(d_exp, 4 * k + 4)
                for i in range(2):
                    last = M(at[i][:, :], ones[:, :], df_sq[:, 512 * i:512 * i + 512], start=True, stop=True)
                last.then_inc(nsum, 1)

            for i in range(24):
                project(7 + i // 8, i // 4 % 2, i % 4)
                h, what = (i - 1) // 4, (i - 1) % 4
                if i == 0:
                    sums4(2, at[3])
                elif i == 19:
                    df_sums(0)
                elif h < 4:
                    if what == 0:
                        df_scores(h)
                    elif what == 2:
                        df_tr(h)
                    elif what == 3:
                        df_out(h)

            def out_unit(n_, parts=(0, 1), chunks=range(8)):
                o_, half = OUT_UNITS[n_]
                u = 2 * NB + n_
                w = unit(u % SLOTS_A)
                for b in parts:
                    if b == 0 and chunks[0] == 0:
                        wait_unit(u)
                        if half == 0 and o_ < 2:
                            pe.wait_ge(pj_evac, NB)
                        if half == 0 and o_ >= 2:
                            pe.wait_ge(h_add, 2 * (o_ - 1))
                        if n_ == 0:
                            pe.wait_ge(ny, 2)
                        if n_ == 2:
                            pe.wait_ge(ny, 3)
                    for c in chunks:
                        cc = 8 * half + c
                        last = M(pj[2 * (o_ % 2) + b][:, :], yT[:, cc, b * P:(b + 1) * P], w[:, c, :], start=cc == 0, stop=cc == DC - 1)
                    if b == 1 and chunks[-1] == 7:
                        last.then_inc(slot_free if n_ >= len(OUT_UNITS) - SLOTS_A else unit_used, 1)

            df_scores(4)
            for h in range(4, DFH):
                if h % 2 == 0:
                    out_unit((h - 4) // 2, (0,))
                else:
                    out_unit((h - 5) // 2, (1,))
                df_tr(h)
                if h + 1 < DFH:
                    df_scores(h + 1)
                df_out(h)
            out_unit(2, chunks=range(0, 4))
            df_sums(1)
            out_unit(3, chunks=range(0, 4))
            pe.wait_ge(ny, 4)
            pe.sem_inc(slot_free, SLOTS_B - SLOTS_A)
            for n_ in (2, 3):
                out_unit(n_, chunks=range(4, 8))
            def h_transpose(k):
                pe.wait_ge(h_add, TB * (k + 1))
                for m in (2 * k, 2 * k + 1):
                    if m >= 2:
                        pe.wait_ge(tr_evac, DC // 4 + m - 1)
                    for k2 in range(2):
                        for b in range(TB):
                            c = 2 * m + k2
                            last = TR(at[2 + m % 2][:, k2 * T + b * P:k2 * T + b * P + P], xt[:, b, c * P:(c + 1) * P], ident[:, :])
                    last.then_inc(tr_done, 1)

            def h_logits(k):
                pe.wait_ge(tr_evac, DC // 4 + 2 * k + 2)
                if k == 0:
                    pe.wait_ge(rw_in, 16 * 7)
                for c in range(4 * k, 4 * k + 4):
                    for b in range(TB):
                        last = M(at[0][:, 36 * b:36 * b + 36], xnT[:, c, b * P:(b + 1) * P], rw[:, c, :],
                                 start=c == 0 and b == 0, stop=c == DC - 1, skip_group_check=True)
                if k == 3:
                    last.then_inc(rt_done, 1)

            out_unit(4)
            h_transpose(0)
            out_unit(5)
            h_transpose(1)
            h_logits(0)
            out_unit(6)
            h_transpose(2)
            h_logits(1)
            out_unit(7)
            h_logits(2)
            h_transpose(3)
            h_logits(3)
            pe.wait_ge(rt_sel, 1)
            M(at[1][:, 0:NE], before_b[:, :], selb[:, 0, :], start=True, stop=True)
            M(at[1][:, NE:2 * NE], before_b[:, :], selb[:, 1, :], start=True, stop=False)
            M(at[1][:, NE:2 * NE], ones_b[:, :], selb[:, 0, :], start=False, stop=True)
            M(at[2][:, 0:NE], ones_b[:, :], selb[:, 0, :], start=True, stop=False)
            M(at[2][:, 0:NE], ones_b[:, :], selb[:, 1, :], start=False, stop=True).then_inc(rk_done, 1)
            pe.sem_inc(e_hT, 1)
            pe.sem_inc(e_comb, 1)
            pe.sem_inc(e_yev, 1)

            def landed(n_, k):
                s = slot_of(k)
                base = 16 * (UNITS_A // SLOTS_A) if s < SLOTS_A else 0
                pe.wait_ge(ring_in[s], n_ * 16 + base + 16)
                return s

            def pe_items(i_, n0, nq):
                ns = nq * SLOT
                pe.wait_ge(e_sel, i_ + 1)
                for c in range(DC):
                    if c % 8 == 0:
                        pe.wait_ge(h_lo, c // 8 + 1)
                        pe.wait_ge(h_lo_v, c // 8 + 1)
                    if c % 4 == 0 and c >= 8:
                        pe.wait_ge(e_gev, i_ * 4 + c // 4 - 1)
                    k = 0
                    for part in (hi, mid, lo):
                        for b in range(TB):
                            last = M(psb[4 + (c // 4) % 2][:, (c % 4) * P:(c % 4) * P + ns], part[:, b, c * P:(c + 1) * P],
                                     selS[:, b, 0:nq, :].rearrange("p q s -> p (q s)"), start=k == 0, stop=k == 5)
                            k += 1
                    if c % 4 == 3:
                        last.then_inc(e_gath, 1)
                pe.wait_ge(e_gev, i_ * 4 + 4)
                for q in range(nq):
                    n_ = n0 + q
                    for m in range(2):
                        for half in range(2):
                            s = landed(n_, 2 * m + half)
                            for c in range(8):
                                cc = 8 * half + c
                                i = c % 2
                                last = M(psb[m][64 * i:64 * i + 64, :], xeT[:, cc, 64 * q:64 * q + 64], unit(s)[:, c, :],
                                         start=cc < 2, stop=cc >= DC - 2)
                            last.then_inc(slot_free, 1)
                    for m, (ready, src) in enumerate(((e_a1, a1), (e_a3, a3))):
                        pe.wait_ge(ready, n_ + 1)
                        for f in range(EC):
                            last = M(psb[2][:, 256 * m + 64 * f:256 * m + 64 * f + 64], src[:, f * P:(f + 1) * P], stack2[:, :],
                                     start=True, stop=True)
                    last.then_inc(e_hT, 1)
                    if q == 0:
                        pe.wait_ge(e_selw, i_ + 1)
                        for b in range(TB):
                            last = TR(psb[6][:, b * P:b * P + P], selW[:, b, :, :].rearrange("p q s -> p (q s)"), ident[:, :])
                        last.then_inc(e_gt, 1)
                    pe.wait_ge(e_h, n_ + 2)
                    pe.wait_ge(e_yev, n_ * 2 + 1)
                    for half in range(2):
                        s = landed(n_, 4 + half)
                        for f in range(2):
                            for i in range(4):
                                last = M(psb[3 + i // 2][64 * (i % 2):64 * (i % 2) + 64, :], hT[:, 2 * half + f, :],
                                         unit2(s)[:, f, 512 * i:512 * i + 512],
                                         start=half == 0 and f == 0, stop=half == 1 and f == 1)
                        last.then_inc(slot_free, 1)
                pe.wait_ge(e_gtev, i_ + 1)
                pe.wait_ge(e_yev, n0 * 2 + 2 * nq + 1)
                for k in range(8):
                    b, c = k // 4, k % 4
                    if k >= 2:
                        pe.wait_ge(e_acc, i_ * 8 + k - 1)
                    M(psb[6 + k % 2][:, :], gT[:, b * P:b * P + P], ye[:, 512 * c:512 * c + 512],
                      start=True, stop=True).then_inc(e_comb, 1)

            with pe.Fori(0, ITERS) as it:
                pe_items(it, it * QE, QE)
            pe.wait_ge(rk_ready, 2)
            extra = pe.value_load(n_extra[0:1, 0:1], min_val=0, max_val=EXTRA - 1)
            with pe.If(extra > 0):
                with pe.Fori(0, extra) as x_:
                    pe_items(x_ + ITERS, x_ + NE, 1)


_INS = ['x', 'norm_mix_g', 'w_in', 'sb_norm_g', 'ssm_lam_re', 'ssm_lam_im', 'ssm_b_re', 'ssm_b_im', 'ssm_c_re',
        'ssm_c_im', 'ssm_d', 'ssm_log_dt', 'ssm_w_glu', 'ssm_b_glu', 'ssm_norm_g', 'diff_lq1', 'diff_lk1',
        'diff_lq2', 'diff_lk2', 'diff_subln_g', 'w_out', 'norm_ffn_g', 'router_group_w', 'router_group_b',
        'router_expert_w', 'router_expert_b', 'expert_w1', 'expert_w3', 'expert_w2', 'final_norm_g']
_OUTS = [((1, T, D), 'float32')]


def kernel(**inputs):
    import numpy as _np
    import concourse.bacc as _bacc
    from concourse import mybir as _mybir
    from concourse.bass_utils import run_bass_kernel_spmd as _run

    nc = _bacc.Bacc("TRN2", target_bir_lowering=False, num_devices=1)
    arrays, args = {}, []
    for name in _INS:
        a = _np.ascontiguousarray(inputs[name])
        arrays[f"in_{name}_dram"] = a
        args.append(nc.dram_tensor(f"in_{name}_dram", a.shape, _mybir.dt.from_np(a.dtype), kind="ExternalInput").ap())
    for i, (shape, dtype) in enumerate(_OUTS):
        dt = _mybir.dt.from_np(_np.dtype(dtype))
        args.append(nc.dram_tensor(f"out_{i}_dram", shape, dt, kind="ExternalOutput").ap())
    build(nc, *args)
    r = _run(nc, [arrays], core_ids=[0])
    got = tuple(r.results[0][f"out_{i}_dram"] for i in range(len(_OUTS)))
    return got[0]
```

```python
import concourse.bass as bass
from concourse import mybir
from contextlib import ExitStack
import math

D = 2048
T = 256
P = 128
TB = T // P
DC = D // P
SBW = D // 4
SBH = SBW // 64
SSW = D // 4
SG, SN, SC = SSW // 16, 64, 16
ST = SG * SN // P
DFH = (D - SBW - SSW) // 128
IN_COLS = 3 * SBW + SSW + 3 * (D - SBW - SSW)
NG, EPG = 4, 8
NE = NG * EPG
DE = D // 4
EC = DE // P
EPS = 1e-6
LAM_INIT = 0.8 - 0.6 * math.exp(-0.3 * 0)
QSCALE = 64 ** -0.5
NEG = -1e30

UW = 4096
SLOTS_A = 2
SLOTS_B = 6
SLOT = 64
QE = P // SLOT
ITERS = NE // QE
PASSES = T // SLOT
EXTRA = 8

BLOCKS = ([("u", 0, 3 * SBW)] + [("sbq", 0, 0), ("sbk", 0, SBW), ("sbv", 0, 2 * SBW)]
          + [(k, i, 3 * SBW + SSW + o * (D - SBW - SSW) + 512 * i)
             for i in range(2) for o, k in enumerate(("dfq", "dfk", "dfv"))])
NB = len(BLOCKS)
OUT_UNITS = [[(8 * half + c, o) for c in range(8)] for o, half in ((0, 0), (1, 0))]
OUT_UNITS += [[(8 + c, o) for c in range(4) for o in (0, 1)], [(c, 2) for c in range(8)],
              [(12 + c, o) for c in range(4) for o in (0, 1)]]
OUT_UNITS += [[(8 * half + c, o) for c in range(8)] for o, half in ((2, 1), (3, 0), (3, 1))]
UNITS_A = 2 * NB + len(OUT_UNITS)
ROWS = 8 * UNITS_A
BUFS = 4


def rows_done(part):
    return 2 * (part + 1)


def rows_out(n):
    return 8 * (2 * NB + n)


P_BT = 8
S_STEP = [20 + 3 * k // 2 for k in range(ST + 2)]
P_GLU = S_STEP[-1] + 3
P_SB = P_GLU + 2
P_SBN = P_SB + 3 * (SBH // 2) + 1
P_DF = P_SBN + 1
P_DFN = P_DF + 14


def build(nc, x, norm_mix_g, w_in, sb_norm_g, lam_re, lam_im, b_re, b_im, c_re, c_im, ssm_d, log_dt,
          w_glu, b_glu, ssm_norm_g, lq1, lk1, lq2, lk2, subln_g, w_out, norm_ffn_g,
          rg_w, rg_b, re_w, re_b, e_w1, e_w3, e_w2, final_g, out):
    F = mybir.dt.float32
    BF = mybir.dt.bfloat16
    I32 = mybir.dt.int32
    ALU = mybir.AluOpType
    ACT = mybir.ActivationFunctionType
    AX = mybir.AxisListType.X
    ds = bass.ds

    ctx = ExitStack()
    with ctx:
        def sb(name, shape, dt=F):
            return ctx.enter_context(nc.sbuf_tensor(name, shape, dt))

        def sem(name):
            return ctx.enter_context(nc.semaphore(name))

        ring4_at = -(-nc.sbuf_base // 32) * 32
        ring4 = sb("ring4", [P, 4 * UW])
        reg_e = sb("reg_e", [P, 2 * UW])
        reg_x = sb("reg_x", [P, TB * D])
        reg_t_at = -(-nc.sbuf_base // 32) * 32
        reg_t = sb("reg_t", [P, DC * T])
        reg_y = sb("reg_y", [P, DC * T])
        R = mybir.dt.float32r
        act_hi = nc.alloc_sbuf_tensor_at("act_hi", [P, DC, T], R, offset=reg_t_at)
        act_lo = nc.alloc_sbuf_tensor_at("act_lo", [P, DC, T], R, offset=ring4_at + 4 * 2 * UW)
        w_hi = nc.alloc_sbuf_tensor_at("w_hi", [P, BUFS, 512], R, offset=ring4_at + 4 * 3 * UW)
        w_lo = nc.alloc_sbuf_tensor_at("w_lo", [P, BUFS, 512], R, offset=ring4_at + 4 * (3 * UW + BUFS * 512))
        reg_s = sb("reg_s", [P, 4096])
        reg_d = sb("reg_d", [P, 8192])

        def slot(s):
            return ring4[:, s * UW:(s + 1) * UW] if s < 4 else reg_e[:, (s - 4) * UW:(s - 3) * UW]

        def slot_of(j):
            return (j + 4) % SLOTS_B

        def used(n_, k):
            return n_ * 6 + SLOTS_B + k

        def unit(s):
            return slot(s).rearrange("p (c n) -> p c n", n=512)

        def unit2(s):
            return slot(s).rearrange("p (c n) -> p c n", n=D)

        def v3(ap, b):
            return ap.rearrange("p (a b) -> p a b", b=b)

        xt = v3(reg_x[:, :], D)
        h_T = v3(reg_y[:, :], T)
        yT = v3(reg_y[:, :], T)
        xn = v3(reg_y[:, :], D)
        uT = yT[:, 4:8, :]
        ph = reg_e[:, :].rearrange("p (k j t) -> p k j t", k=2, t=T)
        bpad = reg_x[:, :].rearrange("p (k j n) -> p k j n", k=2, n=P)
        s_ab = [reg_d[:, i * 1024:(i + 1) * 1024].rearrange("p (k r t) -> p k r t", k=2, t=T) for i in range(2)]
        s_v = [v3(reg_d[:, 2048 + i * 512:2560 + i * 512], T) for i in range(2)]
        s_w = v3(reg_d[:, 3072:3584], T)
        s_df = [reg_d[:, 3584 + i * 1024:4608 + i * 1024].rearrange("p (k r t) -> p k r t", k=2, t=T) for i in range(2)]
        s_s = [v3(reg_d[:, 5632 + i * 512:6144 + i * 512], T) for i in range(2)]
        bnat = reg_d[:, 6656:7680].rearrange("p (k j c) -> p k j c", k=2, c=32)
        cnat = reg_d[:, 7680:8192].rearrange("p (q d n) -> p q d n", q=4, d=2)
        cnat2 = reg_s[:, 0:512].rearrange("p (q d n) -> p q d n", q=4, d=2)
        sq = v3(reg_s[:, 0:1024], T)
        sk = v3(reg_s[:, 1024:3072], T)
        sv = v3(reg_s[:, 3072:4096], 512)
        dq = v3(reg_d[:, 0:2048], T)
        dk = reg_d[:, 2048:6144].rearrange("p (h r t) -> p h r t", h=DFH, r=2)
        dv = v3(reg_d[:, 6144:8192], 1024)
        glu_w = v3(reg_e[:, 0:2048], 512)
        glu_s = v3(reg_e[:, 2048:3072], T)
        nrm_sq = v3(reg_e[:, 3072:4096], T)
        sp_a = v3(reg_e[:, 4096:4864], 384)
        sp_e = v3(reg_e[:, 4864:5632], 384)
        sp_t = v3(reg_e[:, 5632:6400], 384)
        sb_w = v3(reg_e[:, 6400:7168], 384)
        df_p0 = reg_e[:, 0:256]
        df_p1 = reg_e[:, 256:768]
        df_t = reg_e[:, 768:1152]
        df_a = reg_e[:, 1152:1536]
        df_aT = reg_e[:, 1536:1920]
        df_sq = reg_e[:, 2048:3072]
        df_rt = reg_e[:, 3072:4096]
        rstd_t = reg_e[:, 7680:7936]

        ident = sb("ident", [P, P])
        ones = sb("ones", [P, P])
        tri_neg = sb("tri_neg", [P, P])
        ones_neg = sb("ones_neg", [P, P])
        ident_b = sb("ident_b", [P, P], BF)
        ones_b = sb("ones_b", [P, P], BF)
        before_b = sb("before_b", [P, P], BF)
        mask_b = sb("mask_b", [P, 2, P], BF)
        smask_b = sb("smask_b", [P, P], BF)
        stack2 = sb("stack2", [P, SLOT])
        rowm = sb("rowm", [P, 4])
        cmask = sb("cmask", [P, 2])
        iota_i = reg_s[:, 3072:3072 + SLOT].bitcast(I32)
        iota_s = sb("iota_s", [P, SLOT])
        prow = sb("prow", [DC, 4, P])
        pcol = sb("pcol", [P, 64])
        g_mix, g_ffn = pcol[:, 0:16], pcol[:, 16:32]
        g_sb, g_ssm, b_gl, d_sk = (pcol[:, 32 + 4 * i:36 + 4 * i] for i in range(4))
        g_df = pcol[:, 48:49]
        spar = reg_s[0:ST, 1024:1024 + 3 * P].rearrange("p (k n) -> p k n", n=P)
        sw = sb("sw", [P, 24, ST])
        scol = sw[:, 19:24, :]
        pw = sb("pw", [P, 4, ST])
        dt2 = sb("dt2", [ST, 2])
        ki = sb("ki", [P, ST], I32)
        crT = sb("crT", [P, 2, ST, 32])
        lamv = sb("lamv", [P, 4, 64])
        lam_s = sb("lam_s", [P, 8])
        rmsc = sb("rmsc", [P, 16])
        dfc = sb("dfc", [P, 2, 16])
        rw = sb("rw", [P, DC, 4 + NE])
        rbias = sb("rbias", [P, 4 + NE])

        psb = [ctx.enter_context(nc.psum_tensor(f"ps{i}", [P, 512], F)) for i in range(8)]
        pj, at = psb[0:4], psb[4:8]

        def out_bank(o, b):
            return (pj[b], pj[2 + b], at[2 + b], pj[b])[o]

        ring_in = [sem(f"ring_in{i}") for i in range(SLOTS_B)]
        row_hi = sem("row_hi")
        row_lo = sem("row_lo")
        row_used = sem("row_used")
        y_hi = sem("y_hi")
        y_lo = sem("y_lo")
        slot_free = sem("slot_free")
        x_in = [sem(f"x_in{i}") for i in range(2)]
        lam_in = sem("lam_in")
        par_in = sem("par_in")
        c_in = sem("c_in")
        lq_in = sem("lq_in")
        b_in = sem("b_in")
        glu_in = sem("glu_in")
        rw_in = sem("rw_in")
        x2_in = sem("x2_in")
        fg_in = sem("fg_in")
        cst = sem("cst")
        b_zero = sem("b_zero")
        gchain = sem("gchain")
        vchain = sem("vchain")
        achain = sem("achain")
        xsum = sem("xsum")
        xnorm_v = sem("xnorm_v")
        tr_evac_v = sem("tr_evac_v")
        xnorm = sem("xnorm")
        rstd_s = sem("rstd_s")
        tr_done = sem("tr_done")
        tr_evac = sem("tr_evac")
        pT_done = sem("pT_done")
        pT_evac = sem("pT_evac")
        sp_done = sem("sp_done")
        sp_read = sem("sp_read")
        sT_done = sem("sT_done")
        bT_done = sem("bT_done")
        bT_evac = sem("bT_evac")
        cT_done = sem("cT_done")
        c_ready = sem("c_ready")
        pj_evac = sem("pj_evac")
        bu_done = sem("bu_done")
        s_prod = sem("s_prod")
        s_rot = sem("s_rot")
        s_scan = sem("s_scan")
        s_out = sem("s_out")
        s_state = sem("s_state")
        sy_used = sem("sy_used")
        sy_evac = sem("sy_evac")
        gelu_s = sem("gelu_s")
        glu_done = sem("glu_done")
        glu_sig = sem("glu_sig")
        glu_y = sem("glu_y")
        nsq = sem("nsq")
        nsum = sem("nsum")
        nrt = sem("nrt")
        ny = sem("ny")
        k_zero = sem("k_zero")
        dk_zero = sem("dk_zero")
        z_done = sem("z_done")
        z_abs = sem("z_abs")
        z_sp = sem("z_sp")
        z_cum = sem("z_cum")
        z_w = sem("z_w")
        sbo_done = sem("sbo_done")
        sbo_evac = sem("sbo_evac")
        d_sc = sem("d_sc")
        d_max = sem("d_max")
        d_exp = sem("d_exp")
        d_a = sem("d_a")
        d_tr = sem("d_tr")
        d_aT = sem("d_aT")
        d_pv = sem("d_pv")
        d_y = sem("d_y")
        lam_sum = sem("lam_sum")
        lam_exp = sem("lam_exp")
        h_add = sem("h_add")
        h_sq = sem("h_sq")
        h_rs = sem("h_rs")
        hn_s = sem("hn_s")
        h_hi = sem("h_hi")
        h_r1 = sem("h_r1")
        h_r1_v = sem("h_r1_v")
        h_mid = sem("h_mid")
        h_lo = sem("h_lo")
        h_lo_v = sem("h_lo_v")
        rt_done = sem("rt_done")
        rt_sel = sem("rt_sel")
        rt_m = sem("rt_m")
        rt_e = sem("rt_e")
        rk_done = sem("rk_done")
        rk_ready = sem("rk_ready")
        e_sel = sem("e_sel")
        e_selw = sem("e_selw")
        e_gath = sem("e_gath")
        e_gev = sem("e_gev")
        e_gt = sem("e_gt")
        e_gtev = sem("e_gtev")
        e_a1 = sem("e_a1")
        e_a3 = sem("e_a3")
        e_hT = sem("e_hT")
        e_silu = sem("e_silu")
        e_h = sem("e_h")
        e_yev = sem("e_yev")
        e_comb = sem("e_comb")
        e_acc = sem("e_acc")
        f_sq = sem("f_sq")
        f_rs = sem("f_rs")
        f_out = sem("f_out")
        f_st = sem("f_st")

        block = ctx.enter_context(nc.Block())

        hi = reg_t[:, 0:2048].bitcast(BF).rearrange("p (b d) -> p b d", d=D)
        mid = reg_t[:, 2048:4096].bitcast(BF).rearrange("p (b d) -> p b d", d=D)
        lo = reg_s[:, 0:2048].bitcast(BF).rearrange("p (b d) -> p b d", d=D)
        lg = v3(reg_s[:, 2048:2048 + 2 * 36], 36)
        sel = v3(reg_s[:, 2128:2128 + 2 * NE], NE)
        selb = reg_s[:, 2256:2256 + NE].bitcast(BF).rearrange("p (b e) -> p b e", e=NE)
        x_cnt = reg_s[:, 2192:2192 + NE]
        x_q = v3(reg_s[:, 2288:2288 + 2 * NE], NE)
        rtmp = reg_s[:, 2352:2352 + 256]
        posx = v3(reg_s[:, 2608:2608 + 2 * (NE + EXTRA)], NE + EXTRA)
        gatx = v3(reg_s[:, 2688:2688 + 2 * (NE + EXTRA)], NE + EXTRA)
        pos, gat = posx[:, :, 0:NE], gatx[:, :, 0:NE]
        x_n = reg_s[:, 2768:2768 + NE]
        x_c = reg_s[:, 2800:2800 + NE]
        x_e = reg_s[:, 2832:2832 + NE]
        x_id = reg_s[:, 2864:2864 + EXTRA]
        n_extra = reg_s[:, 2872:2873].bitcast(I32)
        ids = reg_s[:, 2880:2880 + EXTRA].bitcast(I32)
        x_in_e = v3(reg_s[:, 2900:2900 + EXTRA * NE], NE)
        x_t = reg_s[:, 3156:3156 + 2 * EXTRA * NE].rearrange("p (b x e) -> p b x e", b=2, e=NE)
        r_ = lambda o, w: v3(rtmp[:, o:o + 2 * w], w)
        r_gm, r_m1, r_m2, r_mx, r_gs, r_dn, r_w1, r_w2 = (r_(2 * i, 1) for i in range(8))
        r_tp, r_el, r_e1, r_e2, r_s8, r_g8, r_t8 = (r_(16 + 16 * i, EPG) for i in range(7))
        r_goh, r_xg, r_ex, r_desc = r_(128, NG), r_(136, 5), r_(146, 5), rtmp[:, 156:164]
        r_big = rtmp[:, 164:228].rearrange("p (b k e) -> p b k e", b=2, e=EPG)
        xeT = v3(reg_y[:, 0:2048], P)
        a1 = reg_y[:, 2048:2560]
        a3 = reg_y[:, 2560:3072]
        hs = reg_y[:, 3072:3328]
        hT = v3(reg_y[:, 3328:3584], SLOT)
        gT = reg_y[:, 3584:3840]
        selS = reg_y[:, 3840:3968].bitcast(BF).rearrange("p (b q s) -> p b q s", b=2, q=QE)
        selW = reg_s[:, 3840:4096].rearrange("p (b q s) -> p b q s", b=2, q=QE)
        hn = v3(reg_d[:, 0:4096], D)
        hr1 = v3(reg_d[:, 4096:8192], D)

        def piece(t, u):
            return t[:, u % 2, D // 2 * (u // 2):D // 2 * (u // 2) + D // 2]

        ye = reg_d[:, 4096:6144]
        fg = reg_d[:, 0:2048]
        junk = (reg_d[:, 2048:4096], reg_d[:, 6144:8192])
        fin = dfc[:, 0, 0:8]

        w_in_u = w_in.rearrange("l (c p) n -> p (l c) n", p=P)
        w_out_u = w_out.rearrange("l (c p) n -> p (l c) n", p=P)
        x_v = x.rearrange("o (b p) d -> p (o b) d", p=P)
        out_v = out.rearrange("o (b p) d -> p (o b) d", p=P)
        w1_v = e_w1.rearrange("l e (h c p) n -> p (l e) h c n", h=2, p=P)
        w3_v = e_w3.rearrange("l e (h c p) n -> p (l e) h c n", h=2, p=P)
        w2_v = e_w2.rearrange("l e (h c p) n -> p (l e) h c n", h=2, p=P)

        @block.sync
        def _(sp):
            for b in range(TB):
                sp.dma_start(xt[:, b, :], x_v[:, b, :]).then_inc(x_in[b], 16)
            sp.dma_start(spar[:, 0, :], lam_re.rearrange("l (j h) n -> (l j) (h n)", h=2)).then_inc(lam_in, 16)
            sp.dma_start(spar[:, 1, :], lam_im.rearrange("l (j h) n -> (l j) (h n)", h=2)).then_inc(lam_in, 16)
            sp.dma_start(dt2[:, :], log_dt.rearrange("l (j h) -> (l j) h", h=2)).then_inc(lam_in, 16)
            sp.dma_start(prow[:, 0, :], norm_mix_g.rearrange("l (c p) -> (l c) p", p=P)).then_inc(par_in, 16)
            sp.dma_start(prow[:, 1, :], norm_ffn_g.rearrange("l (c p) -> (l c) p", p=P)).then_inc(par_in, 16)
            for i, r in enumerate((sb_norm_g, ssm_norm_g, b_glu)):
                sp.dma_start(prow[4 * i:4 * i + 4, 2, :], r.rearrange("l (c p) -> (l c) p", p=P)).then_inc(par_in, 16)
            sp.dma_start(prow[12:16, 2, :], ssm_d.rearrange("l (q g) c -> (l q) (g c)", q=4)).then_inc(par_in, 16)
            sp.dma_start(prow[0:1, 3, :], subln_g).then_inc(par_in, 16)

            def later_parameters():
                for k, (cn, c) in enumerate(((cnat, c_re), (cnat2, c_im))):
                    cv = c.rearrange("l (q g) c n -> (l g c) q n", q=4)
                    for d in range(2):
                        sp.dma_start(cn[:, :, d, :], cv).then_inc(c_in, 16)
                for i, r in enumerate((lq1, lk1, lq2, lk2)):
                    sp.dma_start(lamv[:, i, :], r.broadcast_to([P, 64])).then_inc(lq_in, 16)
                for k in range(NG):
                    sp.dma_start(rw[:, :, NG + EPG * k:NG + EPG * (k + 1)],
                                 re_w[:, k].rearrange("l (c p) e -> p (l c) e", p=P)).then_inc(rw_in, 16)
                sp.dma_start(rw[:, :, 0:NG], rg_w.rearrange("l (c p) e -> p (l c) e", p=P)).then_inc(rw_in, 16)
                sp.dma_start(rbias[:, 0:NG], rg_b.broadcast_to([P, NG])).then_inc(rw_in, 16)
                sp.dma_start(rbias[:, NG:], re_b.rearrange("l g e -> l (g e)").broadcast_to([P, NE])).then_inc(rw_in, 16)

            for n in range(UNITS_A):
                s = n % SLOTS_A
                if n < 2 * NB:
                    c0 = BLOCKS[n // 2][2]
                    src = w_in_u[:, 8 * (n % 2):8 * (n % 2) + 8, c0:c0 + 512]
                else:
                    (c0, o), (c1, o1) = OUT_UNITS[n - 2 * NB][0], OUT_UNITS[n - 2 * NB][-1]
                    src = w_out_u[:, c0:c1 + 1, 512 * o:512 * o1 + 512]
                if n >= SLOTS_A:
                    sp.wait_ge(row_lo, 8 * (n - SLOTS_A + 1))
                sp.dma_start(slot(s).rearrange("p (c n) -> p c n", n=src.shape[-1]), src).then_inc(ring_in[s], 16)
                if n == 1:
                    later_parameters()
                if n == 12:
                    sp.wait_ge(bu_done, ST)
                    for b in range(TB):
                        sp.dma_start(xt[:, b, :], x_v[:, b, :]).then_inc(x2_in, 16)

            def item(n_, e):
                for k in range(6):
                    s = slot_of(k)
                    sp.wait_ge(slot_free, n_ * 6 + k + 1)
                    w = (w1_v, w3_v, w2_v)[k // 2]
                    src = w[:, ds(e, 1), k % 2, :, :]
                    sp.dma_start(unit(s) if k < 4 else unit2(s), src.rearrange("p e c n -> p (e c) n")).then_inc(ring_in[s], 16)

            with sp.Fori(0, NE) as e:
                item(e, e)
            sp.wait_ge(rk_ready, 2)
            extra = sp.value_load(n_extra[0:1, 0:1], min_val=0, max_val=EXTRA - 1)
            with sp.If(extra > 0):
                with sp.Fori(0, extra) as x_:
                    item(x_ + NE, sp.value_load(ids[0:1, ds(x_, 1)], min_val=0, max_val=NE - 1))
            for k in range(2 * TB):
                sp.wait_ge(f_out, k + 1)
                w = slice(D // 2 * (k % 2), D // 2 * (k % 2) + D // 2)
                sp.dma_start(out_v[:, k // 2, w], xt[:, k // 2, w]).then_inc(f_st, 16)
            sp.wait_ge(f_st, 16 * 2 * TB)

        @block.gpsimd
        def _(g):
            n = [0]

            def link(ins):
                n[0] += 1
                ins.then_inc(gchain, 1)
                g.wait_ge(gchain, n[0])

            G = nc.gpsimd
            link(G.memset(ident[:], 0.0))
            pick_ident = G.affine_select(out=ident[:, :], in_=ident[:, :], compare_op=ALU.not_equal, fill=1.0, base=0,
                                         pattern=[[-1, P]], channel_multiplier=1)
            pick_ident.then_inc(cst, 1)
            for t, val in ((ones, 1.0), (tri_neg, -1.0), (ones_neg, -1.0), (ident_b, 0.0), (ones_b, 1.0),
                           (before_b, 1.0), (mask_b, 0.0), (smask_b, 0.0), (stack2, 0.0), (rowm, 1.0), (cmask, 1.0)):
                last = G.memset(t[:], val)
            link(last)

            def pick(t, pattern, base, cm, op, fill):
                return G.affine_select(out=t, in_=t, compare_op=op, fill=fill, base=base, pattern=pattern,
                                       channel_multiplier=cm)

            pick(ident_b[:, :], [[-1, P]], 0, 1, ALU.not_equal, 1.0)
            pick(tri_neg[:, :], [[-1, P]], 0, 1, ALU.is_ge, 0.0)
            pick(before_b[:, :], [[1, P]], 0, -1, ALU.is_gt, 0.0)
            pick(mask_b[:, :, :], [[0, 2], [-1, P]], 0, 1, ALU.is_ge, NEG)
            pick(smask_b[:, :], [[1, P]], 0, -1, ALU.is_gt, NEG)
            for k in range(QE):
                link(pick(stack2[:, :], [[-1, SLOT]], -SLOT * k, 1, ALU.not_equal, 1.0))
            pick(rowm[:, :], [[-32, 4]], 0, 1, ALU.is_ge, 0.0)
            link(pick(cmask[:, :], [[-64, 2]], 0, 1, ALU.is_ge, 0.0))
            pick(rowm[:, :], [[32, 4]], 31, -1, ALU.is_ge, 0.0)
            pick(cmask[:, :], [[64, 2]], 63, -1, ALU.is_ge, 0.0)
            link(G.iota(iota_i, [[1, SLOT]], base=0, channel_multiplier=0))
            G.tensor_copy(iota_s[:, :], iota_i).then_inc(cst, 1)
            G.memset(bnat[:, :, :, :], 0.0).then_inc(b_zero, 1)
            g.wait_ge(b_zero, 1)
            for k, b in enumerate((b_re, b_im)):
                bv = b.rearrange("l (j h) n c -> (l h) n j c", h=2)
                for h in range(2):
                    g.dma_start(bnat[64 * h:64 * h + 64, k, :, 16 * h:16 * h + 16], bv[h]).then_inc(b_in, 16)
            G.memset(ph[:, 0, :, 0:1], 1.0)
            G.memset(ph[:, 1, :, 0:1], 0.0).then_inc(k_zero, 1)

            row = [0]

            def lows(done):
                while row[0] < min(done + BUFS, ROWS):
                    i = row[0]
                    u, c = i // 8, i % 8
                    g.wait_ge(row_hi, i + 1)
                    G.tensor_tensor(w_lo[:, i % BUFS, :], unit(u % SLOTS_A)[:, c, :], w_hi[:, i % BUFS, :], ALU.subtract).then_inc(row_lo, 1)
                    row[0] += 1
                g.wait_ge(row_lo, row[0])

            lows(rows_done(7))
            g.wait_ge(k_zero, 1)
            g.wait_ge(cT_done, 2)
            link(G.memset(sk[64:128, 0:8:2, :], 0.0))
            G.memset(sk[0:64, 1:8:2, :], 0.0).then_inc(dk_zero, 1)
            g.wait_ge(dk_zero, 1)
            lows(rows_done(S_STEP[-1]))
            g.wait_ge(sy_used, ST)
            link(G.memset(dk[64:128, :, 0, :], 0.0))
            G.memset(dk[0:64, :, 1, :], 0.0).then_inc(dk_zero, 1)
            g.wait_ge(dk_zero, 2)
            lows(ROWS)
            def h_rest(u):
                g.wait_ge(h_hi, u + 1)
                G.tensor_tensor(piece(hr1, u), piece(hn, u), piece(hi, u), ALU.subtract).then_inc(h_r1, 1)

            def h_low(u):
                g.wait_ge(h_mid, u + 1)
                G.tensor_tensor(piece(lo, u), piece(hr1, u), piece(mid, u), ALU.subtract).then_inc(h_lo, 1)

            for u in range(2):
                h_rest(u)
            h_low(1)
            h_low(3)

        @block.scalar
        def _(a):
            A = nc.scalar
            cp = ACT.Copy
            half = D // 2
            a.wait_ge(x_in[0], 16)
            A.activation(xn[:, 0, :], xt[:, 0, :], ACT.Square, accum_out=rmsc[:, 0:1]).then_inc(xsum, 1)
            a.wait_ge(x_in[1], 16)
            A.activation(xn[:, 1, 0:half], xt[:, 1, 0:half], ACT.Square, accum_out=rmsc[:, 14:15]).then_inc(xsum, 1)
            a.wait_ge(rstd_s, 1)
            A.activation(rmsc[:, 4:6], rmsc[:, 2:4], ACT.Sqrt).then_inc(achain, 1)
            a.wait_ge(rstd_s, 2)
            for i in range(2):
                w = slice(half * i, half * i + half)
                A.activation(xn[:, 0, w], xt[:, 0, w], cp, scale=rmsc[:, 6:7]).then_inc(xnorm, 1)
            row = [0]

            def highs(done):
                while row[0] < min(done + BUFS, ROWS):
                    i = row[0]
                    u, c = i // 8, i % 8
                    if c == 0:
                        a.wait_ge(ring_in[u % SLOTS_A], 16 * (u // SLOTS_A + 1))
                    if i >= BUFS:
                        a.wait_ge(row_used, i - BUFS + 1)
                    A.activation(w_hi[:, i % BUFS, :], unit(u % SLOTS_A)[:, c, :], cp).then_inc(row_hi, 1)
                    row[0] += 1

            a.wait_ge(pT_evac, 1)
            for n_ in range(DC // 2):
                a.wait_ge(tr_done, n_ + 1)
                for k in range(2):
                    c = 2 * n_ + k
                    last = A.activation(act_hi[:, c, :], pj[n_ % 4][:, k * T:(k + 1) * T], cp, scale=g_mix[:, c:c + 1])
                last.then_inc(tr_evac, 1)
                if n_ >= 4:
                    highs(n_ - 3 - BUFS)

            def evac(n_):
                kind, i, _c = BLOCKS[n_]
                highs(16 * (n_ + 1))
                a.wait_ge(row_used, 16 * (n_ + 1))
                for k in range(2):
                    src = pj[2 * (n_ % 2) + k]
                    if kind == "u":
                        last = A.activation(uT[:, 2 * k:2 * k + 2, :], v3(src[:, :], T), cp)
                    elif kind in ("sbq", "dfq"):
                        q = sq if kind == "sbq" else dq
                        last = A.activation(q[:, 4 * i + 2 * k:4 * i + 2 * k + 2, :], v3(src[:, :], T), cp, scale=QSCALE)
                    elif kind == "sbk":
                        for h in range(2):
                            rows = slice(64 * h, 64 * h + 64)
                            last = A.activation(sk[rows, 4 * k + h:4 * k + h + 3:2, :], v3(src[rows, :], T), cp)
                    elif kind == "dfk":
                        for h in range(2):
                            rows = slice(64 * h, 64 * h + 64)
                            last = A.activation(dk[rows, 4 * i + 2 * k:4 * i + 2 * k + 2, h, :], v3(src[rows, :], T), cp)
                    elif kind == "sbv":
                        last = A.activation(sv[:, k, :], src[:, :], cp)
                    else:
                        last = A.activation(dv[:, k, 512 * i:512 * i + 512], src[:, :], cp)
                last.then_inc(pj_evac, 1)

            evac(0)
            for n_ in range(8):
                k, q = n_ // 4, n_ % 4
                highs(rows_done(P_BT + n_))
                a.wait_ge(bT_done, n_ + 1)
                a.wait_ge(xnorm, 2)
                a.wait_ge(xnorm_v, 2)
                for i in range(4):
                    last = A.activation(bpad[:, k, 4 * q + i, :], at[2 + n_ % 2][:, 0:P], cp, scale=rowm[:, i:i + 1])
                last.then_inc(bT_evac, 1)
            a.wait_ge(dk_zero, 1)
            for n_ in (1, 2, 3):
                evac(n_)
            highs(rows_done(S_STEP[-1]))
            a.wait_ge(s_state, ST)
            a.dma_start(glu_w[:, :, :], w_glu.rearrange("l (c p) n -> p (l c) n", p=P)).then_inc(glu_in, 16)
            for q in range(4):
                a.wait_ge(sy_evac, q + 1)
                A.activation(uT[:, q, :], uT[:, q, :], ACT.Gelu_apprx_tanh).then_inc(gelu_s, 1)
            evac(4)
            highs(rows_done(P_GLU))
            for q in range(4):
                a.wait_ge(glu_done, 2 * (q // 2) + 2)
                A.activation(glu_s[:, q, :], at[q // 2][:, (q % 2) * T:(q % 2) * T + T], ACT.Sigmoid,
                             bias=b_gl[:, q:q + 1]).then_inc(glu_sig, 1)
            a.wait_ge(glu_y, 1)
            A.activation(nrm_sq[:, :, :], yT[:, 4:8, :], ACT.Square).then_inc(nsq, 1)
            highs(rows_done(P_SB))
            a.wait_ge(nsum, 1)
            A.activation(rstd_t, at[2][:, 0:T], ACT.Sqrt, scale=1.0 / SSW, bias=lam_s[:, 6:7]).then_inc(nrt, 1)
            for hp in range(SBH // 2):
                p = P_SB + 3 * hp
                highs(rows_done(p))
                a.wait_ge(z_done, hp + 1)
                for k in range(2):
                    A.activation(sp_a[:, k, :], at[k][:, 0:384], ACT.Abs).then_inc(z_abs, 1)
                a.wait_ge(z_abs, 6 * hp + 2)
                if hp == 0:
                    a.wait_ge(nrt, 1)
                A.activation(sp_e[:, :, :], sp_a[:, :, :], ACT.Exp, scale=-1.0).then_inc(z_abs, 2)
                a.wait_ge(z_abs, 6 * hp + 4)
                A.activation(sp_a[:, :, :], sp_e[:, :, :], ACT.Ln, bias=1.0).then_inc(z_abs, 2)
                highs(rows_done(p + 2))
                a.wait_ge(z_cum, hp + 1)
                if hp:
                    a.wait_ge(sbo_done, hp)
                for k in range(2):
                    last = A.activation(sb_w[:, k, :], at[k][:, 0:384], ACT.Exp)
                last.then_inc(z_w, 1)
                highs(rows_done(p + 3))
                a.wait_ge(sbo_done, hp + 1)
                A.activation(yT[:, hp, :], at[2][:, 0:T], cp).then_inc(sbo_evac, 1)
                if hp == 0:
                    a.wait_ge(dk_zero, 2)
                    evac(5)
            evac(6)
            a.wait_ge(ny, 1)
            a.wait_ge(sbo_evac, SBH // 2)
            A.activation(nrm_sq[:, :, :], yT[:, 0:4, :], ACT.Square).then_inc(nsq, 1)
            highs(rows_done(P_SBN))
            a.wait_ge(nsum, 2)
            A.activation(rstd_t, at[3][:, 0:T], ACT.Sqrt, scale=1.0 / SBW, bias=lam_s[:, 6:7]).then_inc(nrt, 1)
            a.wait_ge(lam_sum, 1)
            A.activation(lam_s[:, 2:4], lam_s[:, 0:2], ACT.Exp).then_inc(lam_exp, 1)

            def df_exp(h):
                a.wait_ge(d_max, h + 1)
                nm, su = dfc[:, h % 2, 0:4], dfc[:, h % 2, 4:8]
                if h:
                    a.wait_ge(d_a, h)
                for r in range(2):
                    A.activation(df_p0[:, r * P:(r + 1) * P], at[0][:, r * P:(r + 1) * P], ACT.Exp,
                                 bias=nm[:, r:r + 1], accum_out=su[:, r:r + 1])
                for r in range(2):
                    last = A.activation(df_p1[:, r * T:(r + 1) * T], at[1][:, r * T:(r + 1) * T], ACT.Exp,
                                        bias=nm[:, 2 + r:3 + r], accum_out=su[:, 2 + r:3 + r])
                last.then_inc(d_exp, 1)

            def df_copy(h):
                a.wait_ge(d_pv, h + 1)
                A.activation(yT[:, 8 + h, :], at[3][:, (h % 2) * T:(h % 2) * T + T], cp).then_inc(d_y, 1)

            def df_squares(k):
                a.wait_ge(d_y, 4 * k + 4)
                A.activation(v3(df_sq, T), yT[:, 8 + 4 * k:12 + 4 * k, :], ACT.Square).then_inc(nsq, 1)

            def df_roots(k):
                a.wait_ge(nsum, 3 + k)
                a.wait_ge(ny, 2 + k)
                for i in range(2):
                    last = A.activation(df_rt[:, 512 * i:512 * i + 512], at[i][:, :], ACT.Sqrt, scale=1.0 / P, bias=lam_s[:, 6:7])
                last.then_inc(nrt, 1)

            def y_high(k):
                if k == 0:
                    a.wait_ge(row_used, 16 * NB)
                a.wait_ge(ny, (2, 1, 3, 4)[k])
                A.activation(act_hi[:, 4 * k:4 * k + 4, :], yT[:, 4 * k:4 * k + 4, :], cp).then_inc(y_hi, 1)

            for h in range(4):
                highs(rows_done(P_DF + 3 * h))
                df_exp(h)
                highs(rows_done(P_DF + 3 * h + 3))
                df_copy(h)
                if h == 1:
                    evac(7)
            df_squares(0)
            evac(8)
            highs(rows_done(P_DFN))
            df_roots(0)
            y_high(0)
            evac(9)
            y_high(1)
            for h in range(4, DFH):
                highs(rows_out(0) + 4 * (h - 4))
                df_exp(h)
                highs(rows_out(0) + 4 * (h - 3))
                df_copy(h)
                if h == 6:
                    y_high(2)
            df_squares(1)
            highs(rows_out(2) + 2)
            df_roots(1)
            highs(rows_out(3) + 2)
            y_high(3)
            def h_squares(k):
                a.wait_ge(h_add, TB * (k + 1))
                w = slice(512 * k, 512 * k + 512)
                for b in range(TB):
                    last = A.activation(hr1[:, b, w], xt[:, b, w], ACT.Square, accum_out=fin[:, 4 * b + k:4 * b + k + 1])
                last.then_inc(h_sq, 1)

            def h_evac(n_):
                a.wait_ge(tr_done, DC // 2 + n_ + 1)
                for k in range(2):
                    c = 2 * n_ + k
                    last = A.activation(h_T[:, c, :], pj[2 + n_ % 2][:, k * T:(k + 1) * T], cp, scale=g_ffn[:, c:c + 1])
                last.then_inc(tr_evac, 1)

            highs(rows_out(5))
            h_squares(0)
            h_squares(1)
            highs(rows_out(6))
            h_squares(2)
            h_evac(0)
            h_evac(1)
            highs(rows_out(6) + 4)
            h_evac(2)
            h_evac(3)
            highs(rows_out(7))
            h_evac(4)
            h_evac(5)
            highs(rows_out(8))
            h_squares(3)
            h_evac(6)
            a.wait_ge(h_rs, 1)
            A.activation(rmsc[:, 4:6], rmsc[:, 2:4], ACT.Sqrt).then_inc(achain, 1)
            a.wait_ge(h_rs, 2)
            def h_high(u):
                if u < 2:
                    A.activation(piece(hn, u), piece(xt, u), cp, scale=rmsc[:, 10 + u % 2:11 + u % 2]).then_inc(hn_s, 1)
                A.activation(piece(hi, u), piece(xt, u), cp, scale=rmsc[:, 10 + u % 2:11 + u % 2]).then_inc(h_hi, 1)

            def h_middle(u):
                a.wait_ge(h_r1 if u < 2 else h_r1_v, u % 2 + 1)
                A.activation(piece(mid, u), piece(hr1, u), cp).then_inc(h_mid, 1)

            for u in range(4):
                h_high(u)
            for u in range(4):
                h_middle(u)
            a.wait_ge(rt_m, 1)
            A.activation(r_ex, r_xg, ACT.Exp).then_inc(rt_e, 1)
            a.wait_ge(h_r1, 2)
            a.dma_start(fg, final_g.unsqueeze(0).broadcast_to([P, D])).then_inc(fg_in, 16)

            def a_items(i_, n0, nq):
                for q in range(nq):
                    n_ = n0 + q
                    a.wait_ge(slot_free, used(n_, 2))
                    a.wait_ge(e_hT, n_ + 1)
                    A.activation(a1, psb[0][:, :], cp).then_inc(e_a1, 1)
                    a.wait_ge(e_hT, n_ + 2)
                    a.wait_ge(e_h, n_ + 1)
                    A.activation(hs, psb[2][:, 0:256], ACT.Silu).then_inc(e_silu, 1)
                    a.wait_ge(slot_free, used(n_, 6))
                    a.wait_ge(e_comb, i_ * 8 + 1)
                    for b in range(2):
                        last = A.activation(ye[64 * q:64 * q + 64, 512 * b:512 * b + 512], psb[3][64 * b:64 * b + 64, :], cp)
                    last.then_inc(e_yev, 1)

            with a.Fori(0, ITERS) as it:
                a_items(it, it * QE, QE)
            a.wait_ge(rk_ready, 2)
            extra = a.value_load(n_extra[0:1, 0:1], min_val=0, max_val=EXTRA - 1)
            with a.If(extra > 0):
                with a.Fori(0, extra) as x_:
                    a_items(x_ + ITERS, x_ + NE, 1)
            for b in range(TB):
                for c in range(4):
                    a.wait_ge(e_acc, (extra + (ITERS - 1)) * 8 + 4 * b + c + 1)
                    w = slice(512 * c, 512 * c + 512)
                    last = A.activation(junk[b][:, w], xt[:, b, w], ACT.Square, accum_out=fin[:, 4 * b + c:4 * b + c + 1])
                last.then_inc(f_sq, 1)
                a.wait_ge(f_rs, 2 * b + 1)
                A.activation(rmsc[:, 4 + b:5 + b], rmsc[:, 2 + b:3 + b], ACT.Sqrt).then_inc(f_sq, 1)

        @block.vector
        def _(v):
            V = nc.vector
            n = [0]

            def link(ins):
                n[0] += 1
                ins.then_inc(vchain, 1)
                v.wait_ge(vchain, n[0])

            MAGIC = 1.5 * 2.0 ** 23

            def exp_rows(dst, src, k, f, t, kint):
                link(V.tensor_scalar(dst, src, -87.0, 88.0, ALU.max, ALU.min))
                src = dst
                link(V.tensor_scalar(t, src, 1.0 / math.log(2.0), MAGIC, ALU.mult, ALU.add))
                link(V.tensor_scalar(k, t, MAGIC, -126.0, ALU.subtract, ALU.max))
                link(V.tensor_scalar(k, k, 127.0, None, ALU.min))
                link(V.scalar_tensor_tensor(f, k, -0.693359375, src, ALU.mult, ALU.add))
                link(V.scalar_tensor_tensor(f, k, 2.12194440054690583e-4, f, ALU.mult, ALU.add))
                link(V.tensor_scalar(t, f, 1.0 / 5040, None, ALU.mult))
                for c in (1.0 / 720, 1.0 / 120, 1.0 / 24, 1.0 / 6, 0.5, 1.0):
                    link(V.scalar_tensor_tensor(t, t, c, f, ALU.add, ALU.mult))
                link(V.tensor_scalar(kint, k, 127.0, 2.0 ** 23, ALU.add, ALU.mult))
                link(V.scalar_tensor_tensor(dst, t, 1.0, kint.bitcast(F), ALU.add, ALU.mult))

            V.memset(lam_s[:, 6:7], EPS)
            v.wait_ge(x_in[1], 16)
            half = D // 2
            V.scalar_tensor_tensor(xn[:, 1, half:], xt[:, 1, half:], 1.0, xt[:, 1, half:], ALU.mult, ALU.mult,
                                   accum_out=rmsc[:, 15:16]).then_inc(xsum, 1)
            v.wait_ge(xsum, 3)
            link(V.tensor_tensor(rmsc[:, 1:2], rmsc[:, 14:15], rmsc[:, 15:16], ALU.add))
            V.tensor_scalar(rmsc[:, 2:4], rmsc[:, 0:2], 1.0 / D, EPS, ALU.mult, ALU.add).then_inc(rstd_s, 1)
            v.wait_ge(achain, 1)
            V.reciprocal(rmsc[:, 6:8], rmsc[:, 4:6]).then_inc(rstd_s, 1)
            v.wait_ge(rstd_s, 2)
            for i in range(2):
                w = slice(half * i, half * i + half)
                V.tensor_scalar(xn[:, 1, w], xt[:, 1, w], rmsc[:, 7:8], None, ALU.mult).then_inc(xnorm_v, 1)
            v.wait_ge(lam_in, 16 * 3)
            V.tensor_copy(spar[:, 2, :].rearrange("p (h n) -> p h n", h=2),
                          dt2[:, :].unsqueeze(2).broadcast_to([ST, 2, 64])).then_inc(sp_done, 1)
            v.wait_ge(pT_done, 1)
            V.tensor_copy(pcol[:, 0:49], at[0][:, 0:49]).then_inc(pT_evac, 1)
            v.wait_ge(pT_evac, 1)
            for n_ in range(DC // 2):
                v.wait_ge(tr_evac, n_ + 1)
                for k in range(2):
                    c = 2 * n_ + k
                    last = V.scalar_tensor_tensor(act_lo[:, c, :], pj[n_ % 4][:, k * T:(k + 1) * T], g_mix[:, c:c + 1],
                                                  act_hi[:, c, :], ALU.mult, ALU.subtract)
                last.then_inc(tr_evac_v, 1)
            v.wait_ge(sT_done, 1)
            V.tensor_copy(sw[:, 0:3, :], at[1][:, 0:3 * ST].rearrange("p (k j) -> p k j", j=ST)).then_inc(sp_read, 1)
            v.wait_ge(sp_read, 1)
            R = lambda i: sw[:, i, :]
            exp_rows(R(16), R(2), R(5), R(6), R(7), ki[:, :])
            link(V.tensor_tensor(R(2), R(0), R(16), ALU.mult))
            link(V.tensor_tensor(R(3), R(1), R(16), ALU.mult))
            exp_rows(R(4), R(2), R(5), R(6), R(7), ki[:, :])
            link(V.tensor_scalar(R(5), R(3), 1.0 / (2 * math.pi), MAGIC, ALU.mult, ALU.add))
            link(V.tensor_scalar(R(5), R(5), MAGIC, None, ALU.subtract))
            c1 = 6.28125
            c2 = 1.935307179586e-3 - (1.935307179586e-3 % 2.0 ** -20)
            c3 = 2 * math.pi - c1 - c2
            link(V.scalar_tensor_tensor(R(6), R(5), -c1, R(3), ALU.mult, ALU.add))
            link(V.scalar_tensor_tensor(R(6), R(5), -c2, R(6), ALU.mult, ALU.add))
            link(V.scalar_tensor_tensor(R(6), R(5), -c3, R(6), ALU.mult, ALU.add))
            link(V.tensor_scalar(R(6), R(6), 0.5, None, ALU.mult))
            link(V.tensor_tensor(R(7), R(6), R(6), ALU.mult))
            V.tensor_scalar(R(8), R(7), 1.0 / math.factorial(13), None, ALU.mult)
            link(V.tensor_scalar(R(9), R(7), -1.0 / math.factorial(14), None, ALU.mult))
            for k in (11, 9, 7, 5, 3):
                V.scalar_tensor_tensor(R(8), R(8), (-1) ** ((k - 1) // 2) / math.factorial(k), R(7), ALU.add, ALU.mult)
                link(V.scalar_tensor_tensor(R(9), R(9), (-1) ** ((k + 1) // 2) / math.factorial(k + 1), R(7), ALU.add, ALU.mult))
            V.scalar_tensor_tensor(R(8), R(8), 1.0, R(6), ALU.add, ALU.mult)
            link(V.scalar_tensor_tensor(R(9), R(9), -0.5, R(7), ALU.add, ALU.mult))
            link(V.tensor_scalar(R(9), R(9), 1.0, None, ALU.add))
            link(V.tensor_tensor(R(10), R(8), R(8), ALU.mult))
            V.tensor_scalar(R(20), R(10), -2.0, 1.0, ALU.mult, ALU.add)
            link(V.scalar_tensor_tensor(R(21), R(8), -2.0, R(9), ALU.mult, ALU.mult))
            V.tensor_tensor(R(12), R(0), R(0), ALU.mult)
            V.tensor_tensor(R(13), R(1), R(1), ALU.mult)
            V.tensor_copy(R(19), R(4))
            V.scalar_tensor_tensor(R(11), R(4), -1.0, R(21), ALU.mult, ALU.mult)
            link(V.tensor_tensor(R(10), R(4), R(20), ALU.mult))
            V.tensor_tensor(R(12), R(12), R(13), ALU.add)
            link(V.tensor_scalar(R(10), R(10), 1.0, None, ALU.subtract))
            V.reciprocal(R(13), R(12))
            V.tensor_tensor(R(14), R(10), R(0), ALU.mult)
            V.tensor_tensor(R(15), R(11), R(1), ALU.mult)
            V.tensor_tensor(R(16), R(11), R(0), ALU.mult)
            link(V.tensor_tensor(R(17), R(10), R(1), ALU.mult))
            V.tensor_tensor(R(14), R(14), R(15), ALU.add)
            link(V.tensor_tensor(R(16), R(16), R(17), ALU.subtract))
            V.tensor_tensor(R(22), R(14), R(13), ALU.mult)
            link(V.tensor_tensor(R(23), R(16), R(13), ALU.mult))
            v.wait_ge(cT_done, 2)
            fre = scol[:, 3, :].unsqueeze(2).broadcast_to([P, ST, 32])
            fim = scol[:, 4, :].unsqueeze(2).broadcast_to([P, ST, 32])
            cr = at[0][:, :].rearrange("p (j c) -> p j c", c=32)
            ci = at[1][:, :].rearrange("p (j c) -> p j c", c=32)
            tc1 = reg_d[:, 0:512].rearrange("p (j c) -> p j c", c=32)
            tc2 = reg_d[:, 512:1024].rearrange("p (j c) -> p j c", c=32)
            for o, (f0, f1, op, sg) in enumerate(((fre, fim, ALU.subtract, 1.0), (fim, fre, ALU.add, -1.0))):
                link(V.tensor_tensor(tc1, cr, f0, ALU.mult))
                link(V.tensor_tensor(tc2, ci, f1, ALU.mult))
                link(V.tensor_tensor(tc1, tc1, tc2, op))
                for h in range(2):
                    last = V.tensor_scalar(crT[:, o, :, 16 * h:16 * h + 16], tc1[:, :, 16 * h:16 * h + 16],
                                           cmask[:, h:h + 1], sg, ALU.mult, ALU.mult)
                last.then_inc(c_ready, 1)
                v.wait_ge(c_ready, o + 1)
            v.wait_ge(k_zero, 1)
            link(V.tensor_copy(pw[:, 0:2, :], scol[:, 1:3, :]))
            w_ = 1
            while w_ < T:
                pr = pw[:, 0, :].unsqueeze(2).broadcast_to([P, ST, w_])
                pi = pw[:, 1, :].unsqueeze(2).broadcast_to([P, ST, w_])
                er, ei = ph[:, 0, :, 0:w_], ph[:, 1, :, 0:w_]
                t1 = reg_d[:, 0:2048].rearrange("p (j t) -> p j t", j=ST)[:, :, 0:w_]
                t2 = reg_d[:, 2048:4096].rearrange("p (j t) -> p j t", j=ST)[:, :, 0:w_]
                V.tensor_tensor(t1, er, pr, ALU.mult)
                link(V.tensor_tensor(t2, ei, pi, ALU.mult))
                link(V.tensor_tensor(ph[:, 0, :, w_:2 * w_], t1, t2, ALU.subtract))
                V.tensor_tensor(t1, er, pi, ALU.mult)
                link(V.tensor_tensor(t2, ei, pr, ALU.mult))
                link(V.tensor_tensor(ph[:, 1, :, w_:2 * w_], t1, t2, ALU.add))
                w_ *= 2
                if w_ < T:
                    V.tensor_tensor(pw[:, 2, :], pw[:, 0, :], pw[:, 0, :], ALU.mult)
                    link(V.tensor_tensor(pw[:, 3, :], pw[:, 1, :], pw[:, 1, :], ALU.mult))
                    link(V.scalar_tensor_tensor(pw[:, 1, :], pw[:, 0, :], 2.0, pw[:, 1, :], ALU.mult, ALU.mult))
                    link(V.tensor_tensor(pw[:, 0, :], pw[:, 2, :], pw[:, 3, :], ALU.subtract))

            def ph_b(k, j):
                return ph[:, k, j, :].unsqueeze(1).broadcast_to([P, 2, T])

            def s_tile(j):
                v.wait_ge(bu_done, j + 1)
                bu, ab, vv, df, st = v3(at[j % 2][:, :], T), s_ab[j % 2], s_v[j % 2], s_df[j % 2], s_s[j % 2]
                V.tensor_tensor(ab[:, 0, :, :], bu, ph_b(0, j), ALU.mult)
                V.tensor_tensor(ab[:, 1, :, :], bu, ph_b(1, j), ALU.mult).then_inc(s_prod, 1)
                v.wait_ge(s_prod, j + 1)
                V.tensor_tensor(vv[:, 0, :], ab[:, 0, 0, :], ab[:, 1, 1, :], ALU.subtract)
                V.tensor_tensor(vv[:, 1, :], ab[:, 0, 1, :], ab[:, 1, 0, :], ALU.add).then_inc(s_rot, 1)
                v.wait_ge(s_rot, j + 1)
                rr = scol[:, 0, j:j + 1].broadcast_to([P, T])
                for k in range(2):
                    last = V.tensor_tensor_scan(s_w[:, k, :], rr, vv[:, k, :], 0.0, ALU.mult, ALU.add)
                last.then_inc(s_scan, 1)
                v.wait_ge(s_scan, j + 1)
                V.tensor_tensor(df[:, 0, :, :], s_w[:, :, :], ph_b(0, j), ALU.mult)
                V.tensor_tensor(df[:, 1, :, :], s_w[:, :, :], ph_b(1, j), ALU.mult).then_inc(s_out, 1)
                v.wait_ge(s_out, j + 1)
                if j >= 2:
                    v.wait_ge(sy_used, j - 1)
                V.tensor_tensor(st[:, 0, :], df[:, 0, 0, :], df[:, 1, 1, :], ALU.add)
                V.tensor_tensor(st[:, 1, :], df[:, 0, 1, :], df[:, 1, 0, :], ALU.subtract).then_inc(s_state, 1)

            def s_skip(q):
                v.wait_ge(sy_used, 4 * q + 4)
                V.scalar_tensor_tensor(uT[:, q, :], uT[:, q, :], d_sk[:, q:q + 1], at[2 + q % 2][:, 0:T],
                                       ALU.mult, ALU.add).then_inc(sy_evac, 1)

            for j in range(ST):
                s_tile(j)
                if j >= 7 and j % 4 == 3:
                    s_skip(j // 4 - 1)
            s_skip(3)
            for q in range(4):
                v.wait_ge(glu_sig, q + 1)
            last = V.tensor_tensor(uT[:, :, :], uT[:, :, :], glu_s[:, :, :], ALU.mult)
            last.then_inc(glu_y, 1)

            def norm_four(n_, first, gain):
                v.wait_ge(nrt, n_)
                link(V.reciprocal(rstd_t, rstd_t))
                for q in range(4):
                    last = V.scalar_tensor_tensor(yT[:, first + q, :], yT[:, first + q, :], gain[:, q:q + 1], rstd_t,
                                                  ALU.mult, ALU.mult)
                last.then_inc(ny, 1)
            norm_four(1, 4, g_ssm)
            v.wait_ge(lq_in, 16 * 4)
            for i in range(2):
                link(V.tensor_tensor(lamv[:, 2 * i, :], lamv[:, 2 * i, :], lamv[:, 2 * i + 1, :], ALU.mult))
                last = V.reduce_sum(lam_s[:, i:i + 1], lamv[:, 2 * i, :], axis=AX)
            last.then_inc(lam_sum, 1)
            for hp in range(SBH // 2):
                v.wait_ge(z_abs, 6 * hp + 6)
                if hp:
                    v.wait_ge(z_cum, hp)
                for k in range(2):
                    last = V.scalar_tensor_tensor(sp_t[:, k, :], at[k][:, 0:384], 0.0, sp_a[:, k, :], ALU.max, ALU.add)
                last.then_inc(z_sp, 1)
            norm_four(2, 0, g_sb)
            v.wait_ge(lam_exp, 1)
            link(V.tensor_tensor(lam_s[:, 4:5], lam_s[:, 2:3], lam_s[:, 3:4], ALU.subtract))
            link(V.tensor_scalar(lam_s[:, 5:6], lam_s[:, 4:5], LAM_INIT, None, ALU.add))
            link(V.tensor_scalar(g_df, g_df, 1.0 - LAM_INIT, None, ALU.mult))

            def df_max(h):
                v.wait_ge(d_sc, h + 1)
                if h >= 2:
                    v.wait_ge(d_a, h - 1)
                mx = dfc[:, h % 2, 8:12]
                V.reduce_max(mx[:, 0:2], at[0][:, 0:2 * P].rearrange("p (r k) -> p r k", r=2), axis=AX)
                link(V.reduce_max(mx[:, 2:4], at[1][:, :].rearrange("p (r k) -> p r k", r=2), axis=AX))
                V.tensor_scalar(dfc[:, h % 2, 0:4], mx, -1.0, None, ALU.mult).then_inc(d_max, 1)

            def df_norm(h, n_):
                w = slice(T * (h % 4), T * (h % 4 + n_))
                link(V.reciprocal(df_rt[:, w], df_rt[:, w]))
                y_ = yT[:, 8 + h:8 + h + n_, :]
                return V.scalar_tensor_tensor(y_, y_, g_df, v3(df_rt[:, w], T), ALU.mult, ALU.mult)

            def df_diff(h):
                v.wait_ge(d_exp, h + 1)
                ri = dfc[:, h % 2, 12:16]
                link(V.reciprocal(ri, dfc[:, h % 2, 4:8]))
                link(V.tensor_scalar(ri[:, 1:4:2], ri[:, 1:4:2], lam_s[:, 5:6], None, ALU.mult))
                V.tensor_scalar(df_t[:, 0:P], df_p0[:, P:2 * P], ri[:, 1:2], None, ALU.mult)
                link(V.tensor_scalar(df_t[:, P:3 * P], df_p1[:, T:2 * T], ri[:, 3:4], None, ALU.mult))
                if h:
                    v.wait_ge(d_tr, h)
                V.scalar_tensor_tensor(df_a[:, 0:P], df_p0[:, 0:P], ri[:, 0:1], df_t[:, 0:P], ALU.mult, ALU.subtract)
                V.scalar_tensor_tensor(df_a[:, P:3 * P], df_p1[:, 0:T], ri[:, 2:3], df_t[:, P:3 * P],
                                       ALU.mult, ALU.subtract).then_inc(d_a, 1)
                if h == 4:
                    v.wait_ge(nrt, 3)
                    df_norm(0, 2)
                if h == 5:
                    df_norm(2, 2).then_inc(ny, 1)
                v.wait_ge(d_tr, h + 1)
                if h:
                    v.wait_ge(d_pv, h)
                V.tensor_copy(df_aT, at[2][:, 0:384]).then_inc(d_aT, 1)

            def y_low(k):
                v.wait_ge(y_hi, k + 1)
                w = slice(4 * k, 4 * k + 4)
                V.tensor_tensor(act_lo[:, w, :], yT[:, w, :], act_hi[:, w, :], ALU.subtract).then_inc(y_lo, 1)

            for h in range(4):
                df_max(h)
                df_diff(h)
            y_low(0)
            for h in range(4, DFH):
                df_max(h)
                if h == 4:
                    y_low(1)
                df_diff(h)
                if h == 6:
                    y_low(2)
            v.wait_ge(nrt, 4)
            df_norm(4, 4).then_inc(ny, 1)
            y_low(3)
            v.wait_ge(x2_in, 16 * TB)
            for k in range(4):
                v.wait_ge(row_used, rows_out((5, 5, 6, 8)[k]))
                for b in range(TB):
                    w = slice(512 * k, 512 * k + 512)
                    V.tensor_tensor(xt[:, b, w], out_bank(k, b)[:, :], xt[:, b, w], ALU.add).then_inc(h_add, 1)
            v.wait_ge(tr_done, DC)
            for k in range(2):
                c = DC - 2 + k
                last = V.tensor_scalar(h_T[:, c, :], pj[3][:, k * T:(k + 1) * T], g_ffn[:, c:c + 1], None, ALU.mult)
            last.then_inc(tr_evac, 1)
            v.wait_ge(h_sq, 4)
            link(V.reduce_sum(rmsc[:, 8:10], v3(fin, 4), axis=AX))
            V.tensor_scalar(rmsc[:, 2:4], rmsc[:, 8:10], 1.0 / D, EPS, ALU.mult, ALU.add).then_inc(h_rs, 1)
            link(V.tensor_scalar(r_desc, iota_s[:, 0:EPG], -1.0, float(EPG), ALU.mult, ALU.add))
            v.wait_ge(achain, 2)
            V.reciprocal(rmsc[:, 10:12], rmsc[:, 4:6]).then_inc(h_rs, 1)
            v.wait_ge(h_rs, 2)
            v.wait_ge(rt_done, 1)
            v.wait_ge(rw_in, 16 * 7)
            for b in range(TB):
                last = V.scalar_tensor_tensor(lg[:, b, :], at[0][:, 36 * b:36 * b + 36], rmsc[:, 10 + b:11 + b], rbias[:, :],
                                              ALU.mult, ALU.add)
            link(last)

            def along(ap, w):
                return ap.broadcast_to([P, TB, w])

            def first_hit(dst, src, mx, w):
                link(V.reduce_max(mx, src, axis=AX))
                link(V.tensor_tensor(r_tp[:, :, 0:w], src, along(mx, w), ALU.is_ge))
                link(V.tensor_tensor(r_tp[:, :, 0:w], r_tp[:, :, 0:w], r_desc[:, 0:w].unsqueeze(1).broadcast_to([P, TB, w]), ALU.mult))
                link(V.reduce_max(r_mx, r_tp[:, :, 0:w], axis=AX))
                link(V.tensor_tensor(dst, r_tp[:, :, 0:w], along(r_mx, w), ALU.is_equal))

            o4 = [P, TB, NG, EPG]
            g4 = r_goh.unsqueeze(3).broadcast_to(o4)

            def by_group(ap):
                return ap.unsqueeze(2).broadcast_to(o4)

            first_hit(r_goh, lg[:, :, 0:NG], r_gm, NG)
            V.tensor_tensor(r_xg[:, :, 0:NG], lg[:, :, 0:NG], along(r_gm, NG), ALU.subtract)
            link(V.tensor_tensor(r_big, lg[:, :, NG:].rearrange("p b (k e) -> p b k e", e=EPG), g4, ALU.mult))
            link(V.reduce_sum(r_el, r_big.rearrange("p b k e -> p b e k"), axis=AX))
            first_hit(r_e1, r_el, r_m1, EPG)
            link(V.scalar_tensor_tensor(r_el, r_e1, NEG, r_el, ALU.mult, ALU.add))
            first_hit(r_e2, r_el, r_m2, EPG)
            V.tensor_tensor(r_xg[:, :, NG:NG + 1], r_m2, r_m1, ALU.subtract).then_inc(rt_m, 1)
            link(V.tensor_tensor(r_s8, r_e1, r_e2, ALU.add))
            sel4, gat4, selb4 = (t.rearrange("p b (k e) -> p b k e", e=EPG) for t in (sel, gat, selb))
            V.tensor_tensor(selb4, by_group(r_s8), g4, ALU.mult).then_inc(rt_sel, 1)
            link(V.tensor_tensor(sel4, by_group(r_s8), g4, ALU.mult))
            v.wait_ge(rk_done, 1)
            rk = at[1][:, 0:2 * NE].rearrange("p (b e) -> p b e", e=NE)
            V.tensor_copy(x_cnt, at[2][:, 0:NE])
            link(V.scalar_tensor_tensor(pos, rk, 1.0, sel[:, :, :], ALU.add, ALU.mult))
            V.tensor_scalar(pos, pos, 1.0, None, ALU.subtract).then_inc(rk_ready, 1)
            v.wait_ge(rk_ready, 1)

            def extra_items():
                link(V.tensor_scalar(x_n, x_cnt, float(SLOT), None, ALU.is_gt))
                for k in range(2, PASSES):
                    link(V.scalar_tensor_tensor(x_n, x_cnt, float(SLOT * k), x_n, ALU.is_gt, ALU.add))
                link(V.tensor_tensor_scan(x_e, ones[:, 0:NE], x_n, 0.0, ALU.mult, ALU.add))
                link(V.tensor_tensor(x_c, x_e, x_n, ALU.subtract))
                V.tensor_copy(n_extra, x_e[:, NE - 1:NE])
                o8, o9 = [P, EXTRA, NE], [P, TB, EXTRA, NE]
                c8, e8 = x_c.unsqueeze(1).broadcast_to(o8), x_e.unsqueeze(1).broadcast_to(o8)
                i8 = iota_s[:, 0:EXTRA].unsqueeze(2).broadcast_to(o8)
                V.tensor_tensor(x_in_e, i8, c8, ALU.is_ge)
                link(V.tensor_tensor(x_t[:, 1], i8, e8, ALU.is_lt))
                link(V.tensor_tensor(x_in_e, x_in_e, x_t[:, 1], ALU.mult))
                link(V.tensor_tensor(x_t[:, 0], x_in_e, iota_s[:, 0:NE].unsqueeze(1).broadcast_to(o8), ALU.mult))
                link(V.reduce_sum(x_id, x_t[:, 0], axis=AX))
                V.tensor_copy(ids, x_id)
                link(V.tensor_scalar(x_c, x_c, 1.0, float(SLOT), ALU.subtract, ALU.mult))
                link(V.tensor_tensor(x_q[:, :, :], pos, x_c.unsqueeze(1).broadcast_to([P, TB, NE]), ALU.add))
                x9 = x_in_e.unsqueeze(1).broadcast_to(o9)
                link(V.tensor_tensor(x_t, x9, x_q.unsqueeze(2).broadcast_to(o9), ALU.mult))
                link(V.reduce_sum(posx[:, :, NE:], x_t, axis=AX))
                V.scalar_tensor_tensor(posx[:, :, NE:], iota_s[:, 0:EXTRA].unsqueeze(1).broadcast_to([P, TB, EXTRA]), -float(SLOT),
                                       posx[:, :, NE:], ALU.mult, ALU.add)
                link(V.tensor_tensor(x_t, x9, gat.unsqueeze(2).broadcast_to(o9), ALU.mult))
                V.reduce_sum(gatx[:, :, NE:], x_t, axis=AX).then_inc(rk_ready, 1)
                v.wait_ge(rk_ready, 2)

            v.sem_inc(e_h, 1)
            gfb = g_ffn.unsqueeze(2).broadcast_to([P, DC, P])

            def select_slots(i_, n0, nq):
                ob3 = [P, nq, SLOT]
                for b in range(TB):
                    at_s = posx[:, b, ds(n0, nq)].unsqueeze(2).broadcast_to(ob3)
                    last = V.tensor_tensor(selS[:, b, 0:nq, :], at_s, iota_s[:, :].unsqueeze(1).broadcast_to(ob3), ALU.is_equal)
                last.then_inc(e_sel, 1)

            def select_weights(i_, n0, nq):
                ob3 = [P, nq, SLOT]
                v.wait_ge(e_sel, i_ + 1)
                for b in range(TB):
                    w = gatx[:, b, ds(n0, nq)].unsqueeze(2).broadcast_to(ob3)
                    last = V.tensor_tensor(selW[:, b, 0:nq, :], selS[:, b, 0:nq, :], w, ALU.mult)
                last.then_inc(e_selw, 1)

            select_slots(0, 0, QE)
            def h_low(u):
                v.wait_ge(h_mid, u + 1)
                V.tensor_tensor(piece(lo, u), piece(hr1, u), piece(mid, u), ALU.subtract).then_inc(h_lo_v, 1)

            def h_rest(u):
                v.wait_ge(h_hi, u + 1)
                V.scalar_tensor_tensor(piece(hr1, u), piece(xt, u), rmsc[:, 10 + u % 2:11 + u % 2], piece(hi, u),
                                       ALU.mult, ALU.subtract).then_inc(h_r1_v, 1)

            h_rest(2)
            h_low(0)
            h_rest(3)
            h_low(2)

            def gates():
                v.wait_ge(rt_e, 1)
                ex2 = r_ex[:, :, NG:NG + 1]
                link(V.reduce_sum(r_gs, r_ex[:, :, 0:NG], axis=AX))
                link(V.scalar_tensor_tensor(r_dn, ex2, 1.0, r_gs, ALU.add, ALU.mult))
                link(V.reciprocal(r_w1, r_dn))
                link(V.tensor_tensor(r_w2, r_w1, ex2, ALU.mult))
                V.tensor_tensor(r_g8, r_e1, along(r_w1, EPG), ALU.mult)
                link(V.tensor_tensor(r_t8, r_e2, along(r_w2, EPG), ALU.mult))
                link(V.tensor_tensor(r_g8, r_g8, r_t8, ALU.add))
                link(V.tensor_tensor(gat4, by_group(r_g8), g4, ALU.mult))


            def v_items(i_, n0, nq, first=False):
                ns = nq * SLOT
                for k in range(4):
                    v.wait_ge(e_gath, i_ * 4 + k + 1)
                    V.tensor_tensor(xeT[:, 4 * k:4 * k + 4, 0:ns], v3(psb[4 + k % 2][:, :], P)[:, :, 0:ns],
                                    gfb[:, 4 * k:4 * k + 4, 0:ns], ALU.mult).then_inc(e_gev, 1)
                if first:
                    gates()
                    select_weights(0, 0, QE)
                    extra_items()
                for q in range(nq):
                    n_ = n0 + q
                    v.wait_ge(slot_free, used(n_, 4))
                    v.wait_ge(e_hT, n_ + 1)
                    V.tensor_copy(a3, psb[1][:, :]).then_inc(e_a3, 1)
                    v.wait_ge(e_silu, n_ + 1)
                    V.tensor_tensor(hT[:, :, :], v3(psb[2][:, 256:512], SLOT), v3(hs, SLOT), ALU.mult).then_inc(e_h, 1)
                    if q == 0:
                        v.wait_ge(e_gt, i_ + 1)
                        V.tensor_copy(gT[0:ns, :], psb[6][0:ns, 0:256]).then_inc(e_gtev, 1)
                        select_slots(i_ + 1, n0 + nq, nq)
                        select_weights(i_ + 1, n0 + nq, nq)
                    v.wait_ge(slot_free, used(n_, 6))
                    v.wait_ge(e_comb, i_ * 8 + 1)
                    for b in range(2):
                        last = V.tensor_copy(ye[64 * q:64 * q + 64, 1024 + 512 * b:1536 + 512 * b],
                                             psb[4][64 * b:64 * b + 64, :])
                    last.then_inc(e_yev, 1)
                for k in range(8):
                    b, c = k // 4, k % 4
                    v.wait_ge(e_comb, i_ * 8 + k + 2)
                    w = slice(512 * c, 512 * c + 512)
                    V.tensor_tensor(xt[:, b, w], psb[6 + k % 2][:, :], xt[:, b, w], ALU.add).then_inc(e_acc, 1)

            v_items(0, 0, QE, first=True)
            with v.Fori(1, ITERS) as it:
                v_items(it, it * QE, QE)
            extra = v.value_load(n_extra[0:1, 0:1], min_val=0, max_val=EXTRA - 1)
            v.wait_ge(e_comb, ITERS * 8 + 1)
            V.memset(gT[SLOT:, :], 0.0)
            with v.If(extra > 0):
                with v.Fori(0, extra) as x_:
                    v_items(x_ + ITERS, x_ + NE, 1)
            v.wait_ge(fg_in, 16)
            for b in range(TB):
                v.wait_ge(f_sq, 2 * b + 1)
                link(V.reduce_sum(rmsc[:, 12 + b:13 + b], fin[:, 4 * b:4 * b + 4], axis=AX))
                V.tensor_scalar(rmsc[:, 2 + b:3 + b], rmsc[:, 12 + b:13 + b], 1.0 / D, EPS, ALU.mult, ALU.add).then_inc(f_rs, 1)
                v.wait_ge(f_sq, 2 * b + 2)
                V.reciprocal(rmsc[:, 6 + b:7 + b], rmsc[:, 4 + b:5 + b]).then_inc(f_rs, 1)
                v.wait_ge(f_rs, 2 * b + 2)
                for k in range(2):
                    w = slice(D // 2 * k, D // 2 * k + D // 2)
                    V.scalar_tensor_tensor(xt[:, b, w], xt[:, b, w], rmsc[:, 6 + b:7 + b], fg[:, w], ALU.mult, ALU.mult).then_inc(f_out, 1)

        @block.tensor
        def _(pe):
            M = nc.tensor.matmul
            TR = nc.tensor.transpose
            pe.wait_ge(cst, 1)
            for m in range(DC // 2):
                if m % 4 == 0:
                    pe.wait_ge(xnorm, m // 4 + 1)
                    pe.wait_ge(xnorm_v, m // 4 + 1)
                if m >= 4:
                    pe.wait_ge(tr_evac_v, m - 3)
                for k2 in range(2):
                    for b in range(TB):
                        c = 2 * m + k2
                        last = TR(pj[m % 4][:, k2 * T + b * P:k2 * T + b * P + P], xn[:, b, c * P:(c + 1) * P], ident[:, :])
                last.then_inc(tr_done, 1)
                if m == 1:
                    pe.wait_ge(par_in, 16 * 7)
                    for i in range(3):
                        TR(at[0][:, 16 * i:16 * i + 16], prow[:, i, :], ident[0:16, 0:16])
                    TR(at[0][:, 48:49], prow[0:1, 3, :], ident[0:1, 0:1]).then_inc(pT_done, 1)
                if m == 3:
                    pe.wait_ge(sp_done, 1)
                    for i in range(3):
                        last = TR(at[1][:, 16 * i:16 * i + 16], spar[:, i, :], ident[0:16, 0:16])
                    last.then_inc(sT_done, 1)
            pe.wait_ge(cst, 2)

            def b_transpose(n_):
                if n_ == 0:
                    pe.wait_ge(b_in, 16 * 4)
                if n_ >= 2:
                    pe.wait_ge(bT_evac, n_ - 1)
                k, q = n_ // 4, n_ % 4
                TR(at[2 + n_ % 2][:, 0:P], bnat[:, k, 4 * q:4 * q + 4, :].rearrange("p a c -> p (a c)"), ident[:, :]).then_inc(bT_done, 1)

            def c_transpose(k):
                if k == 0:
                    pe.wait_ge(c_in, 16 * 4)
                    pe.wait_ge(pT_evac, 1)
                    pe.wait_ge(sp_read, 1)
                for q in range(4):
                    last = TR(at[k][:, P * q:P * q + P], (cnat, cnat2)[k][:, q, :, :].rearrange("p d n -> p (d n)"), ident[:, :])
                last.then_inc(cT_done, 1)

            row = [0]

            def products(out, lhs, rhs, first, last_):
                for i, (p, q) in enumerate(((0, 0), (0, 1), (1, 0))):
                    last = M(out, lhs[p], rhs[q], start=first and i == 0, stop=last_ and i == 2, skip_group_check=True)
                return last

            def next_row():
                i = row[0]
                row[0] += 1
                pe.wait_ge(row_lo, i + 1)
                return w_hi[:, i % BUFS, :], w_lo[:, i % BUFS, :]

            def project(part):
                n_ = part // 8
                kind = BLOCKS[n_][0]
                if part % 8 == 0:
                    if n_ >= 2:
                        pe.wait_ge(pj_evac, n_ - 1)
                    elif n_ == 0:
                        pe.wait_ge(tr_evac_v, DC // 2 - 2)
                banks = pj[2 * (n_ % 2):2 * (n_ % 2) + 2]
                for cc in (2 * (part % 8), 2 * (part % 8) + 1):
                    w = next_row()
                    if n_ == 0:
                        pe.wait_ge(tr_evac_v, cc // 2 + 1)
                    x_ = act_hi[:, cc, :], act_lo[:, cc, :]
                    if kind in ("sbv", "dfv"):
                        for b in range(TB):
                            last = products(banks[b][:, :], [t[:, b * P:(b + 1) * P] for t in x_], w, cc == 0, cc == DC - 1)
                    else:
                        for ct in range(4):
                            last = products(banks[ct // 2][:, (ct % 2) * T:(ct % 2) * T + T], [t[:, ct * P:(ct + 1) * P] for t in w], x_,
                                            cc == 0 and ct % 2 == 0, cc == DC - 1)
                    last.then_inc(row_used, 1)

            def s_in(j):
                if j == 0:
                    pe.wait_ge(bT_evac, 8)
                    pe.wait_ge(pj_evac, 1)
                    pe.wait_ge(c_ready, 2)
                if j >= 2:
                    pe.wait_ge(s_prod, j - 1)
                for k in range(2):
                    last = M(at[j % 2][:, k * T:(k + 1) * T], bpad[:, k, j, :], uT[:, j // 4, :], start=True, stop=True)
                last.then_inc(bu_done, 1)

            def s_y(j):
                pe.wait_ge(s_state, j + 1)
                q, i = j // 4, j % 4
                if q >= 2 and i == 0:
                    pe.wait_ge(sy_evac, q - 1)
                o = at[2 + q % 2][32 * i:32 * i + 32, 0:T]
                M(o, crT[:, 0, j, :], s_s[j % 2][:, 0, :], start=True, stop=False)
                last = M(o, crT[:, 1, j, :], s_s[j % 2][:, 1, :], start=False, stop=True)
                last.then_inc(sy_used, 1)

            def glu():
                pe.wait_ge(glu_in, 16)
                pe.wait_ge(gelu_s, 4)
                for co in range(4):
                    for c in range(4):
                        last = M(at[co // 2][:, (co % 2) * T:(co % 2) * T + T], glu_w[:, c, co * P:(co + 1) * P], uT[:, c, :],
                                 start=c == 0, stop=c == 3)
                    last.then_inc(glu_done, 1)

            def sums4(n_, bank):
                pe.wait_ge(nsq, n_)
                for q in range(4):
                    last = M(bank[:, 0:T], ones[:, :], nrm_sq[:, q, :], start=q == 0, stop=q == 3)
                last.then_inc(nsum, 1)

            def sb_scores(hp):
                if hp == 0:
                    pe.wait_ge(pj_evac, 4)
                    pe.wait_ge(glu_sig, 4)
                else:
                    pe.wait_ge(z_w, hp)
                for k in range(2):
                    h = 2 * hp + k
                    z = at[k]
                    M(z[:, 0:T], sk[:, h, 0:P], sq[:, hp, :], start=True, stop=True, skip_group_check=True)
                    M(z[:, T:T + P], sk[:, h, P:T], sq[:, hp, P:T], start=False, stop=True, skip_group_check=True)
                    M(z[:, 0:P], ident_b[:, :], smask_b[:, :], start=False, stop=True, skip_group_check=True)
                    last = M(z[:, T:T + P], ident_b[:, :], smask_b[:, :], start=False, stop=True, skip_group_check=True)
                last.then_inc(z_done, 1)

            def sb_cum(hp):
                pe.wait_ge(z_sp, hp + 1)
                for k in range(2):
                    z = at[k]
                    M(z[:, 0:T], tri_neg[:, :], sp_t[:, k, 0:T], start=False, stop=True, skip_group_check=True)
                    M(z[:, P:T], ones_neg[:, :], sp_t[:, k, T:T + P], start=False, stop=True, skip_group_check=True)
                    last = M(z[:, T:T + P], tri_neg[:, :], sp_t[:, k, T:T + P], start=False, stop=True, skip_group_check=True)
                last.then_inc(z_cum, 1)

            def sb_out(hp):
                pe.wait_ge(z_w, hp + 1)
                if hp:
                    pe.wait_ge(sbo_evac, hp)
                else:
                    pe.wait_ge(nrt, 1)
                for k in range(2):
                    h = 2 * hp + k
                    o = at[2][64 * k:64 * k + 64, :]
                    M(o[:, 0:T], sv[:, 0, 64 * h:64 * h + 64], sb_w[:, k, 0:T], start=True, stop=True)
                    last = M(o[:, P:T], sv[:, 1, 64 * h:64 * h + 64], sb_w[:, k, T:T + P], start=False, stop=True, skip_group_check=True)
                last.then_inc(sbo_done, 1)

            def df_scores(h):
                if h == 0:
                    pe.wait_ge(pj_evac, 7)
                    pe.wait_ge(nrt, 2)
                if h == 4:
                    pe.wait_ge(pj_evac, NB - 1)
                    pe.wait_ge(nrt, 3)
                if h:
                    pe.wait_ge(d_exp, h)
                M(at[0][:, 0:2 * P], dq[:, h, 0:P], dk[:, h, :, 0:P], start=True, stop=False)
                M(at[0][:, 0:2 * P], ident_b[:, :], mask_b[:, :, :], start=False, stop=True)
                M(at[1][:, :], dq[:, h, P:T], dk[:, h, :, :], start=True, stop=True)
                M(at[1][:, :].rearrange("p (r k) -> p r k", r=2)[:, :, P:T], ident_b[:, :], mask_b[:, :, :],
                  start=False, stop=True, skip_group_check=True).then_inc(d_sc, 1)

            def df_tr(h):
                pe.wait_ge(d_a, h + 1)
                if h:
                    pe.wait_ge(d_aT, h)
                for k in range(3):
                    last = TR(at[2][:, k * P:(k + 1) * P], df_a[:, k * P:(k + 1) * P], ident[:, :])
                last.then_inc(d_tr, 1)

            def df_out(h):
                pe.wait_ge(d_aT, h + 1)
                if h == 4:
                    pe.wait_ge(pj_evac, NB)
                if h:
                    pe.wait_ge(d_y, h)
                o = at[3][:, (h % 2) * T:(h % 2) * T + T]
                M(o, dv[:, 0, h * P:(h + 1) * P], df_aT[:, 0:T], start=True, stop=True)
                M(o[:, P:T], dv[:, 1, h * P:(h + 1) * P], df_aT[:, T:T + P], start=False, stop=True,
                  skip_group_check=True).then_inc(d_pv, 1)

            def df_sums(k):
                pe.wait_ge(nsq, 3 + k)
                pe.wait_ge(d_exp, 4 * k + 4)
                for i in range(2):
                    last = M(at[i][:, :], ones[:, :], df_sq[:, 512 * i:512 * i + 512], start=True, stop=True)
                last.then_inc(nsum, 1)

            steps = [[] for _i in range(8 * NB)]
            for k in range(2):
                steps[3 + k].append((c_transpose, k))
            for k in range(8):
                steps[P_BT + k].append((b_transpose, k))
            for k in range(ST + 2):
                if k < ST:
                    steps[S_STEP[k]].append((s_in, k))
                if k >= 2:
                    steps[S_STEP[k]].append((s_y, k - 2))
            steps[P_GLU].append((glu,))
            steps[P_SB].append((sums4, 1, at[2]))
            for hp in range(SBH // 2):
                p = P_SB + 3 * hp
                steps[p].append((sb_scores, hp))
                steps[p + 2].append((sb_cum, hp))
                steps[p + 3].append((sb_out, hp))
            steps[P_SBN].append((sums4, 2, at[3]))
            for h in range(4):
                p = P_DF + 3 * h
                steps[p].append((df_scores, h))
                steps[p + 2].append((df_tr, h))
                steps[p + 3].append((df_out, h))
            steps[P_DFN].append((df_sums, 0))
            for part in range(8 * NB):
                project(part)
                for f, *args in steps[part]:
                    f(*args)

            def out_rows(n_, which=range(8)):
                for i in which:
                    cc, o = OUT_UNITS[n_][i]
                    if cc == 0:
                        pe.wait_ge(*((pj_evac, NB - 1), (pj_evac, NB), (d_y, DFH), (h_add, 2))[o])
                    w = next_row()
                    pe.wait_ge(y_lo, cc // 4 + 1)
                    if n_ >= len(OUT_UNITS) - SLOTS_A and i == 7:
                        pe.sem_inc(slot_free, 1)
                    for b in range(TB):
                        last = products(out_bank(o, b)[:, :], [t[:, cc, b * P:(b + 1) * P] for t in (act_hi, act_lo)], w,
                                        cc == 0, cc == DC - 1)
                    last.then_inc(row_used, 1)

            df_scores(4)
            for h in range(4, DFH):
                out_rows((h - 4) // 2, range(4 * (h % 2), 4 * (h % 2) + 4))
                df_tr(h)
                if h + 1 < DFH:
                    df_scores(h + 1)
                df_out(h)
            out_rows(2, range(0, 2))
            df_sums(1)
            out_rows(2, range(2, 8))
            out_rows(3)
            pe.wait_ge(ny, 4)
            pe.sem_inc(slot_free, 2)

            def h_transpose(k):
                pe.wait_ge(h_add, TB * (k + 1))
                for m in (2 * k, 2 * k + 1):
                    if m >= 2:
                        pe.wait_ge(tr_evac, DC // 2 + m - 1)
                    for k2 in range(2):
                        for b in range(TB):
                            c = 2 * m + k2
                            last = TR(pj[2 + m % 2][:, k2 * T + b * P:k2 * T + b * P + P], xt[:, b, c * P:(c + 1) * P], ident[:, :])
                    last.then_inc(tr_done, 1)

            def h_logits(k):
                pe.wait_ge(tr_evac, DC // 2 + 2 * k + 2)
                if k == 0:
                    pe.wait_ge(rw_in, 16 * 7)
                for c in range(4 * k, 4 * k + 4):
                    for b in range(TB):
                        last = M(at[0][:, 36 * b:36 * b + 36], h_T[:, c, b * P:(b + 1) * P], rw[:, c, :],
                                 start=c == 0 and b == 0, stop=c == DC - 1, skip_group_check=True)
                if k == 3:
                    last.then_inc(rt_done, 1)

            out_rows(4)
            out_rows(5)
            h_transpose(0)
            out_rows(6, range(0, 4))
            h_transpose(1)
            h_logits(0)
            out_rows(6, range(4, 8))
            h_transpose(2)
            h_logits(1)
            out_rows(7)
            pe.wait_ge(row_used, ROWS)
            pe.sem_inc(slot_free, 2)
            h_logits(2)
            h_transpose(3)
            h_logits(3)
            pe.wait_ge(rt_sel, 1)
            M(at[1][:, 0:NE], before_b[:, :], selb[:, 0, :], start=True, stop=True)
            M(at[1][:, NE:2 * NE], before_b[:, :], selb[:, 1, :], start=True, stop=False)
            M(at[1][:, NE:2 * NE], ones_b[:, :], selb[:, 0, :], start=False, stop=True)
            M(at[2][:, 0:NE], ones_b[:, :], selb[:, 0, :], start=True, stop=False)
            M(at[2][:, 0:NE], ones_b[:, :], selb[:, 1, :], start=False, stop=True).then_inc(rk_done, 1)
            pe.sem_inc(e_hT, 1)
            pe.sem_inc(e_comb, 1)
            pe.sem_inc(e_yev, 1)

            def landed(n_, k):
                s = slot_of(k)
                base = 16 * (UNITS_A // SLOTS_A) if s < SLOTS_A else 0
                pe.wait_ge(ring_in[s], n_ * 16 + base + 16)
                return s

            def pe_items(i_, n0, nq):
                ns = nq * SLOT
                pe.wait_ge(e_sel, i_ + 1)
                for c in range(DC):
                    if c % 8 == 0:
                        pe.wait_ge(h_lo, c // 8 + 1)
                        pe.wait_ge(h_lo_v, c // 8 + 1)
                    if c % 4 == 0 and c >= 8:
                        pe.wait_ge(e_gev, i_ * 4 + c // 4 - 1)
                    k = 0
                    for part in (hi, mid, lo):
                        for b in range(TB):
                            last = M(psb[4 + (c // 4) % 2][:, (c % 4) * P:(c % 4) * P + ns], part[:, b, c * P:(c + 1) * P],
                                     selS[:, b, 0:nq, :].rearrange("p q s -> p (q s)"), start=k == 0, stop=k == 5)
                            k += 1
                    if c % 4 == 3:
                        last.then_inc(e_gath, 1)
                pe.wait_ge(e_gev, i_ * 4 + 4)
                for q in range(nq):
                    n_ = n0 + q
                    for m in range(2):
                        for half in range(2):
                            s = landed(n_, 2 * m + half)
                            for c in range(8):
                                cc = 8 * half + c
                                i = c % 2
                                last = M(psb[m][64 * i:64 * i + 64, :], xeT[:, cc, 64 * q:64 * q + 64], unit(s)[:, c, :],
                                         start=cc < 2, stop=cc >= DC - 2)
                            last.then_inc(slot_free, 1)
                    for m, (ready, src) in enumerate(((e_a1, a1), (e_a3, a3))):
                        pe.wait_ge(ready, n_ + 1)
                        for f in range(EC):
                            last = M(psb[2][:, 256 * m + 64 * f:256 * m + 64 * f + 64], src[:, f * P:(f + 1) * P], stack2[:, :],
                                     start=True, stop=True)
                    last.then_inc(e_hT, 1)
                    if q == 0:
                        pe.wait_ge(e_selw, i_ + 1)
                        for b in range(TB):
                            last = TR(psb[6][:, b * P:b * P + P], selW[:, b, :, :].rearrange("p q s -> p (q s)"), ident[:, :])
                        last.then_inc(e_gt, 1)
                    pe.wait_ge(e_h, n_ + 2)
                    pe.wait_ge(e_yev, n_ * 2 + 1)
                    for half in range(2):
                        s = landed(n_, 4 + half)
                        for f in range(2):
                            for i in range(4):
                                last = M(psb[3 + i // 2][64 * (i % 2):64 * (i % 2) + 64, :], hT[:, 2 * half + f, :],
                                         unit2(s)[:, f, 512 * i:512 * i + 512],
                                         start=half == 0 and f == 0, stop=half == 1 and f == 1)
                        last.then_inc(slot_free, 1)
                pe.wait_ge(e_gtev, i_ + 1)
                pe.wait_ge(e_yev, n0 * 2 + 2 * nq + 1)
                for k in range(8):
                    b, c = k // 4, k % 4
                    if k >= 2:
                        pe.wait_ge(e_acc, i_ * 8 + k - 1)
                    M(psb[6 + k % 2][:, :], gT[:, b * P:b * P + P], ye[:, 512 * c:512 * c + 512],
                      start=True, stop=True).then_inc(e_comb, 1)

            with pe.Fori(0, ITERS) as it:
                pe_items(it, it * QE, QE)
            pe.wait_ge(rk_ready, 2)
            extra = pe.value_load(n_extra[0:1, 0:1], min_val=0, max_val=EXTRA - 1)
            with pe.If(extra > 0):
                with pe.Fori(0, extra) as x_:
                    pe_items(x_ + ITERS, x_ + NE, 1)


_INS = ['x', 'norm_mix_g', 'w_in', 'sb_norm_g', 'ssm_lam_re', 'ssm_lam_im', 'ssm_b_re', 'ssm_b_im', 'ssm_c_re',
        'ssm_c_im', 'ssm_d', 'ssm_log_dt', 'ssm_w_glu', 'ssm_b_glu', 'ssm_norm_g', 'diff_lq1', 'diff_lk1',
        'diff_lq2', 'diff_lk2', 'diff_subln_g', 'w_out', 'norm_ffn_g', 'router_group_w', 'router_group_b',
        'router_expert_w', 'router_expert_b', 'expert_w1', 'expert_w3', 'expert_w2', 'final_norm_g']
_OUTS = [((1, T, D), 'float32')]


def kernel(**inputs):
    import numpy as _np
    import concourse.bacc as _bacc
    from concourse import mybir as _mybir
    from concourse.bass_utils import run_bass_kernel_spmd as _run

    nc = _bacc.Bacc("TRN2", target_bir_lowering=False, num_devices=1)
    arrays, args = {}, []
    for name in _INS:
        a = _np.ascontiguousarray(inputs[name])
        arrays[f"in_{name}_dram"] = a
        args.append(nc.dram_tensor(f"in_{name}_dram", a.shape, _mybir.dt.from_np(a.dtype), kind="ExternalInput").ap())
    for i, (shape, dtype) in enumerate(_OUTS):
        dt = _mybir.dt.from_np(_np.dtype(dtype))
        args.append(nc.dram_tensor(f"out_{i}_dram", shape, dt, kind="ExternalOutput").ap())
    build(nc, *args)
    r = _run(nc, [arrays], core_ids=[0])
    got = tuple(r.results[0][f"out_{i}_dram"] for i in range(len(_OUTS)))
    return got[0]
```
